# Optimizing a Trainium2 kernel written in Bass

```python
import jax, jax.numpy as jnp
from jax import lax
import numpy as np

D_MODEL = 2048
BATCH = 1
SEQ = 256
DEPTH = 2
DEC_BATCH = 8
DEC_SEQ = 1
PAST_LEN = 2048
PAGE_SIZE = 128

RET_HEADS = 8
RET_HEAD_DIM = 128
RET_WIDTH = RET_HEADS * RET_HEAD_DIM
CONV_CH = D_MODEL - RET_WIDTH
MIX_WIDTH = RET_WIDTH + CONV_CH
CONV_K = 31
P_DIM = 256
RET_CHUNK = 128
ROPE_BASE = 10000.0
EPS = 1e-6
IN_COLS = 4 * RET_WIDTH + 3 * CONV_CH
SPLITS = (RET_WIDTH, 2 * RET_WIDTH, 3 * RET_WIDTH, 4 * RET_WIDTH,
          4 * RET_WIDTH + CONV_CH, 4 * RET_WIDTH + 2 * CONV_CH)

kernel_name = "hymba_retention_conformer_step"

def _rms_norm(x, g):
    xf = x.astype(jnp.float32)
    y = xf * lax.rsqrt(jnp.mean(xf * xf, axis=-1, keepdims=True) + EPS)
    return (y * g.astype(jnp.float32)).astype(x.dtype)

def _layer_norm(x, g, b):
    xf = x.astype(jnp.float32)
    mu = jnp.mean(xf, axis=-1, keepdims=True)
    var = jnp.mean(jnp.square(xf - mu), axis=-1, keepdims=True)
    y = (xf - mu) * lax.rsqrt(var + EPS)
    return (y * g.astype(jnp.float32) + b.astype(jnp.float32)).astype(x.dtype)

def _rope(x, pos):
    half = RET_HEAD_DIM // 2
    inv = ROPE_BASE ** (-jnp.arange(half, dtype=jnp.float32) / half)
    ang = pos.astype(jnp.float32)[:, None] * inv[None, :]
    cos = jnp.cos(ang)[None, :, None, :]
    sin = jnp.sin(ang)[None, :, None, :]
    xf = x.astype(jnp.float32)
    x1, x2 = xf[..., :half], xf[..., half:]
    return jnp.concatenate([x1 * cos - x2 * sin, x1 * sin + x2 * cos], axis=-1)

def _log_gamma():
    return jnp.log1p(-jnp.exp2(-5.0 - jnp.arange(RET_HEADS, dtype=jnp.float32)))

def _retention_chunk(q, k, v, S, log_g):
    L = q.shape[2]
    idx = jnp.arange(L, dtype=jnp.float32)
    rel = idx[:, None] - idx[None, :]
    decay = jnp.where(rel >= 0, jnp.exp(log_g[:, None, None] * jnp.maximum(rel, 0.0)), 0.0)
    scores = jnp.einsum('bhid,bhjd->bhij', q, k) * decay[None]
    o_intra = jnp.einsum('bhij,bhjv->bhiv', scores, v)
    cross_decay = jnp.exp(log_g[:, None] * (idx[None, :] + 1.0))
    o_cross = jnp.einsum('bhid,bhdv->bhiv', q, S) * cross_decay[None, :, :, None]
    k_decay = jnp.exp(log_g[:, None] * (L - 1.0 - idx[None, :]))
    S_new = (jnp.exp(log_g * L)[None, :, None, None] * S
             + jnp.einsum('bhjd,bhjv->bhdv', k * k_decay[None, :, :, None], v))
    return o_intra + o_cross, S_new

def _retention(q, k, v, S0):
    B, H, L, _ = q.shape
    chunk = RET_CHUNK if L % RET_CHUNK == 0 else L
    nc = L // chunk
    log_g = _log_gamma()

    def blocks(t):
        return t.reshape(B, H, nc, chunk, t.shape[-1]).transpose(2, 0, 1, 3, 4)

    def step(S, qkv):
        qc, kc, vc = qkv
        o, S = _retention_chunk(qc, kc, vc, S, log_g)
        return S, o

    S, o = lax.scan(step, S0, (blocks(q), blocks(k), blocks(v)))
    o = o.transpose(1, 2, 0, 3, 4).reshape(B, H, L, RET_HEAD_DIM)
    return o, S

def _mixer(h, S0, buf0, pos, w_in, w_out, g_ret, w_dw, b_dw, g_cn, b_cn, w_pw2, b_pw2):
    Bsz, L, _ = h.shape
    z = h @ w_in
    q, k, v, g_r, a, b, g_c = jnp.split(z, SPLITS, axis=-1)
    heads = lambda t: t.reshape(Bsz, L, RET_HEADS, RET_HEAD_DIM)
    q = _rope(heads(q), pos)
    k = _rope(heads(k), pos) * (RET_HEAD_DIM ** -0.5)
    vf = heads(v).astype(jnp.float32)
    tr = lambda t: t.transpose(0, 2, 1, 3)
    o, S = _retention(tr(q), tr(k), tr(vf), S0.astype(jnp.float32))
    o = tr(o)
    mu = jnp.mean(o, axis=-1, keepdims=True)
    var = jnp.mean(jnp.square(o - mu), axis=-1, keepdims=True)
    o = ((o - mu) * lax.rsqrt(var + EPS)).reshape(Bsz, L, RET_WIDTH) * g_ret.astype(jnp.float32)
    ret_out = o.astype(h.dtype) * jax.nn.silu(g_r)
    u = a * jax.nn.sigmoid(b)
    full = jnp.concatenate([buf0.astype(u.dtype), u], axis=1)
    c = lax.conv_general_dilated(full, w_dw[:, None, :].astype(u.dtype), (1,), 'VALID',
                                 dimension_numbers=('NWC', 'WIO', 'NWC'),
                                 feature_group_count=CONV_CH) + b_dw
    c = jax.nn.silu(_layer_norm(c, g_cn, b_cn))
    c = c @ w_pw2 + b_pw2
    conv_out = c * jax.nn.silu(g_c)
    m = jnp.concatenate([ret_out, conv_out], axis=-1) @ w_out
    return m, S.astype(h.dtype), full[:, -(CONV_K - 1):]

def _trunk(x, p, S_all, buf_all, pos, w_in, w_out, g_ret, w_dw, b_dw, g_cn, b_cn,
           w_pw2, b_pw2, g_pre, g_post, w_ple, g_ple, w_ple_gate):
    new_S, new_buf = [], []
    for i in range(DEPTH):
        hn = _rms_norm(x, g_pre[i])
        m, S, buf = _mixer(hn, S_all[i], buf_all[i], pos, w_in[i], w_out[i], g_ret[i],
                           w_dw[i], b_dw[i], g_cn[i], b_cn[i], w_pw2[i], b_pw2[i])
        h = x + _rms_norm(m, g_post[i])
        e = _rms_norm(p[i] @ w_ple[i], g_ple[i])
        x = h + jax.nn.sigmoid(h @ w_ple_gate[i]) * e
        new_S.append(S)
        new_buf.append(buf)
    return x, jnp.stack(new_S), jnp.stack(new_buf)

def setup_inputs(seed: int = 0) -> dict:
    key = jax.random.key(seed)
    ks = jax.random.split(key, 24)
    f32 = jnp.float32
    nrm = lambda k, shape, s: jax.random.normal(k, shape, f32) * s
    gain = lambda k, shape: 1.0 + 0.02 * jax.random.normal(k, shape, f32)
    return {
        "x_prompt": nrm(ks[0], (BATCH, SEQ, D_MODEL), 1.0),
        "x_sample": nrm(ks[1], (DEC_BATCH, DEC_SEQ, D_MODEL), 1.0),
        "state_ret": nrm(ks[2], (DEPTH, DEC_BATCH, RET_HEADS, RET_HEAD_DIM, RET_HEAD_DIM), 0.05),
        "state_conv": nrm(ks[3], (DEPTH, DEC_BATCH, CONV_K - 1, CONV_CH), 0.5),
        "p_prompt": nrm(ks[4], (DEPTH, BATCH, SEQ, P_DIM), 1.0),
        "p_sample": nrm(ks[5], (DEPTH, DEC_BATCH, DEC_SEQ, P_DIM), 1.0),
        "w_in": nrm(ks[6], (DEPTH, D_MODEL, IN_COLS), D_MODEL ** -0.5),
        "w_out": nrm(ks[7], (DEPTH, MIX_WIDTH, D_MODEL), MIX_WIDTH ** -0.5),
        "g_ret": gain(ks[8], (DEPTH, RET_WIDTH)),
        "w_dw": nrm(ks[9], (DEPTH, CONV_K, CONV_CH), CONV_K ** -0.5),
        "b_dw": nrm(ks[10], (DEPTH, CONV_CH), 0.01),
        "g_cn": gain(ks[11], (DEPTH, CONV_CH)),
        "b_cn": nrm(ks[12], (DEPTH, CONV_CH), 0.01),
        "w_pw2": nrm(ks[13], (DEPTH, CONV_CH, CONV_CH), CONV_CH ** -0.5),
        "b_pw2": nrm(ks[14], (DEPTH, CONV_CH), 0.01),
        "g_pre": gain(ks[15], (DEPTH, D_MODEL)),
        "g_post": gain(ks[16], (DEPTH, D_MODEL)),
        "w_ple": nrm(ks[17], (DEPTH, P_DIM, D_MODEL), P_DIM ** -0.5),
        "g_ple": gain(ks[18], (DEPTH, D_MODEL)),
        "w_ple_gate": nrm(ks[19], (DEPTH, D_MODEL, D_MODEL), D_MODEL ** -0.5),
    }

def reference(x_prompt, x_sample, state_ret, state_conv, p_prompt, p_sample, w_in, w_out,
              g_ret, w_dw, b_dw, g_cn, b_cn, w_pw2, b_pw2, g_pre, g_post, w_ple, g_ple,
              w_ple_gate):
    weights = (w_in, w_out, g_ret, w_dw, b_dw, g_cn, b_cn, w_pw2, b_pw2,
               g_pre, g_post, w_ple, g_ple, w_ple_gate)
    Bp, Lp, _ = x_prompt.shape
    S0_p = jnp.zeros((DEPTH, Bp, RET_HEADS, RET_HEAD_DIM, RET_HEAD_DIM), x_prompt.dtype)
    buf0_p = jnp.zeros((DEPTH, Bp, CONV_K - 1, CONV_CH), x_prompt.dtype)
    pos_p = jnp.arange(Lp, dtype=jnp.int32)
    y_prompt, state_ret_prompt, state_conv_prompt = _trunk(
        x_prompt, p_prompt, S0_p, buf0_p, pos_p, *weights)
    Ls = x_sample.shape[1]
    pos_s = PAST_LEN + jnp.arange(Ls, dtype=jnp.int32)
    y_sample, state_ret_sample, state_conv_sample = _trunk(
        x_sample, p_sample, state_ret, state_conv, pos_s, *weights)
    return (y_prompt, y_sample, state_ret_prompt, state_conv_prompt,
            state_ret_sample, state_conv_sample)


_drawn_inputs = setup_inputs


def setup_inputs(seed=0):
    import zlib

    import numpy as np

    out = dict(_drawn_inputs(seed))
    spreads = {}
    factors = {'g_ret': 52.244,
     'b_dw': 4.937,
     'g_cn': 75.985,
     'b_cn': 151.718,
     'b_pw2': 103.993,
     'g_post': 8.339,
     'g_ple': 13.16}
    for name, (base, spread) in spreads.items():
        noise = np.random.default_rng([zlib.crc32(name.encode()), seed]).standard_normal(out[name].shape)
        drawn = base * np.exp(spread * noise) if base else spread * noise
        out[name] = __import__('jax').numpy.asarray(drawn.astype(out[name].dtype))
    for name, factor in factors.items():
        out[name] = (out[name] * factor).astype(out[name].dtype)
    return out
```

```python
import numpy as np
import concourse.bass as bass
from concourse import mybir
from contextlib import ExitStack

F32 = mybir.dt.float32
F32R = mybir.dt.float32r
ACT = mybir.ActivationFunctionType
ALU = mybir.AluOpType
AX = mybir.AxisListType

P = 128
DEPTH, D_MODEL, SEQ, DEC, PAST = 2, 2048, 256, 8, 2048
HEADS, CONV, TAPS, P_DIM = 8, 1024, 31, 256
EPS = 1e-6
R = SEQ + DEC
KT = D_MODEL // P
CT = CONV // P
PT = P_DIM // P
PAD = TAPS - 1
UW = PAD + R
SLAB = KT * P
RING, RAW = 4, 2

T_C, T_G, T_H, T_W, T_O, T_P, T_T, TILES = 0, 16, 24, 56, 64, 80, 96, 112
S_C, S_G, S_H, S_W, S_O, S_P, S_T, SLABS = 0, 16, 24, 56, 60, 76, 80, 96

V_PRE, V_POST, V_PLE, V_RET, V_BDW, V_GCN, V_BCN, V_BPW, V_DW = 0, 16, 32, 48, 56, 64, 72, 80, 88
VW = V_DW + CT * TAPS

K_ID, K_TRI, K_COS, K_SIN = 0, P, 2 * P, 2 * P + R
K_KDEC = K_SIN + R
K_GI = K_KDEC + 2 * HEADS
K_GAM = K_GI + 3 * HEADS
K_END = K_GAM + HEADS
K_MASK = K_END + HEADS
KW = K_MASK + DEC


def constants():
    c = np.zeros((P, KW), np.float32)
    c[:, K_ID:K_ID + P] = np.eye(P)
    c[:, K_TRI:K_TRI + P] = np.triu(np.ones((P, P)))
    half = P // 2
    inv = (10000.0 ** -(np.arange(half) / half)).astype(np.float32)
    pos = np.concatenate([np.arange(SEQ), np.full(DEC, PAST)]).astype(np.float32)
    ang = (pos[None, :] * inv[:, None]).astype(np.float32)
    cos, sin = np.cos(ang.astype(np.float64)), np.sin(ang.astype(np.float64))
    c[:, K_COS:K_COS + R] = np.concatenate([cos, cos])
    c[:, K_SIN:K_SIN + R] = np.concatenate([-sin, sin])
    log_g = np.log1p(-np.exp2(-5.0 - np.arange(HEADS)))
    row = np.arange(P)
    for h in range(HEADS):
        for chunk in range(2):
            c[:, K_KDEC + 2 * h + chunk] = np.exp(-log_g[h] * (row + P * chunk)) * P ** -0.5
            c[:, K_GI + 3 * h + chunk] = np.exp(log_g[h] * (row + P * chunk))
        c[:, K_GI + 3 * h + 2] = 1.0
        c[:, K_GAM + h] = np.exp(log_g[h])
        c[:, K_END + h] = np.exp(log_g[h] * (SEQ - 1))
    c[:, K_MASK:K_MASK + DEC] = (row[:, None] % DEC) == np.arange(DEC)[None, :]
    return c


def tile_done_at(l, t):
    return t + (TILES * l + 1)


def bank_free_at(l, pair):
    return pair + (TILES // 2 * l + 1)


def read_out_at(l, pair):
    return pair + (TILES // 2 * l + 2)


class Signals:

    def __init__(self, nc):
        self.consts_in = nc.alloc_semaphore("consts_in")
        self.x_in = nc.alloc_semaphore("x_in")
        self.p_in = nc.alloc_semaphore("p_in")
        self.convstate_in = nc.alloc_semaphore("convstate_in")
        self.state_in = nc.alloc_semaphore("state_in")
        self.state_out = nc.alloc_semaphore("state_out")
        self.sprompt_out = nc.alloc_semaphore("sprompt_out")
        self.scp_out = nc.alloc_semaphore("scp_out")
        self.scs_out = nc.alloc_semaphore("scs_out")
        self.y_out = nc.alloc_semaphore("y_out")
        self.hi_ready = nc.alloc_semaphore("hi_ready")
        self.lo_ready = nc.alloc_semaphore("lo_ready")
        self.tile_done = nc.alloc_semaphore("tile_done")
        self.xhi_ready = nc.alloc_semaphore("xhi_ready")
        self.xin_ready = nc.alloc_semaphore("xin_ready")
        self.chi_ready = nc.alloc_semaphore("chi_ready")
        self.c_ready = nc.alloc_semaphore("c_ready")
        self.phi_ready = nc.alloc_semaphore("phi_ready")
        self.pin_ready = nc.alloc_semaphore("pin_ready")
        self.rhi_ready = nc.alloc_semaphore("rhi_ready")
        self.ret_ready = nc.alloc_semaphore("ret_ready")
        self.cohi_ready = nc.alloc_semaphore("cohi_ready")
        self.cout_ready = nc.alloc_semaphore("cout_ready")
        self.hhi_ready = nc.alloc_semaphore("hhi_ready")
        self.h_ready = nc.alloc_semaphore("h_ready")
        self.sq_ready = nc.alloc_semaphore("sq_ready")
        self.sq_used = nc.alloc_semaphore("sq_used")
        self.sum_done = nc.alloc_semaphore("sum_done")
        self.stat_scaled = nc.alloc_semaphore("stat_scaled")
        self.stat_rs = nc.alloc_semaphore("stat_rs")
        self.diag_ready = nc.alloc_semaphore("diag_ready")
        self.bcast_done = nc.alloc_semaphore("bcast_done")
        self.bcast_read = nc.alloc_semaphore("bcast_read")
        self.small_set = nc.alloc_semaphore("small_set")
        self.consts_set = nc.alloc_semaphore("consts_set")
        self.pad_set = nc.alloc_semaphore("pad_set")
        self.rfac_step = nc.alloc_semaphore("rfac_step")
        self.tanh_ready = nc.alloc_semaphore("tanh_ready")
        self.u_ready = nc.alloc_semaphore("u_ready")
        self.ust_ready = nc.alloc_semaphore("ust_ready")
        self.tap_done = nc.alloc_semaphore("tap_done")
        self.sconv_step = nc.alloc_semaphore("sconv_step")
        self.gc_ready = nc.alloc_semaphore("gc_ready")
        self.ln_summed = nc.alloc_semaphore("ln_summed")
        self.mean_done = nc.alloc_semaphore("mean_done")
        self.ln_centered = nc.alloc_semaphore("ln_centered")
        self.ln_squared = nc.alloc_semaphore("ln_squared")
        self.ln_scaled = nc.alloc_semaphore("ln_scaled")
        self.silu_ready = nc.alloc_semaphore("silu_ready")
        self.rope_step = nc.alloc_semaphore("rope_step")
        self.rope_done = nc.alloc_semaphore("rope_done")
        self.kv_ready = nc.alloc_semaphore("kv_ready")
        self.khi_ready = nc.alloc_semaphore("khi_ready")
        self.stack_in = nc.alloc_semaphore("stack_in")
        self.s1_done = nc.alloc_semaphore("s1_done")
        self.rows_ready = nc.alloc_semaphore("rows_ready")
        self.p_ready = nc.alloc_semaphore("p_ready")
        self.vbd_ready = nc.alloc_semaphore("vbd_ready")
        self.s2_done = nc.alloc_semaphore("s2_done")
        self.snew_ready = nc.alloc_semaphore("snew_ready")
        self.sprompt_ready = nc.alloc_semaphore("sprompt_ready")
        self.bn_done = nc.alloc_semaphore("bn_done")
        self.stat_ready = nc.alloc_semaphore("stat_ready")
        self.pool_step = nc.alloc_semaphore("pool_step")
        self.ret_rs = nc.alloc_semaphore("ret_rs")
        self.s3a_done = nc.alloc_semaphore("s3a_done")
        self.os_ready = nc.alloc_semaphore("os_ready")
        self.s3b_done = nc.alloc_semaphore("s3b_done")
        self.og_ready = nc.alloc_semaphore("og_ready")
        self.s4_done = nc.alloc_semaphore("s4_done")
        self.rt_ready = nc.alloc_semaphore("rt_ready")
        self.sg_ready = nc.alloc_semaphore("sg_ready")
        self.h_step = nc.alloc_semaphore("h_step")
        self.e_step = nc.alloc_semaphore("e_step")
        self.gate_step = nc.alloc_semaphore("gate_step")
        self.xnew = nc.alloc_semaphore("xnew")


def build(nc, ctx, x_t, p_t, s_ret, s_conv, vecs_d, consts_d, w_in, w_pw, w_out, w_ple, w_gate,
          y_t, sp_out, scp_out, ss_out, scs_out):
    sb_at = {}
    cursor = [(nc.sbuf_base + 31) // 32 * 32]

    def sb(name, shape, dt=F32, at=None):
        size = int(np.prod(shape[1:])) * 4
        where = cursor[0] if at is None else at
        if at is None:
            cursor[0] = (cursor[0] + size + 31) // 32 * 32
        assert where + size <= nc.sbuf_usable_end, (name, where, size)
        sb_at[name] = (where, where + size)
        return nc.alloc_sbuf_tensor_at(name, shape, dt, offset=where)

    raw = sb("raw", [P, RAW, SLAB])
    whi = sb("whi", [P, RING, SLAB], F32R)
    wlo = sb("wlo", [P, RING, SLAB], F32R)
    a_hi = sb("a_hi", [P, KT, R], F32R)
    a_lo = sb("a_lo", [P, KT, R], F32R)
    b_hi = sb("b_hi", [P, KT, R], F32R)
    b_lo = sb("b_lo", [P, KT, R], F32R)
    c_buf = sb("c_buf", [P, CT, R], at=sb_at["b_hi"][0] + CT * R * 4)
    gc_buf = sb("gc_buf", [P, CT, R], at=sb_at["b_lo"][0] + CT * R * 4)
    x = sb("x", [P, KT, R])
    vecs = sb("vecs", [P, DEPTH, VW])
    cst = sb("cst", [P, KW])
    ones = sb("ones", [P, P])
    ones_mean = sb("ones_mean", [P, P])
    r_x = sb("r_x", [P, R])
    r_t = sb("r_t", [P, R])
    diag = sb("diag", [P, R])
    acc = [sb(f"acc{i}", [P, R]) for i in range(2)]
    sq = sb("sq", [P, 2, R])
    tmp = [sb(f"tmp{i}", [P, R]) for i in range(4)]
    small = sb("small", [P, 192])
    work = cursor[0]
    m_buf = sb("m_buf", [P, KT, R], at=work)
    e_buf = sb("e_buf", [P, KT, R], at=sb_at["m_buf"][1])
    u_buf = sb("u_buf", [P, CT, UW], at=work)
    ln_sq = sb("ln_sq", [P, CT, R], at=work)
    ust = sb("ust", [P, CT, TAPS, DEC], at=sb_at["u_buf"][1])
    s_new = sb("s_new", [P, DEC * P], at=sb_at["u_buf"][1])
    heads_at = sb_at["ust"][1]
    sprod = sb("sprod", [P, CT, DEC, TAPS], at=heads_at)
    cursor[0] = heads_at
    vbd = sb("vbd", [32, DEC, P], F32R)
    zs = sb("zs", [P, 2, R])
    zw = sb("zw", [P, 2, R])
    qk = sb("qk", [P, 2, R])
    vt = sb("vt", [P, R])
    vrow = sb("vrow", [P, 2 * P])
    krow = sb("krow", [P, 2 * P])
    pmat = sb("pmat", [P, 3 * P])
    stack_cols = sb("stack_cols", [P, 2, 4, DEC], F32R)
    stack = sb("stack", [32, 2 * P], F32R)
    og = sb("og", [P, 3, P])
    s_prompt = sb("s_prompt", [P, P])
    gz = sb("gz", [P, R])
    sg = sb("sg", [P, R])
    rt = sb("rt", [P, R])
    qks = sb("qks", [P, 2, DEC])
    vs = sb("vs", [P, DEC])
    os_t = sb("os_t", [P, DEC])
    heads_end = cursor[0]
    cursor[0] = max(heads_end, sb_at["e_buf"][1])
    p_in = sb("p_in", [P, PT, R])
    assert sb_at["sprod"][1] <= heads_end

    def sm(name, at, n):
        return small[:, at:at + n]

    st, rs = sm("st", 0, 3), sm("rs", 4, 3)
    rx3, r2 = sm("rx3", 8, 3), sm("r2", 12, 2)
    kk = small[:, 16:32].rearrange("p (h c) -> p h c", c=2)
    gi = small[:, 32:56].rearrange("p (h c) -> p h c", c=3)
    g2 = small[:, 56:80].rearrange("p (h c) -> p h c", c=3)
    rs8 = small[:, 80:96].rearrange("p (a b) -> p a b", a=2)
    bn = sm("bn", 96, 18)
    mv = small[:, 116:122].rearrange("p (c s) -> p c s", s=2)
    var_t, rs_t, sc_t, nb_t = (small[:, 124 + 4 * i:127 + 4 * i] for i in range(4))
    minus_half = sm("minus_half", 140, 3)
    mean_sc = sm("mean_sc", 144, 3)
    eps3, zero3 = sm("eps3", 148, 3), sm("zero3", 152, 3)
    held = sm("held", 156, 1)

    ps = [nc.alloc_psum_tensor(f"ps{i}", [P, 512], F32) for i in range(8)]
    accum = ps[0:2]
    ps_tr, ps_st, ps_p, ps_o, ps_s0, ps_s1 = ps[2:8]

    ident = cst[:, K_ID:K_ID + P]
    tri = cst[:, K_TRI:K_TRI + P]

    s = Signals(nc)
    raw_in = [nc.alloc_semaphore("raw_even_in"), nc.alloc_semaphore("raw_odd_in")]
    acc_free = [nc.alloc_semaphore("acc_even_free"), nc.alloc_semaphore("acc_odd_free")]

    ST_X, ST_LN, ST_M, ST_E = range(4)

    def stat_at(l, k):
        return 4 * l + k + 1

    def spread_at(l, k):
        return 3 * l + {ST_X: 1, ST_M: 2, ST_E: 3}[k]

    def squares_at(l):
        return KT + 3 * KT * l

    def vec(l, at, n=1):
        return vecs[:, l, bass.ds(at, n)]

    def wide(ap, shape):
        return ap.unsqueeze(1).to_broadcast(shape)

    def rows(t, tile, n=1):
        return t[:, :, :].rearrange("p k r -> p (k r)")[:, bass.ds(tile * R, n * R)]

    block = ctx.enter_context(nc.Block())

    @block.sync
    def _(sp):
        def load(l, slab, src, first_row, cols=SLAB):
            here = slab_static[0] % RAW
            if l or slab_static[0] >= RAW:
                sp.wait_ge(s.lo_ready, slab + (SLABS * l - 1))
            sp.dma_start(raw[:, here, 0:cols], src[bass.ds(first_row, P), :]).then_inc(raw_in[here], 16)
            slab_static[0] += 1

        slab_static = [0]
        for l in range(DEPTH):
            slab_static[0] = 0
            for j in range(4):
                load(l, S_C + j, w_in, P * (56 * l + (40, 32)[j % 2] + j // 2))
            with sp.Fori(1, 4) as i:
                for j in range(4):
                    load(l, 4 * i + (S_C + j), w_in, P * (2 * i + (56 * l + (40, 32)[j % 2] + j // 2)))
            with sp.Fori(0, 2) as i:
                for j in range(4):
                    load(l, 4 * i + (S_G + j), w_in, P * (4 * i + (56 * l + 48 + j)))
            with sp.Fori(0, HEADS) as h:
                for j in range(4):
                    load(l, 4 * h + (S_H + j), w_in, P * (h + (56 * l + HEADS * j)))
            for j in range(4):
                load(l, S_W + j, w_pw, P * (4 * l + j))
            with sp.Fori(0, 4) as i:
                for j in range(4):
                    load(l, 4 * i + (S_O + j), w_out, P * (4 * i + (16 * l + j)))
            for j in range(4):
                load(l, S_P + j, w_ple, P * (4 * l + j), 4 * PT * P)
            with sp.Fori(0, 4) as i:
                for j in range(4):
                    load(l, 4 * i + (S_T + j), w_gate, P * (4 * i + (16 * l + j)))
        for i in range(4):
            sp.wait_ge(s.xnew, KT * (DEPTH - 1) + 4 * i + 4)
            sp.dma_start(y_t[:, 4 * i:4 * i + 4, :], x[:, 4 * i:4 * i + 4, :]).then_inc(s.y_out, 16)
        sp.wait_ge(s.state_out, 16 * HEADS * DEPTH)
        sp.wait_ge(s.sprompt_out, 16 * HEADS * DEPTH + 1)
        sp.wait_ge(s.scp_out, 16 * DEPTH)
        sp.wait_ge(s.scs_out, 16 * DEPTH)
        sp.wait_ge(s.y_out, 16 * 4)

    @block.tensor
    def _(pe):
        def gemm(l, pair, bank, slab, slot, at, k_tiles, hi, lo, k_wait=None, k0=0, mid=None, fresh=True):
            pe.wait_ge(acc_free[bank], bank_free_at(l, pair))
            if fresh:
                pe.wait_ge(s.lo_ready, slab + (SLABS * l + 1))
            for k in range(k_tiles):
                if k_wait:
                    k_wait(k)
                if mid and k == k_tiles // 2:
                    mid()
                w = at + P * k
                pe.matmul(accum[bank][:, 0:R], whi[:, slot, w:w + P], hi[:, k0 + k, :], start=k == 0, stop=False)
                pe.matmul(accum[bank][:, 0:R], whi[:, slot, w:w + P], lo[:, k0 + k, :], start=False, stop=False)
                mm = pe.matmul(accum[bank][:, 0:R], wlo[:, slot, w:w + P], hi[:, k0 + k, :], start=False, stop=k == k_tiles - 1)
            mm.then_inc(s.tile_done, 1)

        def stat_sum(l, k, buf):
            pe.matmul(ps_p[:, 0:1], buf[:, 0:P], ones[:, 0:1], start=True, stop=True)
            pe.matmul(ps_p[:, 1:2], buf[:, P:2 * P], ones[:, 0:1], start=True, stop=True)
            pe.matmul(ps_p[0:DEC, 2:3], buf[:, 2 * P:R], ones[:, 0:1], start=True, stop=True).then_inc(s.sum_done, 1)

        def stat_bcast(l, k):
            pe.wait_ge(s.diag_ready, stat_at(l, k))
            pe.matmul(ps_p[:, 0:P], ones[:, :], diag[:, 0:P], start=True, stop=True)
            pe.matmul(ps_p[:, P:2 * P], ones[:, :], diag[:, P:2 * P], start=True, stop=True)
            pe.matmul(ps_p[:, 2 * P:R], ones[0:DEC, :], diag[0:DEC, 2 * P:R], start=True, stop=True).then_inc(s.bcast_done, 1)

        def ret_scores(l, h):
            n = h + HEADS * l
            pe.wait_ge(s.stack_in, n + 1)
            pe.wait_ge(s.rt_ready, n + 1)
            pe.transpose(ps_tr[:, 0:P], vt[:, 0:P], ident)
            pe.transpose(ps_tr[:, P:2 * P], vt[:, P:2 * P], ident)
            pe.transpose(ps_tr[:, 2 * P:3 * P], qk[:, 1, 0:P], ident)
            pe.transpose(ps_tr[:, 3 * P:4 * P], qk[:, 1, P:2 * P], ident)
            cols = stack_cols[:, :, :, :].rearrange("p a b c -> p (a b c)").bitcast(F32)
            pe.transpose(ps_st[0:32, 0:P], cols[:, 0:32], ident)
            pe.transpose(ps_st[0:32, P:2 * P], cols[:, 32:64], ident)
            pe.matmul(ps_p[:, 0:2 * P], qk[:, 1, 0:P], qk[:, 0, 0:2 * P], start=True, stop=True)
            pe.matmul(ps_p[:, 2 * P:3 * P], qk[:, 1, P:2 * P], qk[:, 0, P:2 * P], start=True, stop=True).then_inc(s.s1_done, 1)

        def ret_values(l, h):
            n = h + HEADS * l
            pe.wait_ge(s.rows_ready, n + 1)
            pe.wait_ge(s.p_ready, n + 1)
            pe.matmul(ps_o[:, 0:P], pmat[:, 0:P], vrow[:, 0:P], start=True, stop=True)
            pe.matmul(ps_o[:, P:2 * P], pmat[:, P:2 * P], vrow[:, 0:P], start=True, stop=False)
            pe.matmul(ps_o[:, P:2 * P], pmat[:, 2 * P:3 * P], vrow[:, P:2 * P], start=False, stop=True)
            pe.matmul(ps_tr[:, 0:P], krow[:, 0:P], vrow[:, 0:P], start=True, stop=False)
            pe.matmul(ps_tr[:, 0:P], krow[:, P:2 * P], vrow[:, P:2 * P], start=False, stop=True)
            pe.wait_ge(s.vbd_ready, n + 1)
            blocks = vbd[:, :, :].rearrange("p b v -> p (b v)")
            pe.matmul(ps_s0[:, :], stack[:, 0:P], blocks[:, 0:4 * P], start=True, stop=True)
            pe.matmul(ps_s1[:, :], stack[:, 0:P], blocks[:, 4 * P:8 * P], start=True, stop=True).then_inc(s.s2_done, 1)

        def ret_samples(l, h):
            pe.wait_ge(s.snew_ready, h + (HEADS * l + 1))
            for b in range(DEC):
                mm = pe.matmul(ps_st[:, 2 * P + b:2 * P + b + 1], s_new[:, b * P:(b + 1) * P], qks[:, 0, b:b + 1], start=True, stop=True)
            mm.then_inc(s.s3a_done, 1)

        def ret_sample_rows(l, h):
            pe.wait_ge(s.os_ready, h + (HEADS * l + 1))
            pe.transpose(ps_st[0:DEC, 3 * P:4 * P], os_t[:, :], ident).then_inc(s.s3b_done, 1)

        def ret_turn(l, h):
            pe.wait_ge(s.og_ready, h + (HEADS * l + 1))
            pe.transpose(ps_tr[:, 0:P], og[:, 0, :], ident)
            pe.transpose(ps_tr[:, P:2 * P], og[:, 1, :], ident)
            pe.transpose(ps_tr[:, 2 * P:R], og[0:DEC, 2, :], cst[0:DEC, K_ID:K_ID + DEC]).then_inc(s.s4_done, 1)

        def head(l, h, prev):
            for j in range(4):
                mid = (lambda: ret_sample_rows(l, h - 1)) if prev and j == 3 else None
                pair = 2 * h + (T_H // 2 + j // 2)
                gemm(l, pair, j % 2, 4 * h + (S_H + j), j, 0, KT, a_hi, a_lo, mid=mid)
                if prev:
                    (ret_scores, ret_values, ret_samples, ret_turn)[j](l, h - 1)
                if isinstance(h, int) and h == 5 and j == 1:
                    pe.wait_ge(s.ln_summed, 2 * l + 1)
                    pe.matmul(ps_p[:, 0:R], ones_mean[:, :], acc[(3 * l + 1) % 2][:, :], start=True, stop=True).then_inc(s.mean_done, 1)
                if isinstance(h, int) and h == 6 and j == 1:
                    pe.wait_ge(s.ln_summed, 2 * l + 2)
                    stat_sum(l, ST_LN, acc[3 * l % 2])
                if isinstance(h, int) and h == 7 and j == 1:
                    stat_bcast(l, ST_LN)

        def sum_x():
            pe.wait_ge(s.sq_used, squares_at(l))
            stat_sum(l, ST_X, acc[3 * l % 2])

        for l in range(DEPTH):
            if l == 0:
                pe.wait_ge(s.consts_in, 16 * 2)
                pe.wait_ge(s.consts_set, 1)
            for j in range(4):
                gemm(l, j // 2, j % 2, S_C + j, j, 0, KT, a_hi, a_lo,
                     k_wait=(lambda k: pe.wait_ge(s.xin_ready, KT * l + k + 1)) if j == 0 else None,
                     mid=(lambda: stat_bcast(l, ST_X)) if j == 1 else None)
                if j == 0:
                    sum_x()
            with pe.Fori(1, 4) as i:
                for j in range(4):
                    gemm(l, 2 * i + j // 2, j % 2, 4 * i + (S_C + j), j, 0, KT, a_hi, a_lo)
            with pe.Fori(0, 2) as i:
                for j in range(4):
                    gemm(l, 2 * i + (T_G // 2 + j // 2), j % 2, 4 * i + (S_G + j), j, 0, KT, a_hi, a_lo)
            head(l, 0, False)
            with pe.Fori(1, 5) as h:
                head(l, h, True)
            for h in (5, 6, 7):
                if h == 6:
                    pe.wait_ge(s.ln_centered, l + 1)
                if h == 7:
                    pe.wait_ge(s.stat_scaled, stat_at(l, ST_LN))
                head(l, h, True)
            for j in range(4):
                for e in range(2):
                    gemm(l, (T_W + 2 * j) // 2, e % 2, S_W + j, j, e * CT * P, CT, a_hi, a_lo, fresh=e == 0,
                         k_wait=(lambda k: pe.wait_ge(s.c_ready, 3 * l + (1, 1, 2, 2, 3, 3, 3, 3)[k])) if j == 0 and e == 0 else None,
                         mid=(lambda: ret_sample_rows(l, 7)) if j == 3 and e == 0 else None)
                if j == 0:
                    pe.wait_ge(s.ln_scaled, 2 * l + 2)
                (ret_scores, ret_values, ret_samples, ret_turn)[j](l, 7)
            with pe.Fori(0, 4) as i:
                for j in range(4):
                    gemm(l, 2 * i + (T_O // 2 + j // 2), j % 2, 4 * i + (S_O + j), j, 0, KT, b_hi, b_lo,
                         k_wait=(lambda k: pe.wait_ge(s.ret_ready, HEADS * l + k + 1) if k < HEADS
                                 else pe.wait_ge(s.cout_ready, CT * l + k - HEADS + 1)) if j == 0 else None)
            for j in range(4):
                for e in range(4):
                    gemm(l, (T_P + 4 * j + e) // 2, e % 2, S_P + j, j, e * PT * P, PT, a_hi, a_lo, fresh=e == 0, k0=CT,
                         k_wait=(lambda k: pe.wait_ge(s.pin_ready, l + 1)) if j == 0 and e == 0 else None)
                if j == 0:
                    pe.wait_ge(s.sq_used, squares_at(l) + KT)
                    stat_sum(l, ST_M, acc[(3 * l + 1) % 2])
                if j == 1:
                    stat_bcast(l, ST_M)
            for j in range(4):
                gemm(l, (T_T + j) // 2, j % 2, S_T + j, j, 0, KT, b_hi, b_lo,
                     k_wait=(lambda k: pe.wait_ge(s.h_ready, 4 * l + k // 4 + 1)) if j == 0 else None)
                if j == 0:
                    pe.wait_ge(s.sq_used, squares_at(l) + 2 * KT)
                    pe.wait_ge(s.bcast_read, spread_at(l, ST_M))
                    stat_sum(l, ST_E, acc[3 * l % 2])
                if j == 1:
                    stat_bcast(l, ST_E)
            with pe.Fori(1, 4) as i:
                for j in range(4):
                    gemm(l, 2 * i + (T_T // 2 + j // 2), j % 2, 4 * i + (S_T + j), j, 0, KT, b_hi, b_lo)
            pe.wait_ge(s.bcast_read, spread_at(l, ST_E))

    @block.scalar
    def _(act):
        def next_hi(l, body, slot, tile, cols=SLAB):
            act.wait_ge(raw_in[slot % RAW], body * 32 + 16 * (SLABS // 2 * l + 3 + slot // 2))
            act.wait_ge(s.tile_done, tile_done_at(l, tile))
            nc.scalar.activation(whi[:, slot, 0:cols], raw[:, slot % RAW, 0:cols], ACT.Copy).then_inc(s.hi_ready, 1)

        def square(n, side, src):
            act.wait_ge(s.sq_used, n - 1)
            nc.scalar.activation(sq[:, side, :], src, ACT.Square).then_inc(s.sq_ready, 1)

        def conv_in(l, i):
            for j in range(4):
                ct = 2 * i + j // 2
                if j % 2 == 0:
                    act.wait_ge(acc_free[0], read_out_at(l, ct))
                    nc.scalar.activation(tmp[2][:, :], tmp[0][:, :], ACT.Tanh, scale=0.5).then_inc(s.tanh_ready, 1)
                    next_hi(l, i, j, 4 * i + j)
                else:
                    next_hi(l, i, j, 4 * i + j)
                    act.wait_ge(s.u_ready, ct + (CT * l + 1))
                    ust_flat = ust[:, :, :, :].rearrange("p c k b -> p (c k b)")
                    nc.scalar.activation(ust_flat[:, bass.ds(ct * (TAPS * DEC) + PAD * DEC, DEC)],
                                         u_flat[:, bass.ds(ct * UW + PAD + SEQ, DEC)], ACT.Copy).then_inc(s.ust_ready, 1)

        def head(l, h, prev):
            n = h + HEADS * l
            kcol = lambda chunk: small[:, bass.ds((h - 1) * 2 + (16 + chunk), 1)]
            act.wait_ge(s.tile_done, tile_done_at(l, 4 * h + T_H))
            if prev or l:
                act.wait_ge(s.rope_done, n)
            nc.scalar.activation(zs[:, 0, :], accum[0][:, 0:R], ACT.Copy)
            nc.scalar.activation(zw[0:64, 0, :], accum[0][64:P, 0:R], ACT.Copy)
            nc.scalar.activation(zw[64:P, 0, :], accum[0][0:64, 0:R], ACT.Copy).then_inc(acc_free[0], 1)
            if prev:
                act.wait_ge(s.s1_done, n)
                nc.scalar.activation(vrow[:, :], ps_tr[:, 0:2 * P], ACT.Copy)
                nc.scalar.activation(krow[:, 0:P], ps_tr[:, 2 * P:3 * P], ACT.Copy, scale=kcol(0))
                nc.scalar.activation(krow[:, P:2 * P], ps_tr[:, 3 * P:4 * P], ACT.Copy, scale=kcol(1))
                nc.scalar.activation(stack[:, :], ps_st[0:32, 0:2 * P], ACT.Copy).then_inc(s.rows_ready, 1)
            next_hi(l, 6 + h, 0, 4 * h + T_H)
            act.wait_ge(s.tile_done, tile_done_at(l, 4 * h + (T_H + 1)))
            nc.scalar.activation(zs[:, 1, :], accum[1][:, 0:R], ACT.Copy)
            nc.scalar.activation(zw[0:64, 1, :], accum[1][64:P, 0:R], ACT.Copy)
            nc.scalar.activation(zw[64:P, 1, :], accum[1][0:64, 0:R], ACT.Copy).then_inc(acc_free[1], 1)
            if prev:
                act.wait_ge(s.s2_done, n)
                act.wait_ge(s.sprompt_out, 16 * n - 15)
                nc.scalar.activation(s_prompt[:, :], ps_tr[:, 0:P], ACT.Copy, scale=cst[:, bass.ds((h - 1) + K_END, 1)]).then_inc(s.sprompt_ready, 1)
                act.wait_ge(s.sprompt_ready, n)
                act.dma_start(sp_out[bass.ds(n * P - P, P), :], s_prompt[:, :]).then_inc(s.sprompt_out, 16)
            next_hi(l, 6 + h, 1, 4 * h + (T_H + 1))
            act.wait_ge(s.tile_done, tile_done_at(l, 4 * h + (T_H + 2)))
            nc.scalar.activation(vt[:, :], accum[0][:, 0:R], ACT.Copy).then_inc(acc_free[0], 1)
            if prev:
                ret_samples_out(l, h)
            act.wait_ge(s.kv_ready, n + 1)
            nc.scalar.activation(stack_cols[:, 0, 0:2, :], wide(qks[:, 1, :], [P, 2, DEC]), ACT.Copy)
            nc.scalar.activation(stack_cols[:, 1, 0:4:2, :], wide(vs[:, :], [P, 2, DEC]), ACT.Copy).then_inc(s.khi_ready, 1)
            next_hi(l, 6 + h, 2, 4 * h + (T_H + 2))
            if isinstance(h, int) and h == 7:
                for c in range(4):
                    channel_silu(l, c)
            if prev:
                ret_normalise(l, h)
            next_hi(l, 6 + h, 3, 4 * h + (T_H + 3))
            if prev:
                ret_round(l, h)
            act.wait_ge(acc_free[1], read_out_at(l, 2 * h + (T_H // 2 + 1)))
            act.wait_ge(s.rt_ready, n + 1)
            nc.scalar.activation(sg[:, :], gz[:, :], ACT.Silu).then_inc(s.sg_ready, 1)
            if prev:
                state_in(l, h)

        def state_in(l, h):
            n = h + HEADS * l
            act.wait_ge(s.s3a_done, n)
            act.wait_ge(s.state_out, 16 * n)
            act.dma_start(s_new[:, :], s_ret[bass.ds(n * P, P), :]).then_inc(s.state_in, 16)

        def ret_samples_out(l, h):
            n = h + HEADS * l
            act.wait_ge(s.s3a_done, n)
            nc.scalar.activation(os_t[:, :], ps_st[:, 2 * P:2 * P + DEC], ACT.Copy).then_inc(s.os_ready, 1)
            act.dma_start(ss_out[bass.ds(n * P - P, P), :], s_new[:, :]).then_inc(s.state_out, 16)

        def ret_normalise(l, h):
            act.wait_ge(s.ret_rs, h + HEADS * l)
            for chunk in range(2):
                nc.scalar.activation(og[:, chunk, :], ps_o[:, chunk * P:(chunk + 1) * P], ACT.Identity,
                                     bias=nb_t[:, chunk:chunk + 1], scale=sc_t[:, chunk:chunk + 1])
            nc.scalar.activation(og[0:DEC, 2, :], ps_st[0:DEC, 3 * P:4 * P], ACT.Identity,
                                 bias=nb_t[0:DEC, 2:3], scale=sc_t[0:DEC, 2:3]).then_inc(s.og_ready, 1)

        def ret_round(l, h):
            act.wait_ge(s.rt_ready, h + (HEADS * l + 1))
            nc.scalar.activation(rows(b_hi, h - 1), rt[:, :], ACT.Copy).then_inc(s.rhi_ready, 1)

        def channel_silu(l, c):
            act.wait_ge(s.ln_scaled, 2 * l + 1 + c // 4)
            nc.scalar.activation(c_buf[:, c, :], c_buf[:, c, :], ACT.Silu, bias=vec(l, V_BCN + c), scale=vec(l, V_GCN + c)).then_inc(s.silu_ready, 1)

        u_flat = u_buf[:, :, :].rearrange("p c r -> p (c r)")
        act.dma_start(x[:, :, :], x_t).then_inc(s.x_in, 16)
        act.dma_start(cst[:, :], consts_d).then_inc(s.consts_in, 16)
        act.dma_start(vecs[:, :, :], vecs_d).then_inc(s.consts_in, 16)
        act.wait_ge(raw_in[0], 16)
        nc.scalar.activation(whi[:, 0, :], raw[:, 0, :], ACT.Copy).then_inc(s.hi_ready, 1)
        act.wait_ge(s.x_in, 16)
        act.wait_ge(s.consts_in, 32)
        for k in range(KT):
            nc.scalar.activation(a_hi[:, k, :], x[:, k, :], ACT.Copy, scale=vec(0, V_PRE + k)).then_inc(s.xhi_ready, 1)
        for j in range(1, 4):
            act.wait_ge(raw_in[j % RAW], 16 * (j // RAW + 1))
            nc.scalar.activation(whi[:, j, :], raw[:, j % RAW, :], ACT.Copy).then_inc(s.hi_ready, 1)
            if j == 1:
                for k in range(KT):
                    if k >= 2:
                        act.wait_ge(s.sq_used, k - 1)
                    nc.scalar.activation(sq[:, k % 2, :], x[:, k, :], ACT.Square).then_inc(s.sq_ready, 1)

        for l in range(DEPTH):
            if l:
                act.wait_ge(s.xnew, KT * l)
            act.dma_start(ust[:, :, 0:PAD, :], s_conv[P * l:P * l + P, :].rearrange("p (c k b) -> p c k b", c=CT, k=PAD)).then_inc(s.convstate_in, 16)
            with act.Fori(0, 4) as i:
                conv_in(l, i)
            act.wait_ge(s.ust_ready, CT * (l + 1))
            act.wait_ge(s.convstate_in, 16 * (l + 1))
            act.dma_start(scp_out[l, :, :, :], u_buf[:, :, SEQ:SEQ + PAD]).then_inc(s.scp_out, 16)
            act.dma_start(scs_out[P * l:P * l + P, :].rearrange("p (c k b) -> p c k b", c=CT, k=PAD), ust[:, :, 1:TAPS, :]).then_inc(s.scs_out, 16)
            with act.Fori(0, 2) as i:
                for j in range(4):
                    act.wait_ge(acc_free[j % 2], read_out_at(l, 2 * i + (T_G // 2 + j // 2)))
                    nc.scalar.activation(rows(gc_buf, 4 * i + j), tmp[j % 2][:, :], ACT.Silu).then_inc(s.gc_ready, 1)
                    next_hi(l, 4 + i, j, 4 * i + (T_G + j))
            if l:
                act.wait_ge(s.pin_ready, l)
            act.dma_start(p_in[:, :, :], p_t[l, :, :, :]).then_inc(s.p_in, 16)
            act.wait_ge(s.scs_out, 16 * (l + 1))
            act.wait_ge(s.sconv_step, 3 * (l + 1))
            act.dma_start(s_new[:, :], s_ret[HEADS * l * P:(HEADS * l + 1) * P, :]).then_inc(s.state_in, 16)
            head(l, 0, False)
            with act.Fori(1, 5) as h:
                head(l, h, True)
            head(l, 5, True)
            act.wait_ge(s.ln_centered, l + 1)
            act.wait_ge(s.scp_out, 16 * (l + 1))
            nc.scalar.activation(ln_sq[:, :, :], c_buf[:, :, :], ACT.Square).then_inc(s.ln_squared, 1)
            head(l, 6, True)
            head(l, 7, True)
            for c in range(4, CT):
                channel_silu(l, c)
            act.wait_ge(s.tile_done, tile_done_at(l, T_W - 1))
            act.wait_ge(s.silu_ready, CT * (l + 1))
            for c0, c1 in ((0, 2), (2, 4), (4, 8)):
                nc.scalar.activation(a_hi[:, c0:c1, :], c_buf[:, c0:c1, :], ACT.Copy).then_inc(s.chi_ready, 1)
            act.wait_ge(s.p_in, 16 * (l + 1))
            nc.scalar.activation(a_hi[:, CT:CT + PT, :], p_in[:, :, :], ACT.Copy).then_inc(s.phi_ready, 1)
            for j in range(4):
                if j == 0:
                    act.wait_ge(s.s1_done, HEADS * (l + 1))
                    nc.scalar.activation(vrow[:, :], ps_tr[:, 0:2 * P], ACT.Copy)
                    for chunk in range(2):
                        nc.scalar.activation(krow[:, chunk * P:(chunk + 1) * P], ps_tr[:, (2 + chunk) * P:(3 + chunk) * P], ACT.Copy,
                                             scale=kk[:, HEADS - 1, chunk:chunk + 1])
                    nc.scalar.activation(stack[:, :], ps_st[0:32, 0:2 * P], ACT.Copy).then_inc(s.rows_ready, 1)
                if j == 1:
                    act.wait_ge(s.s2_done, HEADS * (l + 1))
                    act.wait_ge(s.sprompt_out, 16 * HEADS * (l + 1) - 15)
                    nc.scalar.activation(s_prompt[:, :], ps_tr[:, 0:P], ACT.Copy, scale=cst[:, K_END + 7:K_END + 8]).then_inc(s.sprompt_ready, 1)
                    act.wait_ge(s.sprompt_ready, HEADS * (l + 1))
                    act.dma_start(sp_out[(HEADS * (l + 1) - 1) * P:HEADS * (l + 1) * P, :], s_prompt[:, :]).then_inc(s.sprompt_out, 16)
                if j == 2:
                    ret_samples_out(l, HEADS)
                if j == 3:
                    ret_normalise(l, HEADS)
                for e in range(2):
                    act.wait_ge(acc_free[e], read_out_at(l, T_W // 2 + j))
                    nc.scalar.activation(b_hi[:, CT + 2 * j + e, :], gc_buf[:, 2 * j + e, :], ACT.Copy).then_inc(s.cohi_ready, 1)
                next_hi(l, 14, j, T_W + 2 * j + 1)
            ret_round(l, HEADS)
            act.wait_ge(s.state_out, 16 * HEADS * (l + 1))
            act.wait_ge(s.sprompt_out, 16 * HEADS * (l + 1) + 1)

            def out_body(i, cols):
                for j in range(4):
                    act.wait_ge(s.tile_done, tile_done_at(l, 4 * i + (T_O + j)))
                    square(4 * i + (squares_at(l) + j), j % 2, accum[j % 2][:, 0:R])
                    nc.scalar.activation(rows(m_buf, 4 * i + j), accum[j % 2][:, 0:R], ACT.Copy, scale=vec(l, 4 * i + (V_POST + j))).then_inc(acc_free[j % 2], 1)
                    next_hi(l, 15 + i, j, 4 * i + (T_O + j), cols)

            with act.Fori(0, 3) as i:
                out_body(i, SLAB)
            out_body(3, 4 * PT * P)
            for j in range(4):
                for e in range(4):
                    act.wait_ge(s.tile_done, tile_done_at(l, T_P + 4 * j + e))
                    square(squares_at(l) + KT + 4 * j + e, e % 2, accum[e % 2][:, 0:R])
                    nc.scalar.activation(e_buf[:, 4 * j + e, :], accum[e % 2][:, 0:R], ACT.Copy, scale=vec(l, V_PLE + 4 * j + e)).then_inc(acc_free[e % 2], 1)
                next_hi(l, 19, j, T_P + 4 * j + 3)
                for g in {2: (0, 1), 3: (2, 3)}.get(j, ()):
                    act.wait_ge(s.h_step, 8 * l + (3, 5, 7, 8)[g])
                    nc.scalar.activation(b_hi[:, 4 * g:4 * g + 4, :], x[:, 4 * g:4 * g + 4, :], ACT.Copy).then_inc(s.hhi_ready, 1)

            def gate_tile(i, j, first):
                t = 4 * i + j
                act.wait_ge(s.tile_done, tile_done_at(l, t + T_T))
                if not first or j >= 2:
                    act.wait_ge(s.xnew, t + (KT * l - 1))
                nc.scalar.activation(tmp[j % 2][:, :], accum[j % 2][:, 0:R], ACT.Tanh, scale=0.5).then_inc(acc_free[j % 2], 1)
                if l + 1 < DEPTH or not isinstance(i, int) or i < 3:
                    next_hi(l, 20 + i, j, t + T_T)
                if l + 1 < DEPTH and not (first and j < 2):
                    next_x(t - 2)

            def next_x(t):
                act.wait_ge(s.xnew, t + (KT * l + 1))
                act.wait_ge(s.sq_used, t + (squares_at(l) + 2 * KT - 1))
                nc.scalar.activation(rows(a_hi, t), rows(x, t), ACT.Copy, scale=vec(l + 1, t + V_PRE)).then_inc(s.xhi_ready, 1)
                nc.scalar.activation(sq[:, side_of[0] % 2, :], rows(x, t), ACT.Square).then_inc(s.sq_ready, 1)
                side_of[0] += 1

            side_of = [0]
            for j in range(4):
                gate_tile(0, j, True)
            with act.Fori(1, 3) as i:
                for j in range(4):
                    gate_tile(i, j, False)
            for j in range(4):
                gate_tile(3, j, False)
            if l + 1 < DEPTH:
                next_x(KT - 2)
                next_x(KT - 1)

    @block.vector
    def _(dve):
        v = nc.vector
        dw = lambda l, at: vecs[:, l, bass.ds(at + V_DW, 1)]

        def lo(l, body, slot, cols=SLAB):
            dve.wait_ge(s.hi_ready, body * 4 + (SLABS * l + slot + 1))
            v.tensor_tensor(wlo[:, slot, 0:cols], raw[:, slot % RAW, 0:cols], whi[:, slot, 0:cols].bitcast(F32), ALU.subtract).then_inc(s.lo_ready, 1)

        def x_lo(l, t):
            dve.wait_ge(s.xhi_ready, t + (KT * l + 1))
            v.scalar_tensor_tensor(rows(a_lo, t), rows(x, t), vec(l, t + V_PRE), rows(a_hi, t).bitcast(F32), ALU.mult, ALU.subtract).then_inc(s.xin_ready, 1)

        def stat_scale(l, k, width):
            dve.wait_ge(s.sum_done, stat_at(l, k))
            v.tensor_scalar(st[:, 0:2], ps_p[:, 0:2], 1.0 / width, EPS, ALU.mult, ALU.add)
            v.tensor_scalar(st[0:DEC, 2:3], ps_p[0:DEC, 2:3], 1.0 / width, EPS, ALU.mult, ALU.add).then_inc(s.stat_scaled, 1)

        def stat_diag(l, k):
            dve.wait_ge(s.stat_rs, stat_at(l, k))
            v.tensor_scalar(diag[:, 0:P], ident, rs[:, 0:1], None, ALU.mult)
            v.tensor_scalar(diag[:, P:2 * P], ident, rs[:, 1:2], None, ALU.mult)
            v.tensor_scalar(diag[0:DEC, 2 * P:R], cst[0:DEC, K_ID:K_ID + DEC], rs[0:DEC, 2:3], None, ALU.mult).then_inc(s.diag_ready, 1)

        def stat_read(l, k, dst, by=1.0):
            dve.wait_ge(s.bcast_done, stat_at(l, k))
            v.tensor_scalar(dst[:, :], ps_p[:, 0:R], by, None, ALU.mult).then_inc(s.bcast_read, 1)

        def factors(l):
            at = 6 * l
            dve.wait_ge(s.bcast_read, spread_at(l, ST_X))
            v.tensor_tensor(r2, rs[:, 0:2], rs[:, 0:2], ALU.mult).then_inc(s.rfac_step, 1)
            v.tensor_copy(rx3[:, 0:2], rs[:, 0:2]).then_inc(s.rfac_step, 1)
            v.tensor_copy(rs8[:, 0, :], r_x[:, SEQ:R]).then_inc(s.rfac_step, 1)
            v.tensor_scalar(rs8[:, 1, :], r_x[:, SEQ:R], P ** -0.5, None, ALU.mult).then_inc(s.rfac_step, 1)
            dve.wait_ge(s.rfac_step, at + 4)
            v.tensor_tensor(kk, cst[:, K_KDEC:K_KDEC + 16].rearrange("p (h c) -> p h c", c=2), wide(r2, [P, HEADS, 2]), ALU.mult)
            v.tensor_tensor(gi, cst[:, K_GI:K_GI + 24].rearrange("p (h c) -> p h c", c=3), wide(rx3, [P, HEADS, 3]), ALU.mult).then_inc(s.rfac_step, 1)
            dve.wait_ge(s.rfac_step, at + 5)
            v.tensor_tensor(g2, gi, gi, ALU.mult).then_inc(s.rfac_step, 1)

        def conv_b(l, ct, first=False):
            dve.wait_ge(s.tile_done, tile_done_at(l, 2 * ct))
            v.tensor_tensor(tmp[0][:, :], accum[0][:, 0:R], r_x[:, :], ALU.mult).then_inc(acc_free[0], 1)

        def conv_a(l, ct, first=False):
            dve.wait_ge(s.tile_done, tile_done_at(l, 2 * ct + 1))
            if not first:
                dve.wait_ge(s.u_ready, ct + CT * l)
            v.scalar_tensor_tensor(tmp[1][:, :], accum[1][:, 0:R], 0.5, r_x[:, :], ALU.mult, ALU.mult).then_inc(acc_free[1], 1)

        def conv_u(l, ct):
            dve.wait_ge(s.tanh_ready, ct + (CT * l + 1))
            dve.wait_ge(acc_free[1], read_out_at(l, ct))
            v.scalar_tensor_tensor(u_flat[:, bass.ds(ct * UW + PAD, R)], tmp[2][:, :], 1.0, tmp[1][:, :], ALU.add, ALU.mult).then_inc(s.u_ready, 1)

        def taps(l, ct, k0, k1):
            for k in range(k0, k1):
                before = ct * 32 + (32 * CT * l + k)
                even = c_flat[:, bass.ds(ct * R, SEQ)]
                out = even if k % 2 == 0 else tmp[3][:, 0:SEQ]
                src = u_flat[:, bass.ds(ct * UW + k, SEQ)]
                w = dw(l, ct * TAPS + k)
                if k == 0:
                    dve.wait_ge(s.u_ready, ct + (CT * l + 1))
                    v.tensor_scalar(out, src, w, vec(l, ct + V_BDW), ALU.mult, ALU.add).then_inc(s.tap_done, 1)
                elif k == 1:
                    dve.wait_ge(s.tap_done, before)
                    v.tensor_scalar(out, src, w, None, ALU.mult).then_inc(s.tap_done, 1)
                else:
                    dve.wait_ge(s.tap_done, before - 1)
                    v.scalar_tensor_tensor(out, src, w, out, ALU.mult, ALU.add).then_inc(s.tap_done, 1)
            if k1 == TAPS:
                dve.wait_ge(s.tap_done, ct * 32 + (32 * CT * l + TAPS))
                v.tensor_tensor(even, even, tmp[3][:, 0:SEQ], ALU.add).then_inc(s.tap_done, 1)

        def sample_conv(l):
            at = 3 * l
            dve.wait_ge(s.ust_ready, CT * (l + 1))
            dve.wait_ge(s.convstate_in, 16 * (l + 1))
            w = vecs[:, l, V_DW:VW].rearrange("p (c k) -> p c k", c=CT).unsqueeze(2).to_broadcast([P, CT, DEC, TAPS])
            v.tensor_tensor(sprod[:, :, :, :], ust[:, :, :, :].rearrange("p c k b -> p c b k"), w, ALU.mult).then_inc(s.sconv_step, 1)
            dve.wait_ge(s.sconv_step, at + 1)
            v.tensor_reduce(r_t[:, 0:CT * DEC], sprod[:, :, :, :].rearrange("p c b k -> p (c b) k"), AX.X, ALU.add).then_inc(s.sconv_step, 1)
            dve.wait_ge(s.sconv_step, at + 2)
            bias = vecs[:, l, V_BDW:V_BDW + CT].unsqueeze(2).to_broadcast([P, CT, DEC])
            v.tensor_tensor(c_buf[:, :, SEQ:R], r_t[:, 0:CT * DEC].rearrange("p (c b) -> p c b", c=CT), bias, ALU.add).then_inc(s.sconv_step, 1)

        def ret_scores(l, h):
            dve.wait_ge(s.s1_done, h + HEADS * l)
            kcol = lambda chunk: small[:, bass.ds((h - 1) * 2 + (16 + chunk), 1)]
            v.scalar_tensor_tensor(pmat[:, 0:P], ps_p[:, 0:P], kcol(0), tri, ALU.mult, ALU.mult)
            v.tensor_scalar(pmat[:, P:2 * P], ps_p[:, P:2 * P], kcol(0), None, ALU.mult)
            v.scalar_tensor_tensor(pmat[:, 2 * P:3 * P], ps_p[:, 2 * P:3 * P], kcol(1), tri, ALU.mult, ALU.mult).then_inc(s.p_ready, 1)

        def ret_blocks(l, h):
            dve.wait_ge(s.rows_ready, h + HEADS * l)
            v.tensor_tensor(vbd[:, :, :], wide(stack[:, P:2 * P].bitcast(F32), [32, DEC, P]),
                            cst[0:32, K_MASK:K_MASK + DEC].unsqueeze(2).to_broadcast([32, DEC, P]), ALU.mult).then_inc(s.vbd_ready, 1)

        def ret_state(l, h):
            n = h + HEADS * l
            gamma = cst[:, bass.ds((h - 1) + K_GAM, 1)]
            dve.wait_ge(s.s2_done, n)
            dve.wait_ge(s.state_in, 16 * n)
            v.scalar_tensor_tensor(s_new[:, 0:4 * P], s_new[:, 0:4 * P], gamma, ps_s0[:, :], ALU.mult, ALU.add)
            v.scalar_tensor_tensor(s_new[:, 4 * P:8 * P], s_new[:, 4 * P:8 * P], gamma, ps_s1[:, :], ALU.mult, ALU.add).then_inc(s.snew_ready, 1)
            v.bn_stats(bn[:, 0:6], ps_o[:, 0:P])
            v.bn_stats(bn[:, 6:12], ps_o[:, P:2 * P]).then_inc(s.bn_done, 1)

        def ret_stats(l, h):
            n = h + HEADS * l
            dve.wait_ge(s.s3b_done, n)
            v.bn_stats(bn[0:DEC, 12:18], ps_st[0:DEC, 3 * P:4 * P]).then_inc(s.bn_done, 1)
            dve.wait_ge(s.bn_done, 2 * n)
            v.memset(held, 0.0)
            v.bn_aggr(mv[:, 0, :], bn[:, 0:6])
            v.bn_aggr(mv[:, 1, :], bn[:, 6:12])
            v.bn_aggr(mv[0:DEC, 2, :], bn[0:DEC, 12:18]).then_inc(s.stat_ready, 1)

        def ret_gate(l, h):
            n = h + HEADS * l
            dve.wait_ge(s.s4_done, n)
            dve.wait_ge(s.sg_ready, n + 1)
            if not isinstance(h, int) or h > 1 or l:
                dve.wait_ge(s.ret_ready, n - 1)
            v.scalar_tensor_tensor(rt[:, :], ps_tr[:, 0:R], vec(l, (h - 1) + V_RET), sg[:, :], ALU.mult, ALU.mult).then_inc(s.rt_ready, 1)

        def ret_lo(l, h):
            dve.wait_ge(s.rhi_ready, h + HEADS * l)
            v.tensor_tensor(rows(b_lo, h - 1), rt[:, :], rows(b_hi, h - 1).bitcast(F32), ALU.subtract).then_inc(s.ret_ready, 1)

        def head(l, h, prev, conv=((), (), (), ())):
            n = h + HEADS * l
            body = 7 + h
            if prev:
                ret_scores(l, h)
            lo(l, body, 0)
            if prev:
                ret_blocks(l, h)
            for piece in conv[0]:
                piece()
            dve.wait_ge(acc_free[1], read_out_at(l, 2 * h + T_H // 2))
            v.tensor_tensor(zs[:, :, :], zs[:, :, :], wide(cst[:, K_COS:K_COS + R], [P, 2, R]), ALU.mult).then_inc(s.rope_step, 1)
            v.tensor_tensor(zw[:, :, :], zw[:, :, :], wide(cst[:, K_SIN:K_SIN + R], [P, 2, R]), ALU.mult).then_inc(s.rope_step, 1)
            if prev:
                ret_state(l, h)
            dve.wait_ge(s.rope_step, 2 * n + 2)
            v.tensor_tensor(qk[:, :, :], zs[:, :, :], zw[:, :, :], ALU.add).then_inc(s.rope_done, 1)
            lo(l, body, 1)
            for piece in conv[1]:
                piece()
            dve.wait_ge(acc_free[0], read_out_at(l, 2 * h + (T_H // 2 + 1)))
            if prev:
                dve.wait_ge(s.s3a_done, n)
            dve.wait_ge(s.rope_done, n + 1)
            v.tensor_tensor(qks[:, :, :], qk[:, :, SEQ:R], rs8, ALU.mult)
            v.tensor_tensor(vs[:, :], vt[:, SEQ:R], r_x[:, SEQ:R], ALU.mult).then_inc(s.kv_ready, 1)
            lo(l, body, 2)
            dve.wait_ge(s.khi_ready, n + 1)
            v.tensor_tensor(stack_cols[:, 0, 2:4, :], wide(qks[:, 1, :], [P, 2, DEC]), stack_cols[:, 0, 0:2, :].bitcast(F32), ALU.subtract)
            v.tensor_tensor(stack_cols[:, 1, 1:4:2, :], wide(vs[:, :], [P, 2, DEC]), stack_cols[:, 1, 0:4:2, :].bitcast(F32), ALU.subtract).then_inc(s.stack_in, 1)
            for piece in conv[2]:
                piece()
            if prev:
                ret_stats(l, h)
            dve.wait_ge(s.tile_done, tile_done_at(l, 4 * h + (T_H + 3)))
            dve.wait_ge(s.sg_ready, n + 1)
            v.tensor_tensor(gz[:, :], accum[1][:, 0:R], r_x[:, :], ALU.mult).then_inc(acc_free[1], 1)
            if prev:
                ret_gate(l, h)
            lo(l, body, 3)
            if prev:
                ret_lo(l, h)
            for piece in conv[3]:
                piece()

        u_flat = u_buf[:, :, :].rearrange("p c r -> p (c r)")
        c_flat = c_buf[:, :, :].rearrange("p c r -> p (c r)")
        v.memset(small[:, :], 0.0).then_inc(s.small_set, 1)
        dve.wait_ge(s.small_set, 1)
        v.memset(st[:, 2:3], 1.0).then_inc(acc_free[0], 1)
        v.memset(eps3, EPS)
        v.memset(minus_half, -0.5).then_inc(acc_free[1], 1)
        v.memset(rx3[:, 2:3], 1.0).then_inc(s.rt_ready, 1)
        v.memset(ones[:, :], 1.0).then_inc(s.sg_ready, 1)
        v.memset(ones_mean[:, :], 1.0 / CONV).then_inc(s.consts_set, 1)
        v.memset(r_x[:, 0:1], 0.0).then_inc(s.gc_ready, 1)
        v.memset(r_t[:, 0:1], 0.0).then_inc(s.sprompt_out, 1)
        dve.wait_ge(s.consts_in, 32)
        dve.wait_ge(s.gc_ready, 1)
        lo(0, 0, 0)
        for k in range(KT):
            x_lo(0, k)
        for j in range(1, 4):
            lo(0, 0, j)

        for l in range(DEPTH):
            last = l == DEPTH - 1
            v.memset(u_buf[:, :, 0:PAD], 0.0).then_inc(s.pad_set, 1)
            dve.wait_ge(s.pad_set, l + 1)
            stat_scale(l, ST_X, D_MODEL)
            stat_diag(l, ST_X)
            stat_read(l, ST_X, r_x)
            dve.wait_ge(s.bcast_read, spread_at(l, ST_X))
            for j in range(4):
                (conv_b, conv_a)[j % 2](l, j // 2, j == 1 and l == 0)
                lo(l, 1, j)
                if j % 2:
                    conv_u(l, j // 2)
            factors(l)
            with dve.Fori(1, 4) as i:
                for j in range(4):
                    (conv_b, conv_a)[j % 2](l, 2 * i + j // 2)
                    lo(l, 1 + i, j)
                    if j % 2:
                        conv_u(l, 2 * i + j // 2)
                    taps(l, i - 1, 8 * j, min(8 * j + 8, TAPS))
            sample_conv(l)
            with dve.Fori(0, 2) as i:
                for j in range(4):
                    dve.wait_ge(s.tile_done, tile_done_at(l, 4 * i + (T_G + j)))
                    dve.wait_ge(s.gc_ready, 4 * i + (CT * l + j + 1))
                    v.tensor_tensor(tmp[j % 2][:, :], accum[j % 2][:, 0:R], r_x[:, :], ALU.mult).then_inc(acc_free[j % 2], 1)
                    lo(l, 5 + i, j)
                    taps(l, i + 3, 8 * j, min(8 * j + 8, TAPS))
            split = lambda ct: [(lambda j=j: taps(l, ct, 8 * j, min(8 * j + 8, TAPS)),) for j in range(4)]
            halves = lambda ct, half: [(lambda j=j: taps(l, ct, 16 * half + 4 * j, min(16 * half + 4 * j + 4, TAPS)),) for j in range(4)]
            head(l, 0, False, split(5))
            with dve.Fori(0, 2) as i:
                for half in range(2):
                    head(l, 2 * i + (1 + half), True, halves(i + 6, half))

            def channel_sum(src, dst):
                v.tensor_reduce(dst[:, :], src[:, :, :].rearrange("p c r -> p r c"), AX.X, ALU.add).then_inc(s.ln_summed, 1)

            def mean_sum():
                dve.wait_ge(s.tap_done, 32 * CT * (l + 1))
                dve.wait_ge(s.sconv_step, 3 * (l + 1))
                channel_sum(c_buf, acc[(3 * l + 1) % 2])

            def centre():
                dve.wait_ge(s.mean_done, l + 1)
                v.tensor_tensor(c_buf[:, :, :], c_buf[:, :, :], wide(ps_p[:, 0:R], [P, CT, R]), ALU.subtract).then_inc(s.ln_centered, 1)

            def var_sum():
                dve.wait_ge(s.ln_squared, l + 1)
                channel_sum(ln_sq, acc[3 * l % 2])

            def norm():
                dve.wait_ge(s.bcast_done, stat_at(l, ST_LN))
                for half in range(2):
                    part = c_buf[:, 4 * half:4 * half + 4, :]
                    v.tensor_tensor(part, part, wide(ps_p[:, 0:R], [P, 4, R]), ALU.mult).then_inc(s.ln_scaled, 1)

            head(l, 5, True, ((mean_sum,), (), (centre,), ()))
            head(l, 6, True, ((var_sum,), (), (lambda: stat_scale(l, ST_LN, CONV),), (lambda: stat_diag(l, ST_LN),)))
            head(l, 7, True, ((), (), (norm,), ()))
            for part, (c0, c1) in enumerate(((0, 2), (2, 4), (4, 8))):
                dve.wait_ge(s.chi_ready, 3 * l + part + 1)
                v.tensor_tensor(a_lo[:, c0:c1, :], c_buf[:, c0:c1, :], a_hi[:, c0:c1, :].bitcast(F32), ALU.subtract).then_inc(s.c_ready, 1)
            for j in range(4):
                if j == 0:
                    ret_scores(l, HEADS)
                    ret_blocks(l, HEADS)
                    dve.wait_ge(s.phi_ready, l + 1)
                    v.tensor_tensor(a_lo[:, CT:CT + PT, :], p_in[:, :, :], a_hi[:, CT:CT + PT, :].bitcast(F32), ALU.subtract).then_inc(s.pin_ready, 1)
                if j == 1:
                    ret_state(l, HEADS)
                if j == 3:
                    ret_stats(l, HEADS)
                for e in range(2):
                    c = 2 * j + e
                    dve.wait_ge(s.tile_done, tile_done_at(l, T_W + c))
                    dve.wait_ge(s.gc_ready, CT * (l + 1) + 1)
                    v.scalar_tensor_tensor(gc_buf[:, c, :], accum[e][:, 0:R], vec(l, V_BPW + c), gc_buf[:, c, :], ALU.add, ALU.mult).then_inc(acc_free[e], 1)
                for e in range(2):
                    c = 2 * j + e
                    dve.wait_ge(s.cohi_ready, CT * l + c + 1)
                    v.tensor_tensor(b_lo[:, CT + c, :], gc_buf[:, c, :], b_hi[:, CT + c, :].bitcast(F32), ALU.subtract).then_inc(s.cout_ready, 1)
                lo(l, 15, j)
            ret_gate(l, HEADS)
            ret_lo(l, HEADS)
            with dve.Fori(0, 3) as i:
                for j in range(4):
                    lo(l, 16 + i, j)
            for j in range(4):
                lo(l, 19, j, 4 * PT * P)
            stat_scale(l, ST_M, D_MODEL)
            stat_diag(l, ST_M)
            lo(l, 20, 0)
            stat_read(l, ST_M, r_t)
            dve.wait_ge(s.bcast_read, spread_at(l, ST_M))
            for bank in range(2):
                dve.wait_ge(acc_free[bank], read_out_at(l, T_P // 2 - 1))
            group = lambda t, g: t[:, 4 * g:4 * g + 4, :]

            def scale_m(g):
                v.tensor_tensor(group(m_buf, g), group(m_buf, g), wide(r_t[:, :], [P, 4, R]), ALU.mult).then_inc(s.h_step, 1)

            def add_m(g, behind):
                dve.wait_ge(s.h_step, 8 * l + behind)
                v.tensor_tensor(group(x, g), group(x, g), group(m_buf, g), ALU.add).then_inc(s.h_step, 1)

            def h_lo(g):
                dve.wait_ge(s.hhi_ready, 4 * l + g + 1)
                v.tensor_tensor(group(b_lo, g), group(x, g), group(b_hi, g).bitcast(F32), ALU.subtract).then_inc(s.h_ready, 1)

            scale_m(0)
            scale_m(1)
            add_m(0, 1)
            scale_m(2)
            add_m(1, 2)
            lo(l, 20, 1)
            scale_m(3)
            add_m(2, 4)
            h_lo(0)
            lo(l, 20, 2)
            add_m(3, 6)
            h_lo(1)
            lo(l, 20, 3)
            h_lo(2)
            h_lo(3)
            def gate_mul(t, j):
                dve.wait_ge(acc_free[j % 2], pair_read(l, t, j))
                v.scalar_tensor_tensor(tmp[2 + j % 2][:, :], tmp[j % 2][:, :], 1.0, rows(e_buf, t), ALU.add, ALU.mult).then_inc(s.gate_step, 1)

            def pair_read(l, t, j):
                return read_out_at(l, t // 2 + T_T // 2) if isinstance(t, int) else read_out_at(l, pair_at[0] + (T_T // 2 + j // 2))

            def gate_add(t):
                dve.wait_ge(s.gate_step, t + (KT * l + 1))
                v.tensor_tensor(rows(x, t), rows(x, t), tmp[2 + side_at[0] % 2][:, :], ALU.add).then_inc(s.xnew, 1)

            pair_at, side_at = [0], [0]
            stat_scale(l, ST_E, D_MODEL)
            stat_diag(l, ST_E)
            lo(l, 21, 0)
            stat_read(l, ST_E, r_t, 0.5)
            dve.wait_ge(s.bcast_read, spread_at(l, ST_E))
            for g in range(4):
                v.tensor_tensor(group(e_buf, g), group(e_buf, g), wide(r_t[:, :], [P, 4, R]), ALU.mult).then_inc(s.e_step, 1)
            for j in range(4):
                if j:
                    lo(l, 21, j)
                if j == 0:
                    dve.wait_ge(s.e_step, 4 * l + 4)
                gate_mul(j, j)
                side_at[0] = j
                gate_add(j)
                if j and not last:
                    x_lo(l + 1, j - 1)

            def gate_body(i, more):
                for j in range(4):
                    t = 4 * i + j
                    pair_at[0] = 2 * i
                    gate_mul(t, j)
                    if more:
                        lo(l, 21 + i, j)
                    side_at[0] = j
                    gate_add(t)
                    if not last:
                        x_lo(l + 1, t - 1)

            with dve.Fori(1, 3) as i:
                gate_body(i, True)
            gate_body(3, not last)
            if not last:
                x_lo(l + 1, KT - 1)

    @block.gpsimd
    def _(pool):
        def add_squares(l_at, buf, count=KT):
            for k in range(count):
                n = l_at + k
                pool.wait_ge(s.sq_ready, n + 1)
                if k == 0:
                    if n:
                        pool.wait_ge(s.sq_used, n)
                    nc.gpsimd.tensor_copy(buf[:, :], sq[:, n % 2, :]).then_inc(s.sq_used, 1)
                else:
                    pool.wait_ge(s.sq_used, n)
                    nc.gpsimd.tensor_tensor(buf[:, :], buf[:, :], sq[:, n % 2, :], ALU.add).then_inc(s.sq_used, 1)

        def root(l, k):
            pool.wait_ge(s.stat_scaled, stat_at(l, k))
            nc.gpsimd.tensor_tensor(rs, st, minus_half, ALU.pow).then_inc(s.stat_rs, 1)

        def ret_root(l, h):
            n = h + HEADS * l
            at = 5 * n
            pool.wait_ge(s.stat_ready, n + 1)
            g2_h = small[:, bass.ds(h * 3 + 56, 3)]
            gi_h = small[:, bass.ds(h * 3 + 32, 3)]
            nc.gpsimd.tensor_tensor(var_t, mv[:, :, 1], g2_h, ALU.mult).then_inc(s.pool_step, 1)
            pool.wait_ge(s.pool_step, at + 1)
            nc.gpsimd.tensor_tensor(var_t, var_t, eps3, ALU.add).then_inc(s.pool_step, 1)
            pool.wait_ge(s.pool_step, at + 2)
            nc.gpsimd.tensor_tensor(rs_t, var_t, minus_half, ALU.pow).then_inc(s.pool_step, 1)
            pool.wait_ge(s.pool_step, at + 3)
            nc.gpsimd.tensor_tensor(sc_t, rs_t, gi_h, ALU.mult).then_inc(s.pool_step, 1)
            pool.wait_ge(s.pool_step, at + 4)
            nc.gpsimd.tensor_tensor(mean_sc, mv[:, :, 0], sc_t, ALU.mult).then_inc(s.pool_step, 1)
            pool.wait_ge(s.pool_step, at + 5)
            nc.gpsimd.tensor_tensor(nb_t, zero3, mean_sc, ALU.subtract).then_inc(s.ret_rs, 1)

        add_squares(0, acc[0])
        for l in range(DEPTH):
            root(l, ST_X)
            with pool.Fori(0, 6) as h:
                ret_root(l, h)
            root(l, ST_LN)
            ret_root(l, 6)
            ret_root(l, 7)
            pool.wait_ge(s.mean_done, l + 1)
            add_squares(squares_at(l), acc[(3 * l + 1) % 2])
            root(l, ST_M)
            pool.wait_ge(s.sum_done, stat_at(l, ST_LN))
            add_squares(squares_at(l) + KT, acc[3 * l % 2])
            root(l, ST_E)
            if l < DEPTH - 1:
                add_squares(squares_at(l) + 2 * KT, acc[(3 * l + 1) % 2])


def kernel(x_prompt, x_sample, state_ret, state_conv, p_prompt, p_sample, w_in, w_out, g_ret, w_dw,
           b_dw, g_cn, b_cn, w_pw2, b_pw2, g_pre, g_post, w_ple, g_ple, w_ple_gate):
    import concourse.bacc as bacc
    from concourse.bass_utils import run_bass_kernel_spmd

    def slabs(w, per_tile, tiles_per_slab):
        d, rows_in, cols = w.shape
        k = rows_in // P
        t = w.reshape(d, k, P, cols // (P * tiles_per_slab), tiles_per_slab, P)
        t = t.transpose(0, 3, 2, 4, 1, 5)
        return np.ascontiguousarray(t).reshape(-1, tiles_per_slab * k * P)

    def features_down(rows_by_features):
        r, f = rows_by_features.shape
        return rows_by_features.reshape(r, f // P, P).transpose(2, 1, 0)

    a = {k: np.asarray(w) for k, w in dict(
        x_prompt=x_prompt, x_sample=x_sample, state_ret=state_ret, state_conv=state_conv, p_prompt=p_prompt,
        p_sample=p_sample, w_in=w_in, w_out=w_out, g_ret=g_ret, w_dw=w_dw, b_dw=b_dw, g_cn=g_cn, b_cn=b_cn,
        w_pw2=w_pw2, b_pw2=b_pw2, g_pre=g_pre, g_post=g_post, w_ple=w_ple, g_ple=g_ple, w_ple_gate=w_ple_gate).items()}
    x_all = np.concatenate([a["x_prompt"][0], a["x_sample"][:, 0]])
    p_all = np.concatenate([a["p_prompt"][:, 0], a["p_sample"][:, :, 0]], axis=1)
    column = lambda w: w.reshape(DEPTH, -1, P).transpose(2, 0, 1)
    dw = a["w_dw"].reshape(DEPTH, TAPS, CT, P).transpose(3, 0, 2, 1).reshape(P, DEPTH, CT * TAPS)
    vectors = [column(a[n]) for n in ("g_pre", "g_post", "g_ple", "g_ret", "b_dw", "g_cn", "b_cn", "b_pw2")] + [dw]
    conv_state = a["state_conv"].reshape(DEPTH, DEC, PAD, CT, P).transpose(0, 4, 3, 2, 1)
    ins = {
        "x_t": features_down(x_all),
        "p_t": np.stack([features_down(p) for p in p_all]),
        "s_ret": a["state_ret"].transpose(0, 2, 3, 1, 4).reshape(DEPTH * HEADS * P, DEC * P),
        "s_conv": conv_state.reshape(DEPTH * P, CT * PAD * DEC),
        "vecs": np.concatenate(vectors, axis=2),
        "consts": constants(),
        "w_in": slabs(a["w_in"], KT, 1),
        "w_pw": slabs(a["w_pw2"], CT, 2),
        "w_out": slabs(a["w_out"], KT, 1),
        "w_ple": slabs(a["w_ple"], PT, 4),
        "w_gate": slabs(a["w_ple_gate"], KT, 1),
    }
    outs = {
        "y_t": (P, KT, R),
        "sp_out": (DEPTH * HEADS * P, P),
        "scp_out": (DEPTH, P, CT, PAD),
        "ss_out": (DEPTH * HEADS * P, DEC * P),
        "scs_out": (DEPTH * P, CT * PAD * DEC),
    }
    nc = bacc.Bacc("TRN2", target_bir_lowering=False, num_devices=1, dynamic_dma_scratch_size=1024)
    ins = {k: np.ascontiguousarray(w) for k, w in ins.items()}
    args = [nc.dram_tensor(k, w.shape, F32, kind="ExternalInput").ap() for k, w in ins.items()]
    args += [nc.dram_tensor(k, shape, F32, kind="ExternalOutput").ap() for k, shape in outs.items()]
    with ExitStack() as ctx:
        build(nc, ctx, *args)
    got = run_bass_kernel_spmd(nc, [ins], core_ids=[0]).results[0]
    y = got["y_t"].transpose(2, 1, 0).reshape(R, D_MODEL)
    new_states = got["ss_out"].reshape(DEPTH, HEADS, P, DEC, P).transpose(0, 3, 1, 2, 4)
    conv_prompt = got["scp_out"].transpose(0, 3, 2, 1).reshape(DEPTH, 1, PAD, CONV)
    conv_sample = got["scs_out"].reshape(DEPTH, P, CT, PAD, DEC).transpose(0, 4, 3, 2, 1).reshape(DEPTH, DEC, PAD, CONV)
    return (y[:SEQ].reshape(1, SEQ, D_MODEL), y[SEQ:].reshape(DEC, 1, D_MODEL),
            got["sp_out"].reshape(DEPTH, 1, HEADS, P, P), conv_prompt, new_states, conv_sample)
```

```python
import numpy as np
import concourse.bass as bass
from concourse import mybir
from contextlib import ExitStack

F32 = mybir.dt.float32
F32R = mybir.dt.float32r
ACT = mybir.ActivationFunctionType
ALU = mybir.AluOpType
AX = mybir.AxisListType

P = 128
DEPTH, D_MODEL, SEQ, DEC, PAST = 2, 2048, 256, 8, 2048
HEADS, CONV, TAPS, P_DIM = 8, 1024, 31, 256
EPS = 1e-6
R = SEQ + DEC
KT = D_MODEL // P
CT = CONV // P
PT = P_DIM // P
PAD = TAPS - 1
UW = PAD + R
SLAB = KT * P
RING, RAW = 4, 2

T_C, T_H, T_G, T_W, T_O, T_P, T_T, TILES = 0, 16, 48, 56, 64, 80, 96, 112
S_C, S_H, S_G, S_W, S_O, S_P, S_T, SLABS = 0, 16, 48, 56, 60, 76, 80, 96

V_PRE, V_POST, V_PLE, V_RET, V_BDW, V_GCN, V_BCN, V_BPW, V_DW = 0, 16, 32, 48, 56, 64, 72, 80, 88
VW = V_DW + CT * TAPS

K_ID, K_TRI, K_COS, K_SIN = 0, P, 2 * P, 2 * P + R
K_KDEC = K_SIN + R
K_GI = K_KDEC + 2 * HEADS
K_GAM = K_GI + 3 * HEADS
K_END = K_GAM + HEADS
K_MASK = K_END + HEADS
KW = K_MASK + DEC


CONV_0, CONV_H0, CONV_C, CONV_1, CONV_2, CONV_3 = 12, 25, 22, 22, 13, 27
TAPS_DONE = CT * TAPS + 3 + 3 * 2 + 2 * 2 + 3 + 2


def constants():
    c = np.zeros((P, KW), np.float32)
    c[:, K_ID:K_ID + P] = np.eye(P)
    c[:, K_TRI:K_TRI + P] = np.triu(np.ones((P, P)))
    half = P // 2
    inv = (10000.0 ** -(np.arange(half) / half)).astype(np.float32)
    pos = np.concatenate([np.arange(SEQ), np.full(DEC, PAST)]).astype(np.float32)
    ang = (pos[None, :] * inv[:, None]).astype(np.float32)
    cos, sin = np.cos(ang.astype(np.float64)), np.sin(ang.astype(np.float64))
    c[:, K_COS:K_COS + R] = np.concatenate([cos, cos])
    c[:, K_SIN:K_SIN + R] = np.concatenate([-sin, sin])
    log_g = np.log1p(-np.exp2(-5.0 - np.arange(HEADS)))
    row = np.arange(P)
    for h in range(HEADS):
        for chunk in range(2):
            c[:, K_KDEC + 2 * h + chunk] = np.exp(-log_g[h] * (row + P * chunk)) * P ** -0.5
            c[:, K_GI + 3 * h + chunk] = np.exp(log_g[h] * (row + P * chunk))
        c[:, K_GI + 3 * h + 2] = 1.0
        c[:, K_GAM + h] = np.exp(log_g[h])
        c[:, K_END + h] = np.exp(log_g[h] * (SEQ - 1))
    c[:, K_MASK:K_MASK + DEC] = (row[:, None] % DEC) == np.arange(DEC)[None, :]
    return c


def tile_done_at(l, t):
    return t + (TILES * l + 1)


def bank_free_at(l, pair):
    return pair + (TILES // 2 * l + 1)


def read_out_at(l, pair):
    return pair + (TILES // 2 * l + 2)


class Signals:

    def __init__(self, nc):
        self.vecs_in = nc.alloc_semaphore("vecs_in")
        self.consts_in = nc.alloc_semaphore("consts_in")
        self.x_in = [nc.alloc_semaphore(f"x_in_{g}") for g in range(4)]
        self.p_in = nc.alloc_semaphore("p_in")
        self.convstate_in = nc.alloc_semaphore("convstate_in")
        self.state_in = nc.alloc_semaphore("state_in")
        self.state_out = nc.alloc_semaphore("state_out")
        self.sprompt_out = nc.alloc_semaphore("sprompt_out")
        self.scp_out = nc.alloc_semaphore("scp_out")
        self.scs_out = nc.alloc_semaphore("scs_out")
        self.y_out = nc.alloc_semaphore("y_out")
        self.hi_ready = nc.alloc_semaphore("hi_ready")
        self.lo_ready = nc.alloc_semaphore("lo_ready")
        self.tile_done = nc.alloc_semaphore("tile_done")
        self.xhi_ready = nc.alloc_semaphore("xhi_ready")
        self.xin_ready = nc.alloc_semaphore("xin_ready")
        self.chi_ready = nc.alloc_semaphore("chi_ready")
        self.c_ready = nc.alloc_semaphore("c_ready")
        self.phi_ready = nc.alloc_semaphore("phi_ready")
        self.pin_ready = nc.alloc_semaphore("pin_ready")
        self.rhi_ready = nc.alloc_semaphore("rhi_ready")
        self.ret_ready = nc.alloc_semaphore("ret_ready")
        self.cohi_ready = nc.alloc_semaphore("cohi_ready")
        self.cout_ready = nc.alloc_semaphore("cout_ready")
        self.hhi_ready = nc.alloc_semaphore("hhi_ready")
        self.h_ready = nc.alloc_semaphore("h_ready")
        self.sq_ready = nc.alloc_semaphore("sq_ready")
        self.sq_used = nc.alloc_semaphore("sq_used")
        self.sum_done = nc.alloc_semaphore("sum_done")
        self.stat_scaled = nc.alloc_semaphore("stat_scaled")
        self.stat_rs = nc.alloc_semaphore("stat_rs")
        self.diag_ready = nc.alloc_semaphore("diag_ready")
        self.bcast_done = nc.alloc_semaphore("bcast_done")
        self.bcast_read = nc.alloc_semaphore("bcast_read")
        self.small_set = nc.alloc_semaphore("small_set")
        self.consts_set = nc.alloc_semaphore("consts_set")
        self.pad_set = nc.alloc_semaphore("pad_set")
        self.rfac_step = nc.alloc_semaphore("rfac_step")
        self.tanh_ready = nc.alloc_semaphore("tanh_ready")
        self.u_ready = nc.alloc_semaphore("u_ready")
        self.ust_ready = nc.alloc_semaphore("ust_ready")
        self.tap_done = nc.alloc_semaphore("tap_done")
        self.sconv_step = nc.alloc_semaphore("sconv_step")
        self.gc_ready = nc.alloc_semaphore("gc_ready")
        self.ln_summed = nc.alloc_semaphore("ln_summed")
        self.mean_done = nc.alloc_semaphore("mean_done")
        self.ln_centered = nc.alloc_semaphore("ln_centered")
        self.ln_squared = nc.alloc_semaphore("ln_squared")
        self.ln_scaled = nc.alloc_semaphore("ln_scaled")
        self.silu_ready = nc.alloc_semaphore("silu_ready")
        self.rope_step = nc.alloc_semaphore("rope_step")
        self.rope_done = nc.alloc_semaphore("rope_done")
        self.kv_ready = nc.alloc_semaphore("kv_ready")
        self.khi_ready = nc.alloc_semaphore("khi_ready")
        self.stack_in = nc.alloc_semaphore("stack_in")
        self.s1_done = nc.alloc_semaphore("s1_done")
        self.rows_ready = nc.alloc_semaphore("rows_ready")
        self.p_ready = nc.alloc_semaphore("p_ready")
        self.vbd_ready = nc.alloc_semaphore("vbd_ready")
        self.s2_done = nc.alloc_semaphore("s2_done")
        self.snew_ready = nc.alloc_semaphore("snew_ready")
        self.sprompt_ready = nc.alloc_semaphore("sprompt_ready")
        self.bn_done = nc.alloc_semaphore("bn_done")
        self.stat_ready = nc.alloc_semaphore("stat_ready")
        self.pool_step = nc.alloc_semaphore("pool_step")
        self.ret_rs = nc.alloc_semaphore("ret_rs")
        self.s3a_done = nc.alloc_semaphore("s3a_done")
        self.os_ready = nc.alloc_semaphore("os_ready")
        self.s3b_done = nc.alloc_semaphore("s3b_done")
        self.og_ready = nc.alloc_semaphore("og_ready")
        self.s4_done = nc.alloc_semaphore("s4_done")
        self.rt_ready = nc.alloc_semaphore("rt_ready")
        self.sg_ready = nc.alloc_semaphore("sg_ready")
        self.h_step = nc.alloc_semaphore("h_step")
        self.e_step = nc.alloc_semaphore("e_step")
        self.gate_step = nc.alloc_semaphore("gate_step")
        self.xnew = nc.alloc_semaphore("xnew")


def build(nc, ctx, x_t, p_t, s_ret, s_conv, vecs_d, consts_d, w_in, w_pw, w_out, w_ple, w_gate,
          y_t, sp_out, scp_out, ss_out, scs_out):
    sb_at = {}
    cursor = [(nc.sbuf_base + 31) // 32 * 32]

    def sb(name, shape, dt=F32, at=None):
        size = int(np.prod(shape[1:])) * 4
        where = cursor[0] if at is None else at
        if at is None:
            cursor[0] = (cursor[0] + size + 31) // 32 * 32
        assert where + size <= nc.sbuf_usable_end, (name, where, size)
        sb_at[name] = (where, where + size)
        return nc.alloc_sbuf_tensor_at(name, shape, dt, offset=where)

    raw = sb("raw", [P, RAW, SLAB])
    whi = sb("whi", [P, RING, SLAB], F32R)
    wlo = sb("wlo", [P, RING, SLAB], F32R)
    a_hi = sb("a_hi", [P, KT, R], F32R)
    a_lo = sb("a_lo", [P, KT, R], F32R)
    b_hi = sb("b_hi", [P, KT, R], F32R)
    b_lo = sb("b_lo", [P, KT, R], F32R)
    c_buf = sb("c_buf", [P, CT, R], at=sb_at["b_hi"][0] + CT * R * 4)
    gc_buf = sb("gc_buf", [P, CT, R], at=sb_at["b_lo"][0] + CT * R * 4)
    c_lo = sb("c_lo", [P, CT, R], F32R, at=sb_at["c_buf"][0])
    x = sb("x", [P, KT, R])
    vecs = sb("vecs", [P, DEPTH, VW])
    cst = sb("cst", [P, KW])
    ones = sb("ones", [P, P])
    ones_mean = sb("ones_mean", [P, P])
    r_x = sb("r_x", [P, R])
    r_t = sb("r_t", [P, R])
    diag = sb("diag", [P, R])
    acc = [sb(f"acc{i}", [P, R]) for i in range(2)]
    sq = sb("sq", [P, 2, R])
    tmp = [sb(f"tmp{i}", [P, R]) for i in range(4)]
    small = sb("small", [P, 192])
    work = cursor[0]
    m_buf = sb("m_buf", [P, KT, R], at=work)
    e_buf = sb("e_buf", [P, KT, R], at=sb_at["m_buf"][1])
    u_buf = sb("u_buf", [P, CT, UW], at=work)
    ln_sq = sb("ln_sq", [P, CT, R], at=work)
    c_hi = sb("c_hi", [P, CT, R], F32R, at=work)
    ust = sb("ust", [P, CT, TAPS, DEC], at=sb_at["u_buf"][1])
    s_new = sb("s_new", [P, DEC * P], at=sb_at["u_buf"][1])
    heads_at = sb_at["ust"][1]
    sprod = sb("sprod", [P, CT // 2, DEC, TAPS], at=heads_at)
    cursor[0] = heads_at
    vbd = sb("vbd", [32, DEC, P], F32R)
    zs = sb("zs", [P, 2, R])
    zw = sb("zw", [P, 2, R])
    qk = sb("qk", [P, 2, R])
    vt = sb("vt", [P, R])
    vrow = sb("vrow", [P, 2 * P])
    krow = sb("krow", [P, 2 * P])
    pmat = sb("pmat", [P, 3 * P])
    stack_cols = sb("stack_cols", [P, 2, 4, DEC], F32R)
    stack = sb("stack", [32, P], F32R)
    og = sb("og", [P, 3, P])
    s_prompt = sb("s_prompt", [P, P])
    gz = sb("gz", [P, R])
    sg = sb("sg", [P, R])
    rt = sb("rt", [P, R])
    qks = sb("qks", [P, 2, DEC])
    vs = sb("vs", [P, DEC])
    os_t = sb("os_t", [P, DEC])
    heads_end = cursor[0]
    cursor[0] = max(heads_end, sb_at["e_buf"][1])
    p_in = sb("p_in", [P, PT, R])
    assert sb_at["sprod"][1] <= sb_at["vbd"][1]

    def sm(name, at, n):
        return small[:, at:at + n]

    st, rs = sm("st", 0, 3), sm("rs", 4, 3)
    rx3, r2 = sm("rx3", 8, 3), sm("r2", 12, 2)
    kk = small[:, 16:32].rearrange("p (h c) -> p h c", c=2)
    gi = small[:, 32:56].rearrange("p (h c) -> p h c", c=3)
    g2 = small[:, 56:80].rearrange("p (h c) -> p h c", c=3)
    rs8 = small[:, 80:96].rearrange("p (a b) -> p a b", a=2)
    bn = sm("bn", 96, 18)
    mv = small[:, 116:122].rearrange("p (c s) -> p c s", s=2)
    var_t, rs_t, sc_t, nb_t = (small[:, 124 + 4 * i:127 + 4 * i] for i in range(4))
    minus_half = sm("minus_half", 140, 3)
    mean_sc = sm("mean_sc", 144, 3)
    eps3, zero3 = sm("eps3", 148, 3), sm("zero3", 152, 3)
    held = sm("held", 156, 1)

    ps = [nc.alloc_psum_tensor(f"ps{i}", [P, 512], F32) for i in range(8)]
    accum = ps[0:2]
    ps_tr, ps_st, ps_p, ps_o, ps_s0, ps_s1 = ps[2:8]

    gate_bank = [*accum, ps_o, ps_tr]

    ident = cst[:, K_ID:K_ID + P]
    tri = cst[:, K_TRI:K_TRI + P]

    s = Signals(nc)
    raw_in = [nc.alloc_semaphore("raw_even_in"), nc.alloc_semaphore("raw_odd_in")]
    acc_free = [nc.alloc_semaphore("acc_even_free"), nc.alloc_semaphore("acc_odd_free")]

    ST_X, ST_LN, ST_M, ST_E = range(4)

    def stat_at(l, k):
        return 4 * l + k + 1

    def spread_at(l, k):
        return 3 * l + {ST_X: 1, ST_M: 2, ST_E: 3}[k]

    def squares_at(l):
        return 4 + 3 * KT * l

    def vec(l, at, n=1):
        return vecs[:, l, bass.ds(at, n)]

    def wide(ap, shape):
        return ap.unsqueeze(1).to_broadcast(shape)

    def rows(t, tile, n=1):
        return t[:, :, :].rearrange("p k r -> p (k r)")[:, bass.ds(tile * R, n * R)]

    block = ctx.enter_context(nc.Block())

    @block.sync
    def _(sp):
        def load(l, slab, src, first_row, cols=SLAB):
            here = slab_static[0] % RAW
            if l or slab_static[0] >= RAW:
                sp.wait_ge(s.lo_ready, slab + (SLABS * l - 1))
            sp.dma_start(raw[:, here, 0:cols], src[bass.ds(first_row, P), :]).then_inc(raw_in[here], 16)
            slab_static[0] += 1

        slab_static = [0]
        for l in range(DEPTH):
            slab_static[0] = 0
            for j in range(4):
                load(l, S_C + j, w_in, P * (56 * l + (40, 32)[j % 2] + j // 2))
            with sp.Fori(1, 4) as i:
                for j in range(4):
                    load(l, 4 * i + (S_C + j), w_in, P * (2 * i + (56 * l + (40, 32)[j % 2] + j // 2)))
            with sp.Fori(0, HEADS) as h:
                for j in range(4):
                    load(l, 4 * h + (S_H + j), w_in, P * (h + (56 * l + HEADS * j)))
            with sp.Fori(0, 2) as i:
                for j in range(4):
                    load(l, 4 * i + (S_G + j), w_in, P * (4 * i + (56 * l + 48 + j)))
            for j in range(4):
                load(l, S_W + j, w_pw, P * (4 * l + j))
            with sp.Fori(0, 4) as i:
                for j in range(4):
                    load(l, 4 * i + (S_O + j), w_out, P * (4 * i + (16 * l + j)))
            for j in range(4):
                load(l, S_P + j, w_ple, P * (4 * l + j), 4 * PT * P)
            with sp.Fori(0, 4) as i:
                for j in range(4):
                    load(l, 4 * i + (S_T + j), w_gate, P * (4 * i + (16 * l + j)))
        for i in range(4):
            sp.wait_ge(s.xnew, KT * (DEPTH - 1) + 4 * i + 4)
            sp.dma_start(y_t[:, 4 * i:4 * i + 4, :], x[:, 4 * i:4 * i + 4, :]).then_inc(s.y_out, 16)
        sp.wait_ge(s.state_out, 16 * HEADS * DEPTH)
        sp.wait_ge(s.sprompt_out, 16 * HEADS * DEPTH + 1)
        sp.wait_ge(s.scp_out, 16 * DEPTH)
        sp.wait_ge(s.scs_out, 16 * DEPTH)
        sp.wait_ge(s.y_out, 16 * 4)

    @block.tensor
    def _(pe):
        def gemm(l, pair, bank, slab, slot, at, k_tiles, operands, k_wait=None, among={}, fresh=True):
            pe.wait_ge(acc_free[bank], bank_free_at(l, pair))
            if fresh:
                pe.wait_ge(s.lo_ready, slab + (SLABS * l + 1))
            for k in range(k_tiles):
                if k_wait:
                    k_wait(k)
                if k in among:
                    among[k]()
                w = at + P * k
                hi, lo = operands(k)
                pe.matmul(accum[bank][:, 0:R], whi[:, slot, w:w + P], hi, start=k == 0, stop=False)
                pe.matmul(accum[bank][:, 0:R], whi[:, slot, w:w + P], lo, start=False, stop=False)
                mm = pe.matmul(accum[bank][:, 0:R], wlo[:, slot, w:w + P], hi, start=False, stop=k == k_tiles - 1)
            mm.then_inc(s.tile_done, 1)

        in_a = lambda k: (a_hi[:, k, :], a_lo[:, k, :])
        in_b = lambda k: (b_hi[:, k, :], b_lo[:, k, :])
        in_c = lambda k: (c_hi[:, k, :], c_lo[:, k, :])
        mixed = lambda k: in_b(k) if k < HEADS else in_a(k - HEADS)
        in_p = lambda k: in_a(CT + k)

        def stat_sum(l, k, *bufs):
            for c, (r0, r1) in enumerate(((0, P), (P, 2 * P), (2 * P, R))):
                for buf in bufs:
                    mm = pe.matmul(ps_p[0:r1 - r0, c:c + 1], buf[:, r0:r1], ones[:, 0:1], start=buf is bufs[0], stop=buf is bufs[-1])
            mm.then_inc(s.sum_done, 1)

        def stat_bcast(l, k):
            pe.wait_ge(s.diag_ready, stat_at(l, k))
            pe.matmul(ps_p[:, 0:P], ones[:, :], diag[:, 0:P], start=True, stop=True)
            pe.matmul(ps_p[:, P:2 * P], ones[:, :], diag[:, P:2 * P], start=True, stop=True)
            pe.matmul(ps_p[:, 2 * P:R], ones[0:DEC, :], diag[0:DEC, 2 * P:R], start=True, stop=True).then_inc(s.bcast_done, 1)

        def ret_scores(l, h):
            n = h + HEADS * l
            pe.wait_ge(s.stack_in, n + 1)
            pe.transpose(ps_tr[:, 0:P], vt[:, 0:P], ident)
            pe.transpose(ps_tr[:, P:2 * P], vt[:, P:2 * P], ident)
            pe.transpose(ps_tr[:, 2 * P:3 * P], qk[:, 1, 0:P], ident)
            pe.transpose(ps_tr[:, 3 * P:4 * P], qk[:, 1, P:2 * P], ident)
            cols = stack_cols[:, :, :, :].rearrange("p a b c -> p (a b c)").bitcast(F32)
            pe.transpose(ps_st[0:32, 0:P], cols[:, 0:32], ident)
            pe.transpose(ps_st[0:32, P:2 * P], cols[:, 32:64], ident)
            pe.matmul(ps_p[:, 0:2 * P], qk[:, 1, 0:P], qk[:, 0, 0:2 * P], start=True, stop=True)
            pe.matmul(ps_p[:, 2 * P:3 * P], qk[:, 1, P:2 * P], qk[:, 0, P:2 * P], start=True, stop=True).then_inc(s.s1_done, 1)

        def ret_values(l, h):
            n = h + HEADS * l
            pe.wait_ge(s.rows_ready, n + 1)
            pe.wait_ge(s.p_ready, n + 1)
            pe.matmul(ps_o[:, 0:P], pmat[:, 0:P], vrow[:, 0:P], start=True, stop=True)
            pe.matmul(ps_o[:, P:2 * P], pmat[:, P:2 * P], vrow[:, 0:P], start=True, stop=False)
            pe.matmul(ps_o[:, P:2 * P], pmat[:, 2 * P:3 * P], vrow[:, P:2 * P], start=False, stop=True)
            pe.matmul(ps_tr[:, 0:P], krow[:, 0:P], vrow[:, 0:P], start=True, stop=False)
            pe.matmul(ps_tr[:, 0:P], krow[:, P:2 * P], vrow[:, P:2 * P], start=False, stop=True)
            pe.wait_ge(s.vbd_ready, n + 1)
            pe.wait_ge(s.rt_ready, n + 1)
            blocks = vbd[:, :, :].rearrange("p b v -> p (b v)")
            pe.matmul(ps_s0[:, :], stack[:, 0:P], blocks[:, 0:4 * P], start=True, stop=True)
            pe.matmul(ps_s1[:, :], stack[:, 0:P], blocks[:, 4 * P:8 * P], start=True, stop=True).then_inc(s.s2_done, 1)

        def ret_samples(l, h):
            pe.wait_ge(s.snew_ready, h + (HEADS * l + 1))
            for b in range(DEC):
                mm = pe.matmul(ps_st[:, 2 * P + b:2 * P + b + 1], s_new[:, b * P:(b + 1) * P], qks[:, 0, b:b + 1], start=True, stop=True)
            mm.then_inc(s.s3a_done, 1)

        def ret_sample_rows(l, h):
            pe.wait_ge(s.os_ready, h + (HEADS * l + 1))
            pe.transpose(ps_st[0:DEC, 3 * P:4 * P], os_t[:, :], ident).then_inc(s.s3b_done, 1)

        def ret_turn(l, h):
            pe.wait_ge(s.og_ready, h + (HEADS * l + 1))
            pe.transpose(ps_s0[:, 0:P], og[:, 0, :], ident)
            pe.transpose(ps_s0[:, P:2 * P], og[:, 1, :], ident)
            pe.transpose(ps_s0[:, 2 * P:R], og[0:DEC, 2, :], cst[0:DEC, K_ID:K_ID + DEC]).then_inc(s.s4_done, 1)

        def head(l, h, prev, turn):
            for j in range(4):
                among = {}
                if turn and j == 0:
                    among = {13: lambda: ret_turn(l, h - 2)}
                if prev and j == 3:
                    among = {6: lambda: ret_sample_rows(l, h - 1)}
                gemm(l, 2 * h + (T_H // 2 + j // 2), j % 2, 4 * h + (S_H + j), j, 0, KT, in_a, among=among)
                if prev and j < 3:
                    (ret_scores, ret_values, ret_samples)[j](l, h - 1)

        def sum_x():
            pe.wait_ge(s.sq_used, squares_at(l))
            if l:
                stat_sum(l, ST_X, acc[3 * l % 2])
            else:
                stat_sum(l, ST_X, *(e_buf[:, k, :] for k in range(4)))

        for l in range(DEPTH):
            if l == 0:
                pe.wait_ge(s.consts_in, 16)
                pe.wait_ge(s.consts_set, 1)
            for j in range(4):
                gemm(l, j // 2, j % 2, S_C + j, j, 0, KT, in_a,
                     k_wait=(lambda k: pe.wait_ge(s.xin_ready, KT * l + k + 1)) if j == 0 else None,
                     among={8: lambda: stat_bcast(l, ST_X)} if j == 1 else {})
                if j == 0:
                    sum_x()
            with pe.Fori(1, 4) as i:
                for j in range(4):
                    gemm(l, 2 * i + j // 2, j % 2, 4 * i + (S_C + j), j, 0, KT, in_a)
            head(l, 0, False, False)
            head(l, 1, True, False)
            with pe.Fori(2, HEADS) as h:
                head(l, h, True, True)
            def mean_over_channels():
                pe.wait_ge(s.ln_summed, 2 * l + 1)
                pe.wait_ge(s.p_ready, HEADS * (l + 1))
                pe.matmul(ps_p[:, 0:R], ones_mean[:, :], acc[(3 * l + 1) % 2][:, :], start=True, stop=True).then_inc(s.mean_done, 1)

            def variance_sum():
                pe.wait_ge(s.ln_centered, l + 1)
                pe.wait_ge(s.ln_summed, 2 * l + 2)
                stat_sum(l, ST_LN, acc[3 * l % 2])

            def variance_bcast():
                pe.wait_ge(s.stat_scaled, stat_at(l, ST_LN))
                stat_bcast(l, ST_LN)

            among = {0: {13: lambda: ret_turn(l, 6)}, 1: {12: mean_over_channels}, 3: {6: lambda: ret_sample_rows(l, 7)},
                     4: {4: variance_sum, 13: lambda: ret_turn(l, 7)}, 5: {6: variance_bcast}}
            for t in range(CT):
                gemm(l, (T_G + t) // 2, t % 2, S_G + t, t % 4, 0, KT, in_a, among=among.get(t, {}))
                if t < 3:
                    (ret_scores, ret_values, ret_samples)[t](l, 7)
            for j in range(4):
                for e in range(2):
                    gemm(l, (T_W + 2 * j) // 2, e % 2, S_W + j, j, e * CT * P, CT, in_c, fresh=e == 0,
                         k_wait=(lambda k: pe.wait_ge(s.c_ready, 3 * l + (1, 1, 2, 2, 3, 3, 3, 3)[k])) if j == 0 and e == 0 else None)
            pe.wait_ge(s.ln_scaled, 2 * l + 2)
            with pe.Fori(0, 4) as i:
                for j in range(4):
                    gemm(l, 2 * i + (T_O // 2 + j // 2), j % 2, 4 * i + (S_O + j), j, 0, KT, mixed,
                         k_wait=(lambda k: pe.wait_ge(s.ret_ready, HEADS * l + k + 1) if k < HEADS
                                 else pe.wait_ge(s.cout_ready, CT * l + k - HEADS + 1)) if j == 0 else None)
            for t in range(KT):
                gemm(l, (T_P + t) // 2, t % 2, S_P + t // 4, t // 4, t % 4 * PT * P, PT, in_p, fresh=t % 4 == 0,
                     k_wait=(lambda k: pe.wait_ge(s.pin_ready, l + 1)) if t == 0 else None)
                if t == 1:
                    pe.wait_ge(s.sq_used, squares_at(l) + KT)
                    stat_sum(l, ST_M, acc[(3 * l + 1) % 2])
                if t == 4:
                    stat_bcast(l, ST_M)
            for g in range(4):
                pe.wait_ge(s.h_ready, 4 * l + g + 1)
                for t in range(4):
                    if g == 0:
                        pe.wait_ge(acc_free[t % 2], bank_free_at(l, T_T // 2))
                        pe.wait_ge(s.lo_ready, SLABS * l + S_T + t + 1)
                    for k in range(4 * g, 4 * g + 4):
                        w, out = slice(P * k, P * k + P), gate_bank[t][:, 0:R]
                        hi, lo = in_b(k)
                        pe.matmul(out, whi[:, t, w], hi, start=k == 0, stop=False)
                        pe.matmul(out, whi[:, t, w], lo, start=False, stop=False)
                        mm = pe.matmul(out, wlo[:, t, w], hi, start=False, stop=k == KT - 1)
                    if g == 3:
                        mm.then_inc(s.tile_done, 1)
                if g == 0:
                    pe.wait_ge(s.sq_used, squares_at(l) + 2 * KT)
                    pe.wait_ge(s.bcast_read, spread_at(l, ST_M))
                    stat_sum(l, ST_E, acc[3 * l % 2])
                if g == 2:
                    stat_bcast(l, ST_E)
            with pe.Fori(1, 4) as i:
                for j in range(4):
                    gemm(l, 2 * i + (T_T // 2 + j // 2), j % 2, 4 * i + (S_T + j), j, 0, KT, in_b)
            pe.wait_ge(s.bcast_read, spread_at(l, ST_E))

    @block.scalar
    def _(act):
        def next_hi(l, body, slot, tile, cols=SLAB):
            act.wait_ge(raw_in[slot % RAW], body * 32 + 16 * (SLABS // 2 * l + 3 + slot // 2))
            act.wait_ge(s.tile_done, tile_done_at(l, tile))
            nc.scalar.activation(whi[:, slot, 0:cols], raw[:, slot % RAW, 0:cols], ACT.Copy).then_inc(s.hi_ready, 1)

        def square(n, side, src):
            act.wait_ge(s.sq_used, n - 1)
            nc.scalar.activation(sq[:, side, :], src, ACT.Square).then_inc(s.sq_ready, 1)

        def conv_in(l, i):
            for j in range(4):
                ct = 2 * i + j // 2
                if j % 2 == 0:
                    act.wait_ge(acc_free[0], read_out_at(l, ct))
                    nc.scalar.activation(tmp[2][:, :], tmp[0][:, :], ACT.Tanh, scale=0.5).then_inc(s.tanh_ready, 1)
                    next_hi(l, i, j, 4 * i + j)
                else:
                    next_hi(l, i, j, 4 * i + j)
                    act.wait_ge(s.u_ready, ct + (CT * l + 1))
                    ust_flat = ust[:, :, :, :].rearrange("p c k b -> p (c k b)")
                    nc.scalar.activation(ust_flat[:, bass.ds(ct * (TAPS * DEC) + PAD * DEC, DEC)],
                                         u_flat[:, bass.ds(ct * UW + PAD + SEQ, DEC)], ACT.Copy).then_inc(s.ust_ready, 1)

        def ret_rows(l, h):
            kcol = lambda chunk: small[:, bass.ds((h - 1) * 2 + (16 + chunk), 1)]
            act.wait_ge(s.s1_done, h + HEADS * l)
            nc.scalar.activation(vrow[:, :], ps_tr[:, 0:2 * P], ACT.Copy)
            nc.scalar.activation(krow[:, 0:P], ps_tr[:, 2 * P:3 * P], ACT.Copy, scale=kcol(0))
            nc.scalar.activation(krow[:, P:2 * P], ps_tr[:, 3 * P:4 * P], ACT.Copy, scale=kcol(1))
            nc.scalar.activation(stack[:, :], ps_st[0:32, 0:P], ACT.Copy).then_inc(s.rows_ready, 1)
            for b in range(DEC):
                block_of_b = nc.scalar.activation(vbd[:, b, :], ps_st[0:32, P:2 * P], ACT.Copy, scale=cst[0:32, K_MASK + b:K_MASK + b + 1])
            block_of_b.then_inc(s.vbd_ready, 1)

        def ret_prompt_state(l, h):
            n = h + HEADS * l
            act.wait_ge(s.s2_done, n)
            act.wait_ge(s.sprompt_out, 16 * n - 15)
            nc.scalar.activation(s_prompt[:, :], ps_tr[:, 0:P], ACT.Copy, scale=cst[:, bass.ds((h - 1) + K_END, 1)]).then_inc(s.sprompt_ready, 1)
            act.wait_ge(s.sprompt_ready, n)
            act.dma_start(sp_out[bass.ds(n * P - P, P), :], s_prompt[:, :]).then_inc(s.sprompt_out, 16)

        def gate_silu(l, h):
            n = h + HEADS * l
            act.wait_ge(acc_free[1], read_out_at(l, 2 * h + (T_H // 2 - 1)))
            act.wait_ge(s.rt_ready, n)
            nc.scalar.activation(sg[:, :], gz[:, :], ACT.Silu).then_inc(s.sg_ready, 1)

        def head(l, h, prev, turn):
            n = h + HEADS * l
            if turn:
                ret_normalise(l, h - 1)
            act.wait_ge(s.tile_done, tile_done_at(l, 4 * h + T_H))
            if prev or l:
                act.wait_ge(s.rope_done, n)
            nc.scalar.activation(zs[:, 0, :], accum[0][:, 0:R], ACT.Copy)
            nc.scalar.activation(zw[0:64, 0, :], accum[0][64:P, 0:R], ACT.Copy)
            nc.scalar.activation(zw[64:P, 0, :], accum[0][0:64, 0:R], ACT.Copy).then_inc(acc_free[0], 1)
            if prev:
                ret_rows(l, h)
            next_hi(l, 4 + h, 0, 4 * h + T_H)
            act.wait_ge(s.tile_done, tile_done_at(l, 4 * h + (T_H + 1)))
            nc.scalar.activation(zs[:, 1, :], accum[1][:, 0:R], ACT.Copy)
            nc.scalar.activation(zw[0:64, 1, :], accum[1][64:P, 0:R], ACT.Copy)
            nc.scalar.activation(zw[64:P, 1, :], accum[1][0:64, 0:R], ACT.Copy).then_inc(acc_free[1], 1)
            if prev:
                ret_prompt_state(l, h)
            if turn:
                ret_round(l, h - 1)
            if prev:
                gate_silu(l, h)
            next_hi(l, 4 + h, 1, 4 * h + (T_H + 1))
            act.wait_ge(s.tile_done, tile_done_at(l, 4 * h + (T_H + 2)))
            nc.scalar.activation(vt[:, :], accum[0][:, 0:R], ACT.Copy).then_inc(acc_free[0], 1)
            if prev:
                ret_samples_out(l, h)
            act.wait_ge(s.kv_ready, n + 1)
            nc.scalar.activation(stack_cols[:, 0, 0:2, :], wide(qks[:, 1, :], [P, 2, DEC]), ACT.Copy)
            nc.scalar.activation(stack_cols[:, 1, 0:4:2, :], wide(vs[:, :], [P, 2, DEC]), ACT.Copy).then_inc(s.khi_ready, 1)
            next_hi(l, 4 + h, 2, 4 * h + (T_H + 2))
            next_hi(l, 4 + h, 3, 4 * h + (T_H + 3))
            if prev:
                state_in(l, h)

        def state_in(l, h):
            n = h + HEADS * l
            act.wait_ge(s.s3a_done, n)
            act.wait_ge(s.state_out, 16 * n)
            act.dma_start(s_new[:, :], s_ret[bass.ds(n * P, P), :]).then_inc(s.state_in, 16)

        def ret_samples_out(l, h):
            n = h + HEADS * l
            act.wait_ge(s.s3a_done, n)
            nc.scalar.activation(os_t[:, :], ps_st[:, 2 * P:2 * P + DEC], ACT.Copy).then_inc(s.os_ready, 1)
            act.dma_start(ss_out[bass.ds(n * P - P, P), :], s_new[:, :]).then_inc(s.state_out, 16)

        def ret_normalise(l, h):
            act.wait_ge(s.ret_rs, h + HEADS * l)
            for chunk in range(2):
                nc.scalar.activation(og[:, chunk, :], ps_o[:, chunk * P:(chunk + 1) * P], ACT.Identity,
                                     bias=nb_t[:, chunk:chunk + 1], scale=sc_t[:, chunk:chunk + 1])
            nc.scalar.activation(og[0:DEC, 2, :], ps_st[0:DEC, 3 * P:4 * P], ACT.Identity,
                                 bias=nb_t[0:DEC, 2:3], scale=sc_t[0:DEC, 2:3]).then_inc(s.og_ready, 1)

        def ret_round(l, h):
            act.wait_ge(s.rt_ready, h + (HEADS * l + 1))
            nc.scalar.activation(rows(b_hi, h - 1), rt[:, :], ACT.Copy).then_inc(s.rhi_ready, 1)

        def channel_silu(l, c):
            act.wait_ge(s.ln_scaled, 2 * l + 1 + c // 4)
            nc.scalar.activation(c_buf[:, c, :], c_buf[:, c, :], ACT.Silu, bias=vec(l, V_BCN + c), scale=vec(l, V_GCN + c)).then_inc(s.silu_ready, 1)

        u_flat = u_buf[:, :, :].rearrange("p c r -> p (c r)")
        act.dma_start(vecs[:, :, :], vecs_d).then_inc(s.vecs_in, 16)
        for g in range(4):
            act.dma_start(x[:, 4 * g:4 * g + 4, :], x_t[:, 4 * g:4 * g + 4, :]).then_inc(s.x_in[g], 16)
        act.dma_start(cst[:, :], consts_d).then_inc(s.consts_in, 16)

        def first_hi(j):
            act.wait_ge(raw_in[j % RAW], 16 * (j // RAW + 1))
            nc.scalar.activation(whi[:, j, :], raw[:, j % RAW, :], ACT.Copy).then_inc(s.hi_ready, 1)

        first_hi(0)
        act.wait_ge(s.vecs_in, 16)
        for g in range(4):
            act.wait_ge(s.x_in[g], 16)
            for k in range(4 * g, 4 * g + 4):
                nc.scalar.activation(a_hi[:, k, :], x[:, k, :], ACT.Copy, scale=vec(0, V_PRE + k)).then_inc(s.xhi_ready, 1)
            nc.scalar.activation(e_buf[:, 4 * g:4 * g + 4, :], x[:, 4 * g:4 * g + 4, :], ACT.Square).then_inc(s.sq_ready, 1)
            if g == 1:
                first_hi(1)
        first_hi(2)
        first_hi(3)

        for l in range(DEPTH):
            if l:
                act.wait_ge(s.xnew, KT * l)
            else:
                act.wait_ge(s.sum_done, 1)
            act.dma_start(ust[:, :, 0:PAD, :], s_conv[P * l:P * l + P, :].rearrange("p (c k b) -> p c k b", c=CT, k=PAD)).then_inc(s.convstate_in, 16)
            with act.Fori(0, 4) as i:
                conv_in(l, i)
            act.wait_ge(s.ust_ready, CT * (l + 1))
            act.wait_ge(s.convstate_in, 16 * (l + 1))
            act.dma_start(scp_out[l, :, :, :], u_buf[:, :, SEQ:SEQ + PAD]).then_inc(s.scp_out, 16)
            act.dma_start(scs_out[P * l:P * l + P, :].rearrange("p (c k b) -> p c k b", c=CT, k=PAD), ust[:, :, 1:TAPS, :]).then_inc(s.scs_out, 16)
            if l:
                act.wait_ge(s.pin_ready, l)
            act.dma_start(p_in[:, :, :], p_t[l, :, :, :]).then_inc(s.p_in, 16)
            head(l, 0, False, False)
            act.wait_ge(s.scs_out, 16 * (l + 1))
            act.wait_ge(s.sconv_step, 5 * (l + 1))
            act.dma_start(s_new[:, :], s_ret[HEADS * l * P:(HEADS * l + 1) * P, :]).then_inc(s.state_in, 16)
            head(l, 1, True, False)
            with act.Fori(2, HEADS) as h:
                head(l, h, True, True)
            for t in range(CT):
                if t == 0:
                    ret_normalise(l, 7)
                if t == 4:
                    ret_normalise(l, 8)
                act.wait_ge(acc_free[t % 2], read_out_at(l, (T_G + t) // 2))
                nc.scalar.activation(gc_buf[:, t, :], tmp[t % 2][:, :], ACT.Silu).then_inc(s.gc_ready, 1)
                if t == 0:
                    ret_rows(l, 8)
                    ret_round(l, 7)
                if t == 1:
                    ret_prompt_state(l, 8)
                    gate_silu(l, 8)
                if t == 2:
                    ret_samples_out(l, 8)
                if t == 2:
                    act.wait_ge(s.ln_centered, l + 1)
                    act.wait_ge(s.scp_out, 16 * (l + 1))
                    nc.scalar.activation(ln_sq[:, :, :], c_buf[:, :, :], ACT.Square).then_inc(s.ln_squared, 1)
                if t == 5:
                    ret_round(l, 8)
                next_hi(l, 12 + t // 4, t % 4, T_G + t)
                if t in (5, 6):
                    for c in range(4 * (t - 5), 4 * (t - 5) + 4):
                        channel_silu(l, c)
            for part, (c0, c1) in enumerate(((0, 2), (2, 4), (4, 8))):
                act.wait_ge(s.silu_ready, CT * l + c1)
                nc.scalar.activation(c_hi[:, c0:c1, :], c_buf[:, c0:c1, :], ACT.Copy).then_inc(s.chi_ready, 1)
            act.wait_ge(s.tile_done, tile_done_at(l, T_W - 1))
            act.wait_ge(s.p_in, 16 * (l + 1))
            nc.scalar.activation(a_hi[:, CT:CT + PT, :], p_in[:, :, :], ACT.Copy).then_inc(s.phi_ready, 1)
            for j in range(4):
                for e in range(2):
                    act.wait_ge(acc_free[e], read_out_at(l, T_W // 2 + j))
                    nc.scalar.activation(a_hi[:, 2 * j + e, :], gc_buf[:, 2 * j + e, :], ACT.Copy).then_inc(s.cohi_ready, 1)
                next_hi(l, 14, j, T_W + 2 * j + 1)
            act.wait_ge(s.state_out, 16 * HEADS * (l + 1))
            act.wait_ge(s.sprompt_out, 16 * HEADS * (l + 1) + 1)

            def out_body(i, cols):
                for j in range(4):
                    act.wait_ge(s.tile_done, tile_done_at(l, 4 * i + (T_O + j)))
                    square(4 * i + (squares_at(l) + j), j % 2, accum[j % 2][:, 0:R])
                    nc.scalar.activation(rows(m_buf, 4 * i + j), accum[j % 2][:, 0:R], ACT.Copy, scale=vec(l, 4 * i + (V_POST + j))).then_inc(acc_free[j % 2], 1)
                    next_hi(l, 15 + i, j, 4 * i + (T_O + j), cols)

            with act.Fori(0, 3) as i:
                out_body(i, SLAB)
            out_body(3, 4 * PT * P)
            for t in range(KT):
                act.wait_ge(s.tile_done, tile_done_at(l, T_P + t))
                square(squares_at(l) + KT + t, t % 2, accum[t % 2][:, 0:R])
                nc.scalar.activation(e_buf[:, t, :], accum[t % 2][:, 0:R], ACT.Copy, scale=vec(l, V_PLE + t)).then_inc(acc_free[t % 2], 1)
                if t % 4 == 3:
                    next_hi(l, 19, t // 4, T_P + t)
                for g in {9: (0,), 12: (1,), 15: (2, 3)}.get(t, ()):
                    act.wait_ge(s.h_step, 8 * l + (3, 4, 7, 8)[g])
                    nc.scalar.activation(b_hi[:, 4 * g:4 * g + 4, :], x[:, 4 * g:4 * g + 4, :], ACT.Copy).then_inc(s.hhi_ready, 1)

            def gate_tile(i, j, first):
                t = 4 * i + j
                act.wait_ge(s.tile_done, tile_done_at(l, t + T_T))
                if not first or j >= 2:
                    act.wait_ge(s.xnew, t + (KT * l - 1))
                bank = gate_bank[j] if first else accum[j % 2]
                nc.scalar.activation(tmp[j % 2][:, :], bank[:, 0:R], ACT.Tanh, scale=0.5).then_inc(acc_free[j % 2], 1)
                if l + 1 < DEPTH or not isinstance(i, int) or i < 3:
                    next_hi(l, 20 + i, j, t + T_T)
                if l + 1 < DEPTH and not (first and j < 2):
                    next_x(t - 2)

            def next_x(t):
                act.wait_ge(s.xnew, t + (KT * l + 1))
                act.wait_ge(s.sq_used, t + (squares_at(l) + 2 * KT - 1))
                nc.scalar.activation(rows(a_hi, t), rows(x, t), ACT.Copy, scale=vec(l + 1, t + V_PRE)).then_inc(s.xhi_ready, 1)
                nc.scalar.activation(sq[:, side_of[0] % 2, :], rows(x, t), ACT.Square).then_inc(s.sq_ready, 1)
                side_of[0] += 1

            side_of = [0]
            for j in range(4):
                gate_tile(0, j, True)
            with act.Fori(1, 3) as i:
                for j in range(4):
                    gate_tile(i, j, False)
            for j in range(4):
                gate_tile(3, j, False)
            if l + 1 < DEPTH:
                next_x(KT - 2)
                next_x(KT - 1)

    @block.vector
    def _(dve):
        v = nc.vector
        dw = lambda l, at: vecs[:, l, bass.ds(at + V_DW, 1)]

        def lo(l, body, slot, cols=SLAB):
            dve.wait_ge(s.hi_ready, body * 4 + (SLABS * l + slot + 1))
            v.tensor_tensor(wlo[:, slot, 0:cols], raw[:, slot % RAW, 0:cols], whi[:, slot, 0:cols].bitcast(F32), ALU.subtract).then_inc(s.lo_ready, 1)

        def x_lo(l, t):
            dve.wait_ge(s.xhi_ready, t + (KT * l + 1))
            v.scalar_tensor_tensor(rows(a_lo, t), rows(x, t), vec(l, t + V_PRE), rows(a_hi, t).bitcast(F32), ALU.mult, ALU.subtract).then_inc(s.xin_ready, 1)

        def stat_scale(l, k, width):
            dve.wait_ge(s.sum_done, stat_at(l, k))
            v.tensor_scalar(st[:, 0:2], ps_p[:, 0:2], 1.0 / width, EPS, ALU.mult, ALU.add)
            v.tensor_scalar(st[0:DEC, 2:3], ps_p[0:DEC, 2:3], 1.0 / width, EPS, ALU.mult, ALU.add).then_inc(s.stat_scaled, 1)

        def stat_diag(l, k):
            dve.wait_ge(s.stat_rs, stat_at(l, k))
            v.tensor_scalar(diag[:, 0:P], ident, rs[:, 0:1], None, ALU.mult)
            v.tensor_scalar(diag[:, P:2 * P], ident, rs[:, 1:2], None, ALU.mult)
            v.tensor_scalar(diag[0:DEC, 2 * P:R], cst[0:DEC, K_ID:K_ID + DEC], rs[0:DEC, 2:3], None, ALU.mult).then_inc(s.diag_ready, 1)

        def stat_read(l, k, dst, by=1.0):
            dve.wait_ge(s.bcast_done, stat_at(l, k))
            v.tensor_scalar(dst[:, :], ps_p[:, 0:R], by, None, ALU.mult).then_inc(s.bcast_read, 1)

        def factors(l):
            at = 6 * l
            dve.wait_ge(s.bcast_read, spread_at(l, ST_X))
            v.tensor_tensor(r2, rs[:, 0:2], rs[:, 0:2], ALU.mult).then_inc(s.rfac_step, 1)
            v.tensor_copy(rx3[:, 0:2], rs[:, 0:2]).then_inc(s.rfac_step, 1)
            v.tensor_copy(rs8[:, 0, :], r_x[:, SEQ:R]).then_inc(s.rfac_step, 1)
            v.tensor_scalar(rs8[:, 1, :], r_x[:, SEQ:R], P ** -0.5, None, ALU.mult).then_inc(s.rfac_step, 1)
            dve.wait_ge(s.rfac_step, at + 4)
            v.tensor_tensor(kk, cst[:, K_KDEC:K_KDEC + 16].rearrange("p (h c) -> p h c", c=2), wide(r2, [P, HEADS, 2]), ALU.mult)
            v.tensor_tensor(gi, cst[:, K_GI:K_GI + 24].rearrange("p (h c) -> p h c", c=3), wide(rx3, [P, HEADS, 3]), ALU.mult).then_inc(s.rfac_step, 1)
            dve.wait_ge(s.rfac_step, at + 5)
            v.tensor_tensor(g2, gi, gi, ALU.mult).then_inc(s.rfac_step, 1)

        def conv_b(l, ct, first=False):
            dve.wait_ge(s.tile_done, tile_done_at(l, 2 * ct))
            v.tensor_tensor(tmp[0][:, :], accum[0][:, 0:R], r_x[:, :], ALU.mult).then_inc(acc_free[0], 1)

        def conv_a(l, ct, first=False):
            dve.wait_ge(s.tile_done, tile_done_at(l, 2 * ct + 1))
            if not first:
                dve.wait_ge(s.u_ready, ct + CT * l)
            v.scalar_tensor_tensor(tmp[1][:, :], accum[1][:, 0:R], 0.5, r_x[:, :], ALU.mult, ALU.mult).then_inc(acc_free[1], 1)

        def conv_u(l, ct):
            dve.wait_ge(s.tanh_ready, ct + (CT * l + 1))
            dve.wait_ge(acc_free[1], read_out_at(l, ct))
            v.scalar_tensor_tensor(u_flat[:, bass.ds(ct * UW + PAD, R)], tmp[2][:, :], 1.0, tmp[1][:, :], ALU.add, ALU.mult).then_inc(s.u_ready, 1)

        def taps(l, done, ct, k0, k1, first, last):
            done = done + TAPS_DONE * l
            even = c_flat[:, bass.ds(ct * R, SEQ)]
            odd = tmp[3][:, 0:SEQ]
            for m in range(first, last):
                src = u_flat[:, bass.ds(ct * UW + (k0 + m), SEQ)]
                w = dw(l, ct * TAPS + (k0 + m))
                if m == 0 and k0 == 0:
                    dve.wait_ge(s.u_ready, ct + (CT * l + 1))
                    v.tensor_scalar(even, src, w, vec(l, ct + V_BDW), ALU.mult, ALU.add).then_inc(s.tap_done, 1)
                elif m == 0:
                    dve.wait_ge(s.tap_done, done)
                    v.scalar_tensor_tensor(even, src, w, even, ALU.mult, ALU.add).then_inc(s.tap_done, 1)
                elif m == 1:
                    dve.wait_ge(s.tap_done, done + 1)
                    v.tensor_scalar(odd, src, w, None, ALU.mult).then_inc(s.tap_done, 1)
                else:
                    out = odd if m % 2 else even
                    dve.wait_ge(s.tap_done, done + (m - 1))
                    v.scalar_tensor_tensor(out, src, w, out, ALU.mult, ALU.add).then_inc(s.tap_done, 1)
            if last == k1 - k0:
                dve.wait_ge(s.tap_done, done + (k1 - k0))
                v.tensor_tensor(even, even, odd, ALU.add).then_inc(s.tap_done, 1)

        def sample_products(l, half):
            if half == 0:
                dve.wait_ge(s.ust_ready, CT * (l + 1))
                dve.wait_ge(s.convstate_in, 16 * (l + 1))
            else:
                dve.wait_ge(s.sconv_step, 5 * l + 2)
            c0, n = half * CT // 2, CT // 2
            w = vecs[:, l, V_DW + c0 * TAPS:V_DW + (c0 + n) * TAPS].rearrange("p (c k) -> p c k", c=n).unsqueeze(2).to_broadcast([P, n, DEC, TAPS])
            v.tensor_tensor(sprod[:, :, :, :], ust[:, c0:c0 + n, :, :].rearrange("p c k b -> p c b k"), w, ALU.mult).then_inc(s.sconv_step, 1)

        def sample_sums(l, half):
            dve.wait_ge(s.sconv_step, 5 * l + 2 * half + 1)
            n = CT // 2 * DEC
            v.tensor_reduce(r_t[:, half * n:half * n + n], sprod[:, :, :, :].rearrange("p c b k -> p (c b) k"), AX.X, ALU.add).then_inc(s.sconv_step, 1)
            if half:
                dve.wait_ge(s.sconv_step, 5 * l + 4)
                bias = vecs[:, l, V_BDW:V_BDW + CT].unsqueeze(2).to_broadcast([P, CT, DEC])
                v.tensor_tensor(c_buf[:, :, SEQ:R], r_t[:, 0:CT * DEC].rearrange("p (c b) -> p c b", c=CT), bias, ALU.add).then_inc(s.sconv_step, 1)

        def ret_scores(l, h):
            dve.wait_ge(s.s1_done, h + HEADS * l)
            kcol = lambda chunk: small[:, bass.ds((h - 1) * 2 + (16 + chunk), 1)]
            v.scalar_tensor_tensor(pmat[:, 0:P], ps_p[:, 0:P], kcol(0), tri, ALU.mult, ALU.mult)
            v.tensor_scalar(pmat[:, P:2 * P], ps_p[:, P:2 * P], kcol(0), None, ALU.mult)
            v.scalar_tensor_tensor(pmat[:, 2 * P:3 * P], ps_p[:, 2 * P:3 * P], kcol(1), tri, ALU.mult, ALU.mult).then_inc(s.p_ready, 1)

        def ret_state(l, h):
            n = h + HEADS * l
            gamma = cst[:, bass.ds((h - 1) + K_GAM, 1)]
            dve.wait_ge(s.s2_done, n)
            dve.wait_ge(s.state_in, 16 * n)
            v.scalar_tensor_tensor(s_new[:, 0:4 * P], s_new[:, 0:4 * P], gamma, ps_s0[:, :], ALU.mult, ALU.add)
            v.scalar_tensor_tensor(s_new[:, 4 * P:8 * P], s_new[:, 4 * P:8 * P], gamma, ps_s1[:, :], ALU.mult, ALU.add).then_inc(s.snew_ready, 1)
            v.bn_stats(bn[:, 0:6], ps_o[:, 0:P])
            v.bn_stats(bn[:, 6:12], ps_o[:, P:2 * P]).then_inc(s.bn_done, 1)

        def ret_stats(l, h):
            n = h + HEADS * l
            dve.wait_ge(s.s3b_done, n)
            v.bn_stats(bn[0:DEC, 12:18], ps_st[0:DEC, 3 * P:4 * P]).then_inc(s.bn_done, 1)
            dve.wait_ge(s.bn_done, 2 * n)
            v.memset(held, 0.0)
            v.bn_aggr(mv[:, 0, :], bn[:, 0:6])
            v.bn_aggr(mv[:, 1, :], bn[:, 6:12])
            v.bn_aggr(mv[0:DEC, 2, :], bn[0:DEC, 12:18]).then_inc(s.stat_ready, 1)

        def ret_gate(l, h):
            n = h + HEADS * l
            dve.wait_ge(s.s4_done, n)
            dve.wait_ge(s.sg_ready, n + 1)
            if not isinstance(h, int) or h > 1 or l:
                dve.wait_ge(s.ret_ready, n - 1)
            v.scalar_tensor_tensor(rt[:, :], ps_s0[:, 0:R], vec(l, (h - 1) + V_RET), sg[:, :], ALU.mult, ALU.mult).then_inc(s.rt_ready, 1)

        def ret_lo(l, h):
            dve.wait_ge(s.rhi_ready, h + HEADS * l)
            v.tensor_tensor(rows(b_lo, h - 1), rt[:, :], rows(b_hi, h - 1).bitcast(F32), ALU.subtract).then_inc(s.ret_ready, 1)

        def head(l, h, prev, turn, beside):
            n = h + HEADS * l
            body = 5 + h
            if turn:
                ret_gate(l, h - 1)
            if prev:
                ret_scores(l, h)
            beside[0]()
            lo(l, body, 0)
            dve.wait_ge(acc_free[1], read_out_at(l, 2 * h + T_H // 2))
            v.tensor_tensor(zs[:, :, :], zs[:, :, :], wide(cst[:, K_COS:K_COS + R], [P, 2, R]), ALU.mult).then_inc(s.rope_step, 1)
            v.tensor_tensor(zw[:, :, :], zw[:, :, :], wide(cst[:, K_SIN:K_SIN + R], [P, 2, R]), ALU.mult).then_inc(s.rope_step, 1)
            if prev:
                ret_state(l, h)
            dve.wait_ge(s.rope_step, 2 * n + 2)
            v.tensor_tensor(qk[:, :, :], zs[:, :, :], zw[:, :, :], ALU.add).then_inc(s.rope_done, 1)
            beside[1]()
            if turn:
                ret_lo(l, h - 1)
            lo(l, body, 1)
            dve.wait_ge(acc_free[0], read_out_at(l, 2 * h + (T_H // 2 + 1)))
            if prev:
                dve.wait_ge(s.s3a_done, n)
            dve.wait_ge(s.rope_done, n + 1)
            v.tensor_tensor(qks[:, :, :], qk[:, :, SEQ:R], rs8, ALU.mult)
            v.tensor_tensor(vs[:, :], vt[:, SEQ:R], r_x[:, SEQ:R], ALU.mult).then_inc(s.kv_ready, 1)
            beside[2]()
            dve.wait_ge(s.khi_ready, n + 1)
            v.tensor_tensor(stack_cols[:, 0, 2:4, :], wide(qks[:, 1, :], [P, 2, DEC]), stack_cols[:, 0, 0:2, :].bitcast(F32), ALU.subtract)
            v.tensor_tensor(stack_cols[:, 1, 1:4:2, :], wide(vs[:, :], [P, 2, DEC]), stack_cols[:, 1, 0:4:2, :].bitcast(F32), ALU.subtract).then_inc(s.stack_in, 1)
            if prev:
                ret_stats(l, h)
            lo(l, body, 2)
            beside[3]()
            dve.wait_ge(s.tile_done, tile_done_at(l, 4 * h + (T_H + 3)))
            dve.wait_ge(s.sg_ready, n + 1)
            v.tensor_tensor(gz[:, :], accum[1][:, 0:R], r_x[:, :], ALU.mult).then_inc(acc_free[1], 1)
            lo(l, body, 3)

        def parts(l, segments):
            one_by_one = [(seg, m) for seg in segments for m in range(seg[3] - seg[2])]
            count = len(one_by_one)

            def run(j):
                for seg, m in one_by_one[count * j // 4:count * (j + 1) // 4]:
                    taps(l, *seg, m, m + 1)
            return [lambda j=j: run(j) for j in range(4)]

        u_flat = u_buf[:, :, :].rearrange("p c r -> p (c r)")
        c_flat = c_buf[:, :, :].rearrange("p c r -> p (c r)")
        v.memset(small[:, :], 0.0).then_inc(s.small_set, 1)
        dve.wait_ge(s.small_set, 1)
        v.memset(st[:, 2:3], 1.0).then_inc(acc_free[0], 1)
        v.memset(eps3, EPS)
        v.memset(minus_half, -0.5).then_inc(acc_free[1], 1)
        v.memset(rx3[:, 2:3], 1.0).then_inc(s.rt_ready, 1)
        v.memset(ones[:, :], 1.0).then_inc(s.sg_ready, 1)
        v.memset(ones_mean[:, :], 1.0 / CONV).then_inc(s.consts_set, 1)
        v.memset(r_x[:, 0:1], 0.0).then_inc(s.gc_ready, 1)
        v.memset(r_t[:, 0:1], 0.0).then_inc(s.sprompt_out, 1)
        v.memset(r_t[:, 1:2], 0.0).then_inc(s.sq_used, 1)
        dve.wait_ge(s.gc_ready, 1)
        lo(0, 0, 0)
        dve.wait_ge(s.vecs_in, 16)
        for g in range(4):
            for k in range(4 * g, 4 * g + 4):
                x_lo(0, k)
            if g:
                dve.wait_ge(s.sq_ready, g + 1)
                dve.wait_ge(s.sq_used, g)
                v.tensor_tensor(e_buf[:, 0:4, :], e_buf[:, 0:4, :], e_buf[:, 4 * g:4 * g + 4, :], ALU.add).then_inc(s.sq_used, 1)
            if g == 2:
                lo(0, 0, 1)
        lo(0, 0, 2)
        dve.wait_ge(s.consts_in, 16)

        for l in range(DEPTH):
            last = l == DEPTH - 1
            v.memset(u_buf[:, :, 0:PAD], 0.0).then_inc(s.pad_set, 1)
            dve.wait_ge(s.pad_set, l + 1)
            stat_scale(l, ST_X, D_MODEL)
            stat_diag(l, ST_X)
            stat_read(l, ST_X, r_x)
            dve.wait_ge(s.bcast_read, spread_at(l, ST_X))
            for j in range(4):
                (conv_b, conv_a)[j % 2](l, j // 2, j == 1 and l == 0)
                if j == 0 and l == 0:
                    lo(0, 0, 3)
                lo(l, 1, j)
                if j == 1:
                    factors(l)
                if j % 2:
                    conv_u(l, j // 2)
                if j >= 2:
                    half = CONV_0 // 2
                    taps(l, 0, 0, 0, CONV_0, half * (j - 2), half * (j - 1))
            seen = CONV_C + 1
            with dve.Fori(1, 4) as i:
                beside = parts(l, [((i - 1) * seen + (CONV_0 + 1), i, 0, CONV_C)])
                for j in range(4):
                    (conv_b, conv_a)[j % 2](l, 2 * i + j // 2)
                    beside[j]()
                    lo(l, 1 + i, j)
                    if j % 2:
                        conv_u(l, 2 * i + j // 2)
            at = [CONV_0 + 1 + 3 * seen]

            def segment(ct, k0, k1):
                at[0] += k1 - k0 + 1
                return (at[0] - (k1 - k0 + 1), ct, k0, k1)

            conv_0 = parts(l, [segment(0, CONV_0, CONV_H0)])
            samples = (lambda: sample_products(l, 0), lambda: sample_sums(l, 0),
                       lambda: sample_products(l, 1), lambda: sample_sums(l, 1))
            head(l, 0, False, False, [lambda j=j: (samples[j](), conv_0[j]()) for j in range(4)])
            head(l, 1, True, False, parts(l, [segment(0, CONV_H0, TAPS), segment(1, CONV_C, TAPS), segment(2, CONV_C, TAPS)]))
            start, stride = at[0], TAPS + CONV_2 + 3
            with dve.Fori(0, 2) as i:
                first = start + i * stride
                head(l, 2 * i + 2, True, True, parts(l, [(first, i + 4, 0, CONV_1)]))
                head(l, 2 * i + 3, True, True, parts(l, [(first + (CONV_1 + 1), i + 4, CONV_1, TAPS),
                                                         (first + (TAPS + 2), i + 6, 0, CONV_2)]))
            at[0] += 2 * stride
            head(l, 6, True, True, parts(l, [segment(3, CONV_C, TAPS), segment(6, CONV_2, CONV_3)]))
            head(l, 7, True, True, parts(l, [segment(6, CONV_3, TAPS), segment(7, CONV_2, TAPS)]))
            assert at[0] == TAPS_DONE

            def channel_sum(src, dst):
                v.tensor_reduce(dst[:, :], src[:, :, :].rearrange("p c r -> p r c"), AX.X, ALU.add).then_inc(s.ln_summed, 1)

            def gate_in(t):
                dve.wait_ge(s.tile_done, tile_done_at(l, T_G + t))
                if t >= 2:
                    dve.wait_ge(s.gc_ready, CT * l + t)
                v.tensor_tensor(tmp[t % 2][:, :], accum[t % 2][:, 0:R], r_x[:, :], ALU.mult).then_inc(acc_free[t % 2], 1)

            ret_gate(l, 7)
            dve.wait_ge(s.tap_done, TAPS_DONE * (l + 1))
            dve.wait_ge(s.sconv_step, 5 * (l + 1))
            channel_sum(c_buf, acc[(3 * l + 1) % 2])
            gate_in(0)
            ret_scores(l, 8)
            lo(l, 13, 0)
            ret_lo(l, 7)
            gate_in(1)
            dve.wait_ge(s.mean_done, l + 1)
            v.tensor_tensor(c_buf[:, :, :], c_buf[:, :, :], wide(ps_p[:, 0:R], [P, CT, R]), ALU.subtract).then_inc(s.ln_centered, 1)
            ret_state(l, 8)
            lo(l, 13, 1)
            gate_in(2)
            lo(l, 13, 2)
            ret_stats(l, 8)
            gate_in(3)
            dve.wait_ge(s.ln_squared, l + 1)
            channel_sum(ln_sq, acc[3 * l % 2])
            lo(l, 13, 3)
            stat_scale(l, ST_LN, CONV)
            stat_diag(l, ST_LN)
            gate_in(4)
            ret_gate(l, 8)
            lo(l, 14, 0)
            dve.wait_ge(s.bcast_done, stat_at(l, ST_LN))
            for half in range(2):
                part = c_buf[:, 4 * half:4 * half + 4, :]
                v.tensor_tensor(part, part, wide(ps_p[:, 0:R], [P, 4, R]), ALU.mult).then_inc(s.ln_scaled, 1)
            gate_in(5)
            lo(l, 14, 1)
            ret_lo(l, 8)
            gate_in(6)
            lo(l, 14, 2)
            gate_in(7)
            for part, (c0, c1) in enumerate(((0, 2), (2, 4), (4, 8))):
                dve.wait_ge(s.chi_ready, 3 * l + part + 1)
                v.tensor_tensor(c_lo[:, c0:c1, :], c_buf[:, c0:c1, :], c_hi[:, c0:c1, :].bitcast(F32), ALU.subtract).then_inc(s.c_ready, 1)
            lo(l, 14, 3)
            for j in range(4):
                for e in range(2):
                    c = 2 * j + e
                    dve.wait_ge(s.tile_done, tile_done_at(l, T_W + c))
                    dve.wait_ge(s.gc_ready, CT * (l + 1) + 1)
                    v.scalar_tensor_tensor(gc_buf[:, c, :], accum[e][:, 0:R], vec(l, V_BPW + c), gc_buf[:, c, :], ALU.add, ALU.mult).then_inc(acc_free[e], 1)
                if j == 0:
                    dve.wait_ge(s.phi_ready, l + 1)
                    v.tensor_tensor(a_lo[:, CT:CT + PT, :], p_in[:, :, :], a_hi[:, CT:CT + PT, :].bitcast(F32), ALU.subtract).then_inc(s.pin_ready, 1)
                for e in range(2):
                    c = 2 * j + e
                    dve.wait_ge(s.cohi_ready, CT * l + c + 1)
                    v.tensor_tensor(a_lo[:, c, :], gc_buf[:, c, :], a_hi[:, c, :].bitcast(F32), ALU.subtract).then_inc(s.cout_ready, 1)
                lo(l, 15, j)
            with dve.Fori(0, 3) as i:
                for j in range(4):
                    lo(l, 16 + i, j)
            for j in range(4):
                lo(l, 19, j, 4 * PT * P)
            stat_scale(l, ST_M, D_MODEL)
            stat_diag(l, ST_M)
            lo(l, 20, 0)
            stat_read(l, ST_M, r_t)
            dve.wait_ge(s.bcast_read, spread_at(l, ST_M))
            for bank in range(2):
                dve.wait_ge(acc_free[bank], read_out_at(l, T_P // 2 - 1))
            group = lambda t, g: t[:, 4 * g:4 * g + 4, :]

            def scale_m(g):
                v.tensor_tensor(group(m_buf, g), group(m_buf, g), wide(r_t[:, :], [P, 4, R]), ALU.mult).then_inc(s.h_step, 1)

            def add_m(g, behind):
                dve.wait_ge(s.h_step, 8 * l + behind)
                v.tensor_tensor(group(x, g), group(x, g), group(m_buf, g), ALU.add).then_inc(s.h_step, 1)

            def h_lo(g):
                dve.wait_ge(s.hhi_ready, 4 * l + g + 1)
                v.tensor_tensor(group(b_lo, g), group(x, g), group(b_hi, g).bitcast(F32), ALU.subtract).then_inc(s.h_ready, 1)

            scale_m(0)
            scale_m(1)
            add_m(0, 1)
            add_m(1, 2)
            lo(l, 20, 1)
            h_lo(0)
            scale_m(2)
            scale_m(3)
            lo(l, 20, 2)
            h_lo(1)
            add_m(2, 5)
            add_m(3, 6)
            lo(l, 20, 3)
            h_lo(2)
            h_lo(3)
            def gate_mul(t, j):
                dve.wait_ge(acc_free[j % 2], pair_read(l, t, j))
                v.scalar_tensor_tensor(tmp[2 + j % 2][:, :], tmp[j % 2][:, :], 1.0, rows(e_buf, t), ALU.add, ALU.mult).then_inc(s.gate_step, 1)

            def pair_read(l, t, j):
                return read_out_at(l, t // 2 + T_T // 2) if isinstance(t, int) else read_out_at(l, pair_at[0] + (T_T // 2 + j // 2))

            def gate_add(t):
                dve.wait_ge(s.gate_step, t + (KT * l + 1))
                v.tensor_tensor(rows(x, t), rows(x, t), tmp[2 + side_at[0] % 2][:, :], ALU.add).then_inc(s.xnew, 1)

            pair_at, side_at = [0], [0]
            stat_scale(l, ST_E, D_MODEL)
            stat_diag(l, ST_E)
            lo(l, 21, 0)
            stat_read(l, ST_E, r_t, 0.5)
            dve.wait_ge(s.bcast_read, spread_at(l, ST_E))
            for g in range(4):
                v.tensor_tensor(group(e_buf, g), group(e_buf, g), wide(r_t[:, :], [P, 4, R]), ALU.mult).then_inc(s.e_step, 1)
            for j in range(4):
                if j:
                    lo(l, 21, j)
                if j == 0:
                    dve.wait_ge(s.e_step, 4 * l + 4)
                gate_mul(j, j)
                side_at[0] = j
                gate_add(j)
                if j and not last:
                    x_lo(l + 1, j - 1)

            def gate_body(i, more):
                for j in range(4):
                    t = 4 * i + j
                    pair_at[0] = 2 * i
                    gate_mul(t, j)
                    if more:
                        lo(l, 21 + i, j)
                    side_at[0] = j
                    gate_add(t)
                    if not last:
                        x_lo(l + 1, t - 1)

            with dve.Fori(1, 3) as i:
                gate_body(i, True)
            gate_body(3, not last)
            if not last:
                x_lo(l + 1, KT - 1)

    @block.gpsimd
    def _(pool):
        def add_squares(l_at, buf, count=KT):
            for k in range(count):
                n = l_at + k
                pool.wait_ge(s.sq_ready, n + 1)
                if k == 0:
                    if n:
                        pool.wait_ge(s.sq_used, n)
                    nc.gpsimd.tensor_copy(buf[:, :], sq[:, n % 2, :]).then_inc(s.sq_used, 1)
                else:
                    pool.wait_ge(s.sq_used, n)
                    nc.gpsimd.tensor_tensor(buf[:, :], buf[:, :], sq[:, n % 2, :], ALU.add).then_inc(s.sq_used, 1)

        def root(l, k):
            pool.wait_ge(s.stat_scaled, stat_at(l, k))
            nc.gpsimd.tensor_tensor(rs, st, minus_half, ALU.pow).then_inc(s.stat_rs, 1)

        def ret_root(l, h):
            n = h + HEADS * l
            at = 5 * n
            pool.wait_ge(s.stat_ready, n + 1)
            g2_h = small[:, bass.ds(h * 3 + 56, 3)]
            gi_h = small[:, bass.ds(h * 3 + 32, 3)]
            nc.gpsimd.tensor_tensor(var_t, mv[:, :, 1], g2_h, ALU.mult).then_inc(s.pool_step, 1)
            pool.wait_ge(s.pool_step, at + 1)
            nc.gpsimd.tensor_tensor(var_t, var_t, eps3, ALU.add).then_inc(s.pool_step, 1)
            pool.wait_ge(s.pool_step, at + 2)
            nc.gpsimd.tensor_tensor(rs_t, var_t, minus_half, ALU.pow).then_inc(s.pool_step, 1)
            pool.wait_ge(s.pool_step, at + 3)
            nc.gpsimd.tensor_tensor(sc_t, rs_t, gi_h, ALU.mult).then_inc(s.pool_step, 1)
            pool.wait_ge(s.pool_step, at + 4)
            nc.gpsimd.tensor_tensor(mean_sc, mv[:, :, 0], sc_t, ALU.mult).then_inc(s.pool_step, 1)
            pool.wait_ge(s.pool_step, at + 5)
            nc.gpsimd.tensor_tensor(nb_t, zero3, mean_sc, ALU.subtract).then_inc(s.ret_rs, 1)

        for l in range(DEPTH):
            root(l, ST_X)
            with pool.Fori(0, HEADS) as h:
                ret_root(l, h)
            root(l, ST_LN)
            pool.wait_ge(s.mean_done, l + 1)
            add_squares(squares_at(l), acc[(3 * l + 1) % 2])
            root(l, ST_M)
            pool.wait_ge(s.sum_done, stat_at(l, ST_LN))
            add_squares(squares_at(l) + KT, acc[3 * l % 2])
            root(l, ST_E)
            if l < DEPTH - 1:
                add_squares(squares_at(l) + 2 * KT, acc[(3 * l + 1) % 2])


def kernel(x_prompt, x_sample, state_ret, state_conv, p_prompt, p_sample, w_in, w_out, g_ret, w_dw,
           b_dw, g_cn, b_cn, w_pw2, b_pw2, g_pre, g_post, w_ple, g_ple, w_ple_gate):
    import concourse.bacc as bacc
    from concourse.bass_utils import run_bass_kernel_spmd

    def slabs(w, per_tile, tiles_per_slab):
        d, rows_in, cols = w.shape
        k = rows_in // P
        t = w.reshape(d, k, P, cols // (P * tiles_per_slab), tiles_per_slab, P)
        t = t.transpose(0, 3, 2, 4, 1, 5)
        return np.ascontiguousarray(t).reshape(-1, tiles_per_slab * k * P)

    def features_down(rows_by_features):
        r, f = rows_by_features.shape
        return rows_by_features.reshape(r, f // P, P).transpose(2, 1, 0)

    a = {k: np.asarray(w) for k, w in dict(
        x_prompt=x_prompt, x_sample=x_sample, state_ret=state_ret, state_conv=state_conv, p_prompt=p_prompt,
        p_sample=p_sample, w_in=w_in, w_out=w_out, g_ret=g_ret, w_dw=w_dw, b_dw=b_dw, g_cn=g_cn, b_cn=b_cn,
        w_pw2=w_pw2, b_pw2=b_pw2, g_pre=g_pre, g_post=g_post, w_ple=w_ple, g_ple=g_ple, w_ple_gate=w_ple_gate).items()}
    x_all = np.concatenate([a["x_prompt"][0], a["x_sample"][:, 0]])
    p_all = np.concatenate([a["p_prompt"][:, 0], a["p_sample"][:, :, 0]], axis=1)
    column = lambda w: w.reshape(DEPTH, -1, P).transpose(2, 0, 1)
    dw = a["w_dw"].reshape(DEPTH, TAPS, CT, P).transpose(3, 0, 2, 1).reshape(P, DEPTH, CT * TAPS)
    vectors = [column(a[n]) for n in ("g_pre", "g_post", "g_ple", "g_ret", "b_dw", "g_cn", "b_cn", "b_pw2")] + [dw]
    conv_state = a["state_conv"].reshape(DEPTH, DEC, PAD, CT, P).transpose(0, 4, 3, 2, 1)
    ins = {
        "x_t": features_down(x_all),
        "p_t": np.stack([features_down(p) for p in p_all]),
        "s_ret": a["state_ret"].transpose(0, 2, 3, 1, 4).reshape(DEPTH * HEADS * P, DEC * P),
        "s_conv": conv_state.reshape(DEPTH * P, CT * PAD * DEC),
        "vecs": np.concatenate(vectors, axis=2),
        "consts": constants(),
        "w_in": slabs(a["w_in"], KT, 1),
        "w_pw": slabs(a["w_pw2"], CT, 2),
        "w_out": slabs(a["w_out"], KT, 1),
        "w_ple": slabs(a["w_ple"], PT, 4),
        "w_gate": slabs(a["w_ple_gate"], KT, 1),
    }
    outs = {
        "y_t": (P, KT, R),
        "sp_out": (DEPTH * HEADS * P, P),
        "scp_out": (DEPTH, P, CT, PAD),
        "ss_out": (DEPTH * HEADS * P, DEC * P),
        "scs_out": (DEPTH * P, CT * PAD * DEC),
    }
    nc = bacc.Bacc("TRN2", target_bir_lowering=False, num_devices=1, dynamic_dma_scratch_size=1024)
    ins = {k: np.ascontiguousarray(w) for k, w in ins.items()}
    args = [nc.dram_tensor(k, w.shape, F32, kind="ExternalInput").ap() for k, w in ins.items()]
    args += [nc.dram_tensor(k, shape, F32, kind="ExternalOutput").ap() for k, shape in outs.items()]
    with ExitStack() as ctx:
        build(nc, ctx, *args)
    got = run_bass_kernel_spmd(nc, [ins], core_ids=[0]).results[0]
    y = got["y_t"].transpose(2, 1, 0).reshape(R, D_MODEL)
    new_states = got["ss_out"].reshape(DEPTH, HEADS, P, DEC, P).transpose(0, 3, 1, 2, 4)
    conv_prompt = got["scp_out"].transpose(0, 3, 2, 1).reshape(DEPTH, 1, PAD, CONV)
    conv_sample = got["scs_out"].reshape(DEPTH, P, CT, PAD, DEC).transpose(0, 4, 3, 2, 1).reshape(DEPTH, DEC, PAD, CONV)
    return (y[:SEQ].reshape(1, SEQ, D_MODEL), y[SEQ:].reshape(DEC, 1, D_MODEL),
            got["sp_out"].reshape(DEPTH, 1, HEADS, P, P), conv_prompt, new_states, conv_sample)
```

```python
import numpy as np
import concourse.bass as bass
from concourse import mybir
from contextlib import ExitStack

F32 = mybir.dt.float32
F32R = mybir.dt.float32r
ACT = mybir.ActivationFunctionType
ALU = mybir.AluOpType
AX = mybir.AxisListType

P = 128
DEPTH, D_MODEL, SEQ, DEC, PAST = 2, 2048, 256, 8, 2048
HEADS, CONV, TAPS, P_DIM = 8, 1024, 31, 256
EPS = 1e-6
R = SEQ + DEC
KT = D_MODEL // P
CT = CONV // P
PT = P_DIM // P
PAD = TAPS - 1
UW = PAD + R
SLAB = KT * P
RING, RAW = 4, 2

T_C, T_H, T_G, T_W, T_O, T_OP, T_T, TILES = 0, 16, 48, 56, 64, 76, 96, 112
S_C, S_H, S_G, S_W, S_O, S_OP, S_T, SLABS = 0, 16, 48, 56, 60, 72, 80, 96

V_PRE, V_POST, V_PLE, V_RET, V_BDW, V_GCN, V_BCN, V_BPW, V_DW = 0, 16, 32, 48, 56, 64, 72, 80, 88
VW = V_DW + CT * TAPS

K_ID, K_TRI, K_COS, K_SIN = 0, P, 2 * P, 2 * P + R
K_KDEC = K_SIN + R
K_GI = K_KDEC + 2 * HEADS
K_GAM = K_GI + 3 * HEADS
K_END = K_GAM + HEADS
K_MASK = K_END + HEADS
KW = K_MASK + DEC


CONV_0, CONV_H0, CONV_C, CONV_1, CONV_2, CONV_3 = 12, 25, 20, 22, 13, 27
TAPS_DONE = CT * TAPS + 3 + 3 * 2 + 2 * 2 + 3 + 2


def constants():
    c = np.zeros((P, KW), np.float32)
    c[:, K_ID:K_ID + P] = np.eye(P)
    c[:, K_TRI:K_TRI + P] = np.triu(np.ones((P, P)))
    half = P // 2
    inv = (10000.0 ** -(np.arange(half) / half)).astype(np.float32)
    pos = np.concatenate([np.arange(SEQ), np.full(DEC, PAST)]).astype(np.float32)
    ang = (pos[None, :] * inv[:, None]).astype(np.float32)
    cos, sin = np.cos(ang.astype(np.float64)), np.sin(ang.astype(np.float64))
    c[:, K_COS:K_COS + R] = np.concatenate([cos, cos])
    c[:, K_SIN:K_SIN + R] = np.concatenate([-sin, sin])
    log_g = np.log1p(-np.exp2(-5.0 - np.arange(HEADS)))
    row = np.arange(P)
    for h in range(HEADS):
        for chunk in range(2):
            c[:, K_KDEC + 2 * h + chunk] = np.exp(-log_g[h] * (row + P * chunk)) * P ** -0.5
            c[:, K_GI + 3 * h + chunk] = np.exp(log_g[h] * (row + P * chunk))
        c[:, K_GI + 3 * h + 2] = 1.0
        c[:, K_GAM + h] = np.exp(log_g[h])
        c[:, K_END + h] = np.exp(log_g[h] * (SEQ - 1))
    c[:, K_MASK:K_MASK + DEC] = (row[:, None] % DEC) == np.arange(DEC)[None, :]
    return c


def out_and_ple():
    for j in range(4):
        yield "m", 12 + j, 2 * j, 0
        for e in range(4):
            yield "e", 4 * j + e, 2 * j + 1, e


M_DONE, E_DONE = 28, 32


def tile_done_at(l, t):
    return t + (TILES * l + 1)


def bank_free_at(l, pair):
    return pair + (TILES // 2 * l + 1)


def read_out_at(l, pair):
    return pair + (TILES // 2 * l + 2)


class Signals:

    def __init__(self, nc):
        self.vecs_in = nc.alloc_semaphore("vecs_in")
        self.consts_in = nc.alloc_semaphore("consts_in")
        self.x_in = [nc.alloc_semaphore(f"x_in_{g}") for g in range(4)]
        self.p_in = nc.alloc_semaphore("p_in")
        self.convstate_in = nc.alloc_semaphore("convstate_in")
        self.state_in = nc.alloc_semaphore("state_in")
        self.state_out = nc.alloc_semaphore("state_out")
        self.sprompt_out = nc.alloc_semaphore("sprompt_out")
        self.scp_out = nc.alloc_semaphore("scp_out")
        self.scs_out = nc.alloc_semaphore("scs_out")
        self.y_out = nc.alloc_semaphore("y_out")
        self.hi_ready = nc.alloc_semaphore("hi_ready")
        self.lo_ready = nc.alloc_semaphore("lo_ready")
        self.tile_done = nc.alloc_semaphore("tile_done")
        self.xhi_ready = nc.alloc_semaphore("xhi_ready")
        self.xin_ready = nc.alloc_semaphore("xin_ready")
        self.chi_ready = nc.alloc_semaphore("chi_ready")
        self.c_ready = nc.alloc_semaphore("c_ready")
        self.phi_ready = nc.alloc_semaphore("phi_ready")
        self.pin_ready = nc.alloc_semaphore("pin_ready")
        self.rhi_ready = nc.alloc_semaphore("rhi_ready")
        self.ret_ready = nc.alloc_semaphore("ret_ready")
        self.cohi_ready = nc.alloc_semaphore("cohi_ready")
        self.cout_ready = nc.alloc_semaphore("cout_ready")
        self.hhi_ready = nc.alloc_semaphore("hhi_ready")
        self.h_ready = nc.alloc_semaphore("h_ready")
        self.sq_ready = nc.alloc_semaphore("sq_ready")
        self.sq_used = nc.alloc_semaphore("sq_used")
        self.sum_done = nc.alloc_semaphore("sum_done")
        self.stat_scaled = nc.alloc_semaphore("stat_scaled")
        self.stat_rs = nc.alloc_semaphore("stat_rs")
        self.diag_ready = nc.alloc_semaphore("diag_ready")
        self.bcast_done = nc.alloc_semaphore("bcast_done")
        self.bcast_read = nc.alloc_semaphore("bcast_read")
        self.small_set = nc.alloc_semaphore("small_set")
        self.consts_set = nc.alloc_semaphore("consts_set")
        self.pad_set = nc.alloc_semaphore("pad_set")
        self.rfac_step = nc.alloc_semaphore("rfac_step")
        self.tanh_ready = nc.alloc_semaphore("tanh_ready")
        self.u_ready = nc.alloc_semaphore("u_ready")
        self.ust_ready = nc.alloc_semaphore("ust_ready")
        self.tap_done = nc.alloc_semaphore("tap_done")
        self.sconv_step = nc.alloc_semaphore("sconv_step")
        self.gc_ready = nc.alloc_semaphore("gc_ready")
        self.ln_summed = nc.alloc_semaphore("ln_summed")
        self.mean_done = nc.alloc_semaphore("mean_done")
        self.ln_centered = nc.alloc_semaphore("ln_centered")
        self.ln_squared = nc.alloc_semaphore("ln_squared")
        self.ln_scaled = nc.alloc_semaphore("ln_scaled")
        self.silu_ready = nc.alloc_semaphore("silu_ready")
        self.rope_step = nc.alloc_semaphore("rope_step")
        self.rope_done = nc.alloc_semaphore("rope_done")
        self.kv_ready = nc.alloc_semaphore("kv_ready")
        self.stack_hi_ready = nc.alloc_semaphore("stack_hi_ready")
        self.stack_in = nc.alloc_semaphore("stack_in")
        self.scores_done = nc.alloc_semaphore("scores_done")
        self.rows_ready = nc.alloc_semaphore("rows_ready")
        self.p_ready = nc.alloc_semaphore("p_ready")
        self.vbd_ready = nc.alloc_semaphore("vbd_ready")
        self.values_done = nc.alloc_semaphore("values_done")
        self.snew_ready = nc.alloc_semaphore("snew_ready")
        self.sprompt_ready = nc.alloc_semaphore("sprompt_ready")
        self.bn_done = nc.alloc_semaphore("bn_done")
        self.stat_ready = nc.alloc_semaphore("stat_ready")
        self.pool_step = nc.alloc_semaphore("pool_step")
        self.ret_rs = nc.alloc_semaphore("ret_rs")
        self.sample_out_done = nc.alloc_semaphore("sample_out_done")
        self.os_ready = nc.alloc_semaphore("os_ready")
        self.sample_rows_done = nc.alloc_semaphore("sample_rows_done")
        self.og_ready = nc.alloc_semaphore("og_ready")
        self.turn_done = nc.alloc_semaphore("turn_done")
        self.rt_ready = nc.alloc_semaphore("rt_ready")
        self.sg_ready = nc.alloc_semaphore("sg_ready")
        self.h_step = nc.alloc_semaphore("h_step")
        self.e_step = nc.alloc_semaphore("e_step")
        self.gate_step = nc.alloc_semaphore("gate_step")
        self.xnew = nc.alloc_semaphore("xnew")


def build(nc, ctx, x_t, p_t, s_ret, s_conv, vecs_d, consts_d, w_in, w_pw, w_out, w_ple, w_gate,
          y_t, sp_out, scp_out, ss_out, scs_out):
    sb_at = {}
    cursor = [(nc.sbuf_base + 31) // 32 * 32]

    def sb(name, shape, dt=F32, at=None):
        size = int(np.prod(shape[1:])) * 4
        where = cursor[0] if at is None else at
        if at is None:
            cursor[0] = (cursor[0] + size + 31) // 32 * 32
        assert where + size <= nc.sbuf_usable_end, (name, where, size)
        sb_at[name] = (where, where + size)
        return nc.alloc_sbuf_tensor_at(name, shape, dt, offset=where)

    raw = sb("raw", [P, RAW, SLAB])
    whi = sb("whi", [P, RING, SLAB], F32R)
    wlo = sb("wlo", [P, RING, SLAB], F32R)
    a_hi = sb("a_hi", [P, KT, R], F32R)
    a_lo = sb("a_lo", [P, KT, R], F32R)
    b_hi = sb("b_hi", [P, KT, R], F32R)
    b_lo = sb("b_lo", [P, KT, R], F32R)
    c_buf = sb("c_buf", [P, CT, R], at=sb_at["b_hi"][0] + CT * R * 4)
    gc_buf = sb("gc_buf", [P, CT, R], at=sb_at["b_lo"][0] + CT * R * 4)
    c_lo = sb("c_lo", [P, CT, R], F32R, at=sb_at["c_buf"][0])
    x = sb("x", [P, KT, R])
    vecs = sb("vecs", [P, DEPTH, VW])
    cst = sb("cst", [P, KW])
    ones = sb("ones", [P, P])
    ones_mean = sb("ones_mean", [P, P])
    r_x = sb("r_x", [P, R])
    r_t = sb("r_t", [P, R])
    diag = sb("diag", [P, R])
    acc = [sb(f"acc{i}", [P, R]) for i in range(2)]
    sq = sb("sq", [P, 2, R])
    tmp = [sb(f"tmp{i}", [P, R]) for i in range(4)]
    small = sb("small", [P, 192])
    work = cursor[0]
    m_buf = sb("m_buf", [P, KT, R], at=work)
    e_buf = sb("e_buf", [P, KT, R], at=sb_at["m_buf"][1])
    u_buf = sb("u_buf", [P, CT, UW], at=work)
    ln_sq = sb("ln_sq", [P, CT, R], at=work)
    c_hi = sb("c_hi", [P, CT, R], F32R, at=work)
    ust = sb("ust", [P, CT, TAPS, DEC], at=sb_at["u_buf"][1])
    s_new = sb("s_new", [P, DEC * P], at=sb_at["u_buf"][1])
    heads_at = sb_at["ust"][1]
    sprod = sb("sprod", [P, CT // 2, DEC, TAPS], at=heads_at)
    cursor[0] = heads_at
    vbd = sb("vbd", [32, DEC, P], F32R)
    zs = sb("zs", [P, 2, R])
    zw = sb("zw", [P, 2, R])
    qk = sb("qk", [P, 2, R])
    vt = sb("vt", [P, R])
    vrow = sb("vrow", [P, 2 * P])
    krow = sb("krow", [P, 2 * P])
    pmat = sb("pmat", [P, 3 * P])
    stack_cols = sb("stack_cols", [P, 2, 4, DEC], F32R)
    stack = sb("stack", [32, P], F32R)
    og = sb("og", [P, 3, P])
    s_prompt = sb("s_prompt", [P, P])
    gz = sb("gz", [P, R])
    sg = sb("sg", [P, R])
    rt = sb("rt", [P, R])
    qks = sb("qks", [P, 2, DEC])
    vs = sb("vs", [P, DEC])
    os_t = sb("os_t", [P, DEC])
    heads_end = cursor[0]
    cursor[0] = max(heads_end, sb_at["e_buf"][1])
    p_in = sb("p_in", [P, PT, R])
    assert sb_at["sprod"][1] <= sb_at["vbd"][1]

    def sm(name, at, n):
        return small[:, at:at + n]

    st, rs = sm("st", 0, 3), sm("rs", 4, 3)
    rx3, r2 = sm("rx3", 8, 3), sm("r2", 12, 2)
    kk = small[:, 16:32].rearrange("p (h c) -> p h c", c=2)
    gi = small[:, 32:56].rearrange("p (h c) -> p h c", c=3)
    g2 = small[:, 56:80].rearrange("p (h c) -> p h c", c=3)
    rs8 = small[:, 80:96].rearrange("p (a b) -> p a b", a=2)
    bn = sm("bn", 96, 18)
    mv = small[:, 116:122].rearrange("p (c s) -> p c s", s=2)
    var_t, rs_t, sc_t, nb_t = (small[:, 124 + 4 * i:127 + 4 * i] for i in range(4))
    minus_half = sm("minus_half", 140, 3)
    mean_sc = sm("mean_sc", 144, 3)
    eps3, zero3 = sm("eps3", 148, 3), sm("zero3", 152, 3)
    held = sm("held", 156, 1)

    ps = [nc.alloc_psum_tensor(f"ps{i}", [P, 512], F32) for i in range(8)]
    accum = ps[0:2]
    ps_tr, ps_st, ps_p, ps_o, ps_s0, ps_s1 = ps[2:8]

    first_banks = [*accum, ps_o, accum[1]]

    ident = cst[:, K_ID:K_ID + P]
    tri = cst[:, K_TRI:K_TRI + P]

    s = Signals(nc)
    raw_in = [nc.alloc_semaphore("raw_even_in"), nc.alloc_semaphore("raw_odd_in")]
    acc_free = [nc.alloc_semaphore("acc_even_free"), nc.alloc_semaphore("acc_odd_free")]

    ST_X, ST_LN, ST_M, ST_E = range(4)

    def stat_at(l, k):
        return 4 * l + k + 1

    def spread_at(l, k):
        return 3 * l + {ST_X: 1, ST_M: 2, ST_E: 3}[k]

    def squares_at(l):
        return 4 + 3 * KT * l

    def vec(l, at, n=1):
        return vecs[:, l, bass.ds(at, n)]

    def wide(ap, shape):
        return ap.unsqueeze(1).to_broadcast(shape)

    def rows(t, tile, n=1):
        return t[:, :, :].rearrange("p k r -> p (k r)")[:, bass.ds(tile * R, n * R)]

    block = ctx.enter_context(nc.Block())

    @block.sync
    def _(sp):
        def load(l, slab, j, src, first_row, cols=SLAB, first=False):
            if not first:
                sp.wait_ge(s.lo_ready, slab + (SLABS * l - 1))
            sp.dma_start(raw[:, j % RAW, 0:cols], src[bass.ds(first_row, P), :]).then_inc(raw_in[j % RAW], 16)

        def load_x(g):
            sp.dma_start(x[:, 4 * g:4 * g + 4, :], x_t[:, 4 * g:4 * g + 4, :]).then_inc(s.x_in[g], 16)

        for l in range(DEPTH):
            in_row = 56 * l
            for j in range(4):
                for g in {(0, 0): (0,), (0, 1): (1, 2, 3)}.get((l, j), ()):
                    load_x(g)
                load(l, S_C + j, j, w_in, P * (in_row + (40, 32)[j % 2] + j // 2), first=l == 0 and j < RAW)
            with sp.Fori(1, 4) as i:
                for j in range(4):
                    load(l, 4 * i + (S_C + j), j, w_in, P * (2 * i + (in_row + (40, 32)[j % 2] + j // 2)))
            with sp.Fori(0, HEADS) as h:
                for j in range(4):
                    load(l, 4 * h + (S_H + j), j, w_in, P * (h + (in_row + HEADS * j)))
            with sp.Fori(0, 2) as i:
                for j in range(4):
                    load(l, 4 * i + (S_G + j), j, w_in, P * (4 * i + (in_row + 48 + j)))
            for j in range(4):
                load(l, S_W + j, j, w_pw, P * (4 * l + j))
            with sp.Fori(0, 3) as i:
                for j in range(4):
                    load(l, 4 * i + (S_O + j), j, w_out, P * (4 * i + (16 * l + j)))
            for j in range(4):
                load(l, S_OP + 2 * j, 2 * j, w_out, P * (16 * l + 12 + j))
                load(l, S_OP + 2 * j + 1, 2 * j + 1, w_ple, P * (4 * l + j), 4 * PT * P)
            with sp.Fori(0, 4) as i:
                for j in range(4):
                    load(l, 4 * i + (S_T + j), j, w_gate, P * (4 * i + (16 * l + j)))
        for i in range(4):
            sp.wait_ge(s.xnew, KT * (DEPTH - 1) + 4 * i + 4)
            sp.dma_start(y_t[:, 4 * i:4 * i + 4, :], x[:, 4 * i:4 * i + 4, :]).then_inc(s.y_out, 16)
        sp.wait_ge(s.state_out, 16 * HEADS * DEPTH)
        sp.wait_ge(s.sprompt_out, 16 * HEADS * DEPTH + 1)
        sp.wait_ge(s.scp_out, 16 * DEPTH)
        sp.wait_ge(s.scs_out, 16 * DEPTH)
        sp.wait_ge(s.y_out, 16 * 4)

    @block.tensor
    def _(pe):
        def gemm(l, pair, bank, slab, slot, at, k_tiles, operands, k_wait=None, among={}, fresh=True):
            pe.wait_ge(acc_free[bank], bank_free_at(l, pair))
            if fresh:
                pe.wait_ge(s.lo_ready, slab + (SLABS * l + 1))
            for k in range(k_tiles):
                if k_wait:
                    k_wait(k)
                if k in among:
                    among[k]()
                w = at + P * k
                hi, lo = operands(k)
                pe.matmul(accum[bank][:, 0:R], whi[:, slot, w:w + P], hi, start=k == 0, stop=False)
                pe.matmul(accum[bank][:, 0:R], whi[:, slot, w:w + P], lo, start=False, stop=False)
                mm = pe.matmul(accum[bank][:, 0:R], wlo[:, slot, w:w + P], hi, start=False, stop=k == k_tiles - 1)
            mm.then_inc(s.tile_done, 1)

        in_a = lambda k: (a_hi[:, k, :], a_lo[:, k, :])
        in_b = lambda k: (b_hi[:, k, :], b_lo[:, k, :])
        in_c = lambda k: (c_hi[:, k, :], c_lo[:, k, :])
        mixed = lambda k: in_b(k) if k < HEADS else in_a(k - HEADS)
        in_p = lambda k: in_a(CT + k)

        def stat_sum(l, k, *bufs):
            for c, (r0, r1) in enumerate(((0, P), (P, 2 * P), (2 * P, R))):
                for buf in bufs:
                    mm = pe.matmul(ps_p[0:r1 - r0, c:c + 1], buf[:, r0:r1], ones[:, 0:1], start=buf is bufs[0],
                                   stop=buf is bufs[-1])
            mm.then_inc(s.sum_done, 1)

        def stat_bcast(l, k):
            pe.wait_ge(s.diag_ready, stat_at(l, k))
            pe.matmul(ps_p[:, 0:P], ones[:, :], diag[:, 0:P], start=True, stop=True)
            pe.matmul(ps_p[:, P:2 * P], ones[:, :], diag[:, P:2 * P], start=True, stop=True)
            pe.matmul(ps_p[:, 2 * P:R], ones[0:DEC, :], diag[0:DEC, 2 * P:R], start=True,
                      stop=True).then_inc(s.bcast_done, 1)

        def ret_scores(l, h):
            n = h + HEADS * l
            pe.wait_ge(s.stack_in, n + 1)
            pe.transpose(ps_tr[:, 0:P], vt[:, 0:P], ident)
            pe.transpose(ps_tr[:, P:2 * P], vt[:, P:2 * P], ident)
            pe.transpose(ps_tr[:, 2 * P:3 * P], qk[:, 1, 0:P], ident)
            pe.transpose(ps_tr[:, 3 * P:4 * P], qk[:, 1, P:2 * P], ident)
            cols = stack_cols[:, :, :, :].rearrange("p a b c -> p (a b c)").bitcast(F32)
            pe.transpose(ps_st[0:32, 0:P], cols[:, 0:32], ident)
            pe.transpose(ps_st[0:32, P:2 * P], cols[:, 32:64], ident)
            pe.matmul(ps_p[:, 0:2 * P], qk[:, 1, 0:P], qk[:, 0, 0:2 * P], start=True, stop=True)
            pe.matmul(ps_p[:, 2 * P:3 * P], qk[:, 1, P:2 * P], qk[:, 0, P:2 * P], start=True,
                      stop=True).then_inc(s.scores_done, 1)

        def ret_values(l, h):
            n = h + HEADS * l
            pe.wait_ge(s.rows_ready, n + 1)
            pe.wait_ge(s.p_ready, n + 1)
            pe.matmul(ps_o[:, 0:P], pmat[:, 0:P], vrow[:, 0:P], start=True, stop=True)
            pe.matmul(ps_o[:, P:2 * P], pmat[:, P:2 * P], vrow[:, 0:P], start=True, stop=False)
            pe.matmul(ps_o[:, P:2 * P], pmat[:, 2 * P:3 * P], vrow[:, P:2 * P], start=False, stop=True)
            pe.matmul(ps_tr[:, 0:P], krow[:, 0:P], vrow[:, 0:P], start=True, stop=False)
            pe.matmul(ps_tr[:, 0:P], krow[:, P:2 * P], vrow[:, P:2 * P], start=False, stop=True)
            pe.wait_ge(s.vbd_ready, n + 1)
            pe.wait_ge(s.rt_ready, n + 1)
            blocks = vbd[:, :, :].rearrange("p b v -> p (b v)")
            pe.matmul(ps_s0[:, :], stack[:, 0:P], blocks[:, 0:4 * P], start=True, stop=True)
            pe.matmul(ps_s1[:, :], stack[:, 0:P], blocks[:, 4 * P:8 * P], start=True,
                      stop=True).then_inc(s.values_done, 1)

        def ret_samples(l, h):
            pe.wait_ge(s.snew_ready, h + (HEADS * l + 1))
            for b in range(DEC):
                mm = pe.matmul(ps_st[:, 2 * P + b:2 * P + b + 1], s_new[:, b * P:(b + 1) * P], qks[:, 0, b:b + 1],
                               start=True, stop=True)
            mm.then_inc(s.sample_out_done, 1)

        def ret_sample_rows(l, h):
            pe.wait_ge(s.os_ready, h + (HEADS * l + 1))
            pe.transpose(ps_st[0:DEC, 3 * P:4 * P], os_t[:, :], ident).then_inc(s.sample_rows_done, 1)

        def ret_turn(l, h):
            pe.wait_ge(s.og_ready, h + (HEADS * l + 1))
            pe.transpose(ps_s0[:, 0:P], og[:, 0, :], ident)
            pe.transpose(ps_s0[:, P:2 * P], og[:, 1, :], ident)
            pe.transpose(ps_s0[:, 2 * P:R], og[0:DEC, 2, :], cst[0:DEC, K_ID:K_ID + DEC]).then_inc(s.turn_done, 1)

        def three_tiles(l, tile, slab, operands, k_wait, behind):
            for g, t in ((0, 0), (0, 1), (1, 0), (1, 1), (0, 2), (1, 2), (2, 0), (2, 1), (2, 2), (3, 0), (3, 1),
                         (3, 2)):
                if g == 0:
                    pe.wait_ge(acc_free[t % 2], bank_free_at(l, tile // 2))
                    pe.wait_ge(s.lo_ready, slab + (SLABS * l + t + 1))
                for k in range(4 * g, 4 * g + 4):
                    if t == 0:
                        k_wait(k)
                    w, out = slice(P * k, P * k + P), first_banks[t][:, 0:R]
                    hi, lo = operands(k)
                    pe.matmul(out, whi[:, t, w], hi, start=k == 0, stop=False)
                    pe.matmul(out, whi[:, t, w], lo, start=False, stop=False)
                    mm = pe.matmul(out, wlo[:, t, w], hi, start=False, stop=k == KT - 1)
                if g == 3:
                    mm.then_inc(s.tile_done, 1)
                if t == 2 and g in behind:
                    behind[g]()

        def head(l, h, prev, turn):
            for j in range(4):
                among = {}
                if turn and j == 0:
                    among = {15: lambda: ret_turn(l, h - 2)}
                if prev and j == 3:
                    among = {6: lambda: ret_sample_rows(l, h - 1)}
                gemm(l, 2 * h + (T_H // 2 + j // 2), j % 2, 4 * h + (S_H + j), j, 0, KT, in_a, among=among)
                if prev and j < 3:
                    (ret_scores, ret_values, ret_samples)[j](l, h - 1)

        def sum_x():
            pe.wait_ge(s.sq_used, squares_at(l))
            if l:
                stat_sum(l, ST_X, acc[3 * l % 2])
            else:
                stat_sum(l, ST_X, *(e_buf[:, k, :] for k in range(4)))

        for l in range(DEPTH):
            if l == 0:
                pe.wait_ge(s.consts_set, 1)
            for j in range(4):
                gemm(l, j // 2, j % 2, S_C + j, j, 0, KT, in_a,
                     k_wait=(lambda k: pe.wait_ge(s.xin_ready, KT * l + k + 1)) if j == 0 else None,
                     among={4: sum_x, 14: lambda: stat_bcast(l,
                             ST_X)} if j == 1 and l else {13: sum_x} if j == 1 else {})
                if j == 1 and l == 0:
                    stat_bcast(l, ST_X)
            with pe.Fori(1, 4) as i:
                for j in range(4):
                    gemm(l, 2 * i + j // 2, j % 2, 4 * i + (S_C + j), j, 0, KT, in_a)
            pe.wait_ge(s.consts_in, 16)
            head(l, 0, False, False)
            head(l, 1, True, False)
            with pe.Fori(2, HEADS) as h:
                head(l, h, True, True)
            def mean_over_channels():
                pe.wait_ge(s.ln_summed, 2 * l + 1)
                pe.wait_ge(s.p_ready, HEADS * (l + 1))
                pe.matmul(ps_p[:, 0:R], ones_mean[:, :], acc[(3 * l + 1) % 2][:, :], start=True,
                          stop=True).then_inc(s.mean_done, 1)

            def variance_sum():
                pe.wait_ge(s.ln_centered, l + 1)
                pe.wait_ge(s.ln_summed, 2 * l + 2)
                stat_sum(l, ST_LN, acc[3 * l % 2])

            def variance_bcast():
                pe.wait_ge(s.stat_scaled, stat_at(l, ST_LN))
                stat_bcast(l, ST_LN)

            among = {0: {15: lambda: ret_turn(l, 6)}, 1: {9: mean_over_channels},
                     3: {1: variance_sum, 6: lambda: ret_sample_rows(l, 7)}, 4: {5: variance_bcast,
                             15: lambda: ret_turn(l, 7)}}
            for t in range(CT):
                gemm(l, (T_G + t) // 2, t % 2, S_G + t, t % 4, 0, KT, in_a, among=among.get(t, {}))
                if t < 3:
                    (ret_scores, ret_values, ret_samples)[t](l, 7)
            for j in range(4):
                for e in range(2):
                    gemm(l, (T_W + 2 * j) // 2, e % 2, S_W + j, j, e * CT * P, CT, in_c, fresh=e == 0,
                         k_wait=(lambda k: pe.wait_ge(s.c_ready,
                                                      3 * l + (1, 1, 2, 2, 3, 3, 3,
                                                              3)[k])) if j == 0 and e == 0 else None)
            pe.wait_ge(s.ln_scaled, 2 * l + 2)
            for j in range(4):
                gemm(l, T_O // 2 + j // 2, j % 2, S_O + j, j, 0, KT, mixed,
                     k_wait=(lambda k: pe.wait_ge(s.ret_ready, HEADS * l + k + 2) if k < HEADS
                             else pe.wait_ge(s.cout_ready, CT * l + k - HEADS + 1)) if j == 0 else None)
            with pe.Fori(1, 3) as i:
                for j in range(4):
                    gemm(l, 2 * i + (T_O // 2 + j // 2), j % 2, 4 * i + (S_O + j), j, 0, KT, mixed)
            pe.wait_ge(s.pin_ready, l + 1)
            for n, (kind, _, slab, e) in enumerate(out_and_ple()):
                if kind == "m":
                    gemm(l, (T_OP + n) // 2, n % 2, S_OP + slab, slab % 4, 0, KT, mixed)
                else:
                    gemm(l, (T_OP + n) // 2, n % 2, S_OP + slab, slab % 4, e * PT * P, PT, in_p, fresh=e == 0)
                if T_OP + n == T_O + M_DONE + 1:
                    pe.wait_ge(s.sq_used, squares_at(l) + M_DONE)
                    stat_sum(l, ST_M, acc[(3 * l + 1) % 2])
            stat_bcast(l, ST_M)

            def sum_e():
                pe.wait_ge(s.sq_used, squares_at(l) + E_DONE)
                pe.wait_ge(s.bcast_read, spread_at(l, ST_M))
                stat_sum(l, ST_E, acc[3 * l % 2])

            three_tiles(l, T_T, S_T, in_b, lambda k: pe.wait_ge(s.h_ready, 4 * l + k // 4 + 1),
                        {0: sum_e, 3: lambda: stat_bcast(l, ST_E)})
            gemm(l, T_T // 2 + 1, 1, S_T + 3, 3, 0, KT, in_b)
            with pe.Fori(1, 4) as i:
                for j in range(4):
                    gemm(l, 2 * i + (T_T // 2 + j // 2), j % 2, 4 * i + (S_T + j), j, 0, KT, in_b)
            pe.wait_ge(s.bcast_read, spread_at(l, ST_E))

    @block.scalar
    def _(act):
        def next_hi(l, body, slot, tile, cols=SLAB):
            act.wait_ge(raw_in[slot % RAW], body * 32 + 16 * (SLABS // 2 * l + 3 + slot // 2))
            act.wait_ge(s.tile_done, tile_done_at(l, tile))
            nc.scalar.activation(whi[:, slot, 0:cols], raw[:, slot % RAW, 0:cols], ACT.Copy).then_inc(s.hi_ready, 1)

        def square(n, side, src):
            act.wait_ge(s.sq_used, n - 1)
            nc.scalar.activation(sq[:, side, :], src, ACT.Square).then_inc(s.sq_ready, 1)

        def conv_in(l, i):
            for j in range(4):
                ct = 2 * i + j // 2
                if j % 2 == 0:
                    act.wait_ge(acc_free[0], read_out_at(l, ct))
                    nc.scalar.activation(tmp[2][:, :], tmp[0][:, :], ACT.Tanh, scale=0.5).then_inc(s.tanh_ready, 1)
                    next_hi(l, i, j, 4 * i + j)
                else:
                    next_hi(l, i, j, 4 * i + j)
                    act.wait_ge(s.u_ready, ct + (CT * l + 1))
                    ust_flat = ust[:, :, :, :].rearrange("p c k b -> p (c k b)")
                    nc.scalar.activation(ust_flat[:, bass.ds(ct * (TAPS * DEC) + PAD * DEC, DEC)],
                                         u_flat[:, bass.ds(ct * UW + PAD + SEQ,
                                                           DEC)], ACT.Copy).then_inc(s.ust_ready, 1)

        def ret_rows(l, h):
            kcol = lambda chunk: small[:, bass.ds((h - 1) * 2 + (16 + chunk), 1)]
            act.wait_ge(s.scores_done, h + HEADS * l)
            nc.scalar.activation(vrow[:, :], ps_tr[:, 0:2 * P], ACT.Copy)
            nc.scalar.activation(krow[:, 0:P], ps_tr[:, 2 * P:3 * P], ACT.Copy, scale=kcol(0))
            nc.scalar.activation(krow[:, P:2 * P], ps_tr[:, 3 * P:4 * P], ACT.Copy, scale=kcol(1))
            nc.scalar.activation(stack[:, :], ps_st[0:32, 0:P], ACT.Copy).then_inc(s.rows_ready, 1)
            for b in range(DEC):
                block_of_b = nc.scalar.activation(vbd[:, b, :], ps_st[0:32, P:2 * P], ACT.Copy,
                                                  scale=cst[0:32, K_MASK + b:K_MASK + b + 1])
            block_of_b.then_inc(s.vbd_ready, 1)

        def ret_prompt_state(l, h):
            n = h + HEADS * l
            act.wait_ge(s.values_done, n)
            act.wait_ge(s.sprompt_out, 16 * n - 15)
            nc.scalar.activation(s_prompt[:, :], ps_tr[:, 0:P], ACT.Copy,
                                 scale=cst[:, bass.ds((h - 1) + K_END, 1)]).then_inc(s.sprompt_ready, 1)
            act.wait_ge(s.sprompt_ready, n)
            act.dma_start(sp_out[bass.ds(n * P - P, P), :], s_prompt[:, :]).then_inc(s.sprompt_out, 16)

        def gate_silu(l, h):
            n = h + HEADS * l
            act.wait_ge(acc_free[1], read_out_at(l, 2 * h + (T_H // 2 - 1)))
            act.wait_ge(s.rt_ready, n)
            nc.scalar.activation(sg[:, :], gz[:, :], ACT.Silu).then_inc(s.sg_ready, 1)

        def head(l, h, prev, turn):
            n = h + HEADS * l
            if turn:
                ret_normalise(l, h - 1)
            act.wait_ge(s.tile_done, tile_done_at(l, 4 * h + T_H))
            if prev or l:
                act.wait_ge(s.rope_done, n)
            nc.scalar.activation(zs[:, 0, :], accum[0][:, 0:R], ACT.Copy)
            nc.scalar.activation(zw[0:64, 0, :], accum[0][64:P, 0:R], ACT.Copy)
            nc.scalar.activation(zw[64:P, 0, :], accum[0][0:64, 0:R], ACT.Copy).then_inc(acc_free[0], 1)
            if prev:
                ret_rows(l, h)
            next_hi(l, 4 + h, 0, 4 * h + T_H)
            act.wait_ge(s.tile_done, tile_done_at(l, 4 * h + (T_H + 1)))
            nc.scalar.activation(zs[:, 1, :], accum[1][:, 0:R], ACT.Copy)
            nc.scalar.activation(zw[0:64, 1, :], accum[1][64:P, 0:R], ACT.Copy)
            nc.scalar.activation(zw[64:P, 1, :], accum[1][0:64, 0:R], ACT.Copy).then_inc(acc_free[1], 1)
            if prev:
                ret_prompt_state(l, h)
            if turn:
                ret_round(l, h - 1)
            if prev:
                gate_silu(l, h)
            next_hi(l, 4 + h, 1, 4 * h + (T_H + 1))
            act.wait_ge(s.tile_done, tile_done_at(l, 4 * h + (T_H + 2)))
            nc.scalar.activation(vt[:, :], accum[0][:, 0:R], ACT.Copy).then_inc(acc_free[0], 1)
            if prev:
                ret_samples_out(l, h)
            act.wait_ge(s.kv_ready, n + 1)
            nc.scalar.activation(stack_cols[:, 0, 0:2, :], wide(qks[:, 1, :], [P, 2, DEC]), ACT.Copy)
            nc.scalar.activation(stack_cols[:, 1, 0:4:2, :], wide(vs[:, :], [P, 2, DEC]),
                                 ACT.Copy).then_inc(s.stack_hi_ready, 1)
            next_hi(l, 4 + h, 2, 4 * h + (T_H + 2))
            next_hi(l, 4 + h, 3, 4 * h + (T_H + 3))
            if prev:
                state_in(l, h)

        def state_in(l, h):
            n = h + HEADS * l
            act.wait_ge(s.sample_out_done, n)
            act.wait_ge(s.state_out, 16 * n)
            act.dma_start(s_new[:, :], s_ret[bass.ds(n * P, P), :]).then_inc(s.state_in, 16)

        def ret_samples_out(l, h):
            n = h + HEADS * l
            act.wait_ge(s.sample_out_done, n)
            nc.scalar.activation(os_t[:, :], ps_st[:, 2 * P:2 * P + DEC], ACT.Copy).then_inc(s.os_ready, 1)
            act.dma_start(ss_out[bass.ds(n * P - P, P), :], s_new[:, :]).then_inc(s.state_out, 16)

        def ret_normalise(l, h):
            act.wait_ge(s.ret_rs, h + HEADS * l)
            for chunk in range(2):
                nc.scalar.activation(og[:, chunk, :], ps_o[:, chunk * P:(chunk + 1) * P], ACT.Identity,
                                     bias=nb_t[:, chunk:chunk + 1], scale=sc_t[:, chunk:chunk + 1])
            nc.scalar.activation(og[0:DEC, 2, :], ps_st[0:DEC, 3 * P:4 * P], ACT.Identity,
                                 bias=nb_t[0:DEC, 2:3], scale=sc_t[0:DEC, 2:3]).then_inc(s.og_ready, 1)

        def ret_round(l, h):
            act.wait_ge(s.rt_ready, h + (HEADS * l + 1))
            nc.scalar.activation(rows(b_hi, h - 1), rt[:, :], ACT.Copy).then_inc(s.rhi_ready, 1)

        def channel_silu(l, c):
            act.wait_ge(s.ln_scaled, 2 * l + 1 + c // 4)
            nc.scalar.activation(c_buf[:, c, :], c_buf[:, c, :], ACT.Silu, bias=vec(l, V_BCN + c),
                                 scale=vec(l, V_GCN + c)).then_inc(s.silu_ready, 1)

        u_flat = u_buf[:, :, :].rearrange("p c r -> p (c r)")
        act.dma_start(vecs[:, :, :], vecs_d).then_inc(s.vecs_in, 16)
        act.dma_start(cst[:, :], consts_d).then_inc(s.consts_in, 16)

        def first_hi(j):
            act.wait_ge(raw_in[j % RAW], 16 * (j // RAW + 1))
            nc.scalar.activation(whi[:, j, :], raw[:, j % RAW, :], ACT.Copy).then_inc(s.hi_ready, 1)

        act.wait_ge(s.vecs_in, 16)
        for g in range(4):
            act.wait_ge(s.x_in[g], 16)
            for k in range(4 * g, 4 * g + 4):
                nc.scalar.activation(a_hi[:, k, :], x[:, k, :], ACT.Copy,
                                     scale=vec(0, V_PRE + k)).then_inc(s.xhi_ready, 1)
            if g == 0:
                first_hi(0)
        first_hi(1)
        for g in range(4):
            nc.scalar.activation(e_buf[:, 4 * g:4 * g + 4, :], x[:, 4 * g:4 * g + 4, :],
                                 ACT.Square).then_inc(s.sq_ready, 1)
        first_hi(2)
        first_hi(3)

        for l in range(DEPTH):
            last = l == DEPTH - 1
            if l:
                act.wait_ge(s.xnew, KT * l)
            else:
                act.wait_ge(s.sum_done, 1)
            act.dma_start(ust[:, :, 0:PAD, :], s_conv[P * l:P * l + P, :].rearrange("p (c k b) -> p c k b", c=CT,
                    k=PAD)).then_inc(s.convstate_in, 16)
            with act.Fori(0, 4) as i:
                conv_in(l, i)
            act.wait_ge(s.ust_ready, CT * (l + 1))
            act.wait_ge(s.convstate_in, 16 * (l + 1))
            act.dma_start(scp_out[l, :, :, :], u_buf[:, :, SEQ:SEQ + PAD]).then_inc(s.scp_out, 16)
            act.dma_start(scs_out[P * l:P * l + P, :].rearrange("p (c k b) -> p c k b", c=CT, k=PAD),
                          ust[:, :, 1:TAPS, :]).then_inc(s.scs_out, 16)
            if l:
                act.wait_ge(s.pin_ready, l)
            act.dma_start(p_in[:, :, :], p_t[l, :, :, :]).then_inc(s.p_in, 16)
            head(l, 0, False, False)
            act.wait_ge(s.scs_out, 16 * (l + 1))
            act.wait_ge(s.sconv_step, 5 * (l + 1))
            act.dma_start(s_new[:, :], s_ret[HEADS * l * P:(HEADS * l + 1) * P, :]).then_inc(s.state_in, 16)
            head(l, 1, True, False)
            with act.Fori(2, HEADS) as h:
                head(l, h, True, True)
            for t in range(CT):
                if t == 0:
                    ret_normalise(l, 7)
                if t == 4:
                    ret_normalise(l, 8)
                if t == 2:
                    ret_samples_out(l, 8)
                act.wait_ge(acc_free[t % 2], read_out_at(l, (T_G + t) // 2))
                nc.scalar.activation(gc_buf[:, t, :], tmp[t % 2][:, :], ACT.Silu).then_inc(s.gc_ready, 1)
                if t == 0:
                    ret_rows(l, 8)
                    ret_round(l, 7)
                if t == 1:
                    act.wait_ge(s.ln_centered, l + 1)
                    act.wait_ge(s.scp_out, 16 * (l + 1))
                    nc.scalar.activation(ln_sq[:, :, :], c_buf[:, :, :], ACT.Square).then_inc(s.ln_squared, 1)
                if t == 1:
                    ret_prompt_state(l, 8)
                    gate_silu(l, 8)
                if t == 5:
                    ret_round(l, 8)
                next_hi(l, 12 + t // 4, t % 4, T_G + t)
                for part, c0, c1 in {4: ((0, 0, 2), (1, 2, 4)), 5: ((2, 4, 8),)}.get(t, ()):
                    for c in range(c0, c1):
                        channel_silu(l, c)
                    act.wait_ge(s.silu_ready, CT * l + c1)
                    nc.scalar.activation(c_hi[:, c0:c1, :], c_buf[:, c0:c1, :], ACT.Copy).then_inc(s.chi_ready, 1)
            act.wait_ge(s.tile_done, tile_done_at(l, T_W - 1))
            act.wait_ge(s.p_in, 16 * (l + 1))
            nc.scalar.activation(a_hi[:, CT:CT + PT, :], p_in[:, :, :], ACT.Copy).then_inc(s.phi_ready, 1)
            for j in range(4):
                for e in range(2):
                    act.wait_ge(acc_free[e], read_out_at(l, T_W // 2 + j))
                    nc.scalar.activation(a_hi[:, 2 * j + e, :], gc_buf[:, 2 * j + e, :],
                                         ACT.Copy).then_inc(s.cohi_ready, 1)
                next_hi(l, 14, j, T_W + 2 * j + 1)
            act.wait_ge(s.state_out, 16 * HEADS * (l + 1))
            act.wait_ge(s.sprompt_out, 16 * HEADS * (l + 1) + 1)

            def tile_out(n, side, dst, gain):
                act.wait_ge(s.tile_done, tile_done_at(l, n + T_O))
                square(n + squares_at(l), side, accum[side][:, 0:R])
                nc.scalar.activation(dst, accum[side][:, 0:R], ACT.Copy, scale=vec(l, gain)).then_inc(acc_free[side], 1)

            def out_body(i, cols=(SLAB,) * 4):
                for j in range(4):
                    tile_out(4 * i + j, j % 2, rows(m_buf, 4 * i + j), 4 * i + (V_POST + j))
                    next_hi(l, 15 + i, j, 4 * i + (T_O + j), cols[j])

            out_cols = (SLAB, 4 * PT * P, SLAB, 4 * PT * P)
            with act.Fori(0, 2) as i:
                out_body(i)
            out_body(2, out_cols)
            for n, (kind, tile, slab, e) in enumerate(out_and_ple(), T_OP - T_O):
                if kind == "m":
                    tile_out(n, n % 2, m_buf[:, tile, :], V_POST + tile)
                else:
                    tile_out(n, n % 2, e_buf[:, tile, :], V_PLE + tile)
                if kind == "e" and e == 3:
                    for j in (slab - 1, slab) if slab < 7 else (slab - 1,):
                        next_hi(l, 18 + j // 4, j % 4, T_O + n, out_cols[j] if j < 4 else SLAB)
            for g in range(4):
                act.wait_ge(s.h_step, 8 * l + (2, 4, 6, 8)[g])
                nc.scalar.activation(b_hi[:, 4 * g:4 * g + 4, :], x[:, 4 * g:4 * g + 4, :],
                                     ACT.Copy).then_inc(s.hhi_ready, 1)
                if g == 1:
                    next_hi(l, 19, 3, T_T - 1)

            def gate_tanh(i, j, bank):
                t = 4 * i + j
                act.wait_ge(s.tile_done, tile_done_at(l, t + T_T))
                if not isinstance(i, int) or t >= 2:
                    act.wait_ge(s.xnew, t + (KT * l - 1))
                nc.scalar.activation(tmp[j % 2][:, :], bank[:, 0:R], ACT.Tanh, scale=0.5).then_inc(acc_free[j % 2], 1)

            def next_x(t, side):
                act.wait_ge(s.xnew, t + (KT * l + 1))
                act.wait_ge(s.sq_used, t + (squares_at(l) + 2 * KT - 1))
                nc.scalar.activation(rows(a_hi, t), rows(x, t), ACT.Copy,
                                     scale=vec(l + 1, t + V_PRE)).then_inc(s.xhi_ready, 1)
                nc.scalar.activation(sq[:, side, :], rows(x, t), ACT.Square).then_inc(s.sq_ready, 1)

            for j in range(4):
                gate_tanh(0, j, first_banks[j])
                if j >= 2 and not last:
                    next_x(j - 2, j % 2)
                next_hi(l, 20, j, j + T_T)
            with act.Fori(1, 3) as i:
                for j in range(4):
                    gate_tanh(i, j, accum[j % 2])
                    if not last:
                        next_x(4 * i + (j - 2), j % 2)
                    next_hi(l, 20 + i, j, 4 * i + (j + T_T))
            for j in range(4):
                gate_tanh(3, j, accum[j % 2])
                if not last:
                    next_x(10 + j, j % 2)
                if j < 2 and not last:
                    next_hi(l, 23, j, 12 + j + T_T)
            if not last:
                next_x(14, 0)
                next_x(15, 1)
                next_hi(l, 23, 2, 14 + T_T)
                next_hi(l, 23, 3, 15 + T_T)

    @block.vector
    def _(dve):
        v = nc.vector
        dw = lambda l, at: vecs[:, l, bass.ds(at + V_DW, 1)]

        def lo(l, body, slot, cols=SLAB):
            dve.wait_ge(s.hi_ready, body * 4 + (SLABS * l + slot + 1))
            v.tensor_tensor(wlo[:, slot, 0:cols], raw[:, slot % RAW, 0:cols], whi[:, slot, 0:cols].bitcast(F32),
                            ALU.subtract).then_inc(s.lo_ready, 1)

        def x_lo(l, t):
            dve.wait_ge(s.xhi_ready, t + (KT * l + 1))
            v.scalar_tensor_tensor(rows(a_lo, t), rows(x, t), vec(l, t + V_PRE), rows(a_hi, t).bitcast(F32),
                                   ALU.mult, ALU.subtract).then_inc(s.xin_ready, 1)

        def stat_scale(l, k, width):
            dve.wait_ge(s.sum_done, stat_at(l, k))
            v.tensor_scalar(st[:, 0:2], ps_p[:, 0:2], 1.0 / width, EPS, ALU.mult, ALU.add)
            v.tensor_scalar(st[0:DEC, 2:3], ps_p[0:DEC, 2:3], 1.0 / width, EPS, ALU.mult,
                            ALU.add).then_inc(s.stat_scaled, 1)

        def stat_diag(l, k):
            dve.wait_ge(s.stat_rs, stat_at(l, k))
            v.tensor_scalar(diag[:, 0:P], ident, rs[:, 0:1], None, ALU.mult)
            v.tensor_scalar(diag[:, P:2 * P], ident, rs[:, 1:2], None, ALU.mult)
            v.tensor_scalar(diag[0:DEC, 2 * P:R], cst[0:DEC, K_ID:K_ID + DEC], rs[0:DEC, 2:3], None,
                            ALU.mult).then_inc(s.diag_ready, 1)

        def stat_read(l, k, dst, by=1.0):
            dve.wait_ge(s.bcast_done, stat_at(l, k))
            v.tensor_scalar(dst[:, :], ps_p[:, 0:R], by, None, ALU.mult).then_inc(s.bcast_read, 1)

        def factors(l):
            at = 6 * l
            dve.wait_ge(s.bcast_read, spread_at(l, ST_X))
            v.tensor_tensor(r2, rs[:, 0:2], rs[:, 0:2], ALU.mult).then_inc(s.rfac_step, 1)
            v.tensor_copy(rx3[:, 0:2], rs[:, 0:2]).then_inc(s.rfac_step, 1)
            v.tensor_copy(rs8[:, 0, :], r_x[:, SEQ:R]).then_inc(s.rfac_step, 1)
            v.tensor_scalar(rs8[:, 1, :], r_x[:, SEQ:R], P ** -0.5, None, ALU.mult).then_inc(s.rfac_step, 1)
            dve.wait_ge(s.rfac_step, at + 4)
            v.tensor_tensor(kk, cst[:, K_KDEC:K_KDEC + 16].rearrange("p (h c) -> p h c", c=2),
                            wide(r2, [P, HEADS, 2]), ALU.mult)
            v.tensor_tensor(gi, cst[:, K_GI:K_GI + 24].rearrange("p (h c) -> p h c", c=3), wide(rx3, [P, HEADS, 3]),
                            ALU.mult).then_inc(s.rfac_step, 1)
            dve.wait_ge(s.rfac_step, at + 5)
            v.tensor_tensor(g2, gi, gi, ALU.mult).then_inc(s.rfac_step, 1)

        def conv_b(l, ct, first=False):
            dve.wait_ge(s.tile_done, tile_done_at(l, 2 * ct))
            v.tensor_tensor(tmp[0][:, :], accum[0][:, 0:R], r_x[:, :], ALU.mult).then_inc(acc_free[0], 1)

        def conv_a(l, ct, first=False):
            dve.wait_ge(s.tile_done, tile_done_at(l, 2 * ct + 1))
            if not first:
                dve.wait_ge(s.u_ready, ct + CT * l)
            v.scalar_tensor_tensor(tmp[1][:, :], accum[1][:, 0:R], 0.5, r_x[:, :], ALU.mult,
                                   ALU.mult).then_inc(acc_free[1], 1)

        def conv_u(l, ct):
            dve.wait_ge(s.tanh_ready, ct + (CT * l + 1))
            dve.wait_ge(acc_free[1], read_out_at(l, ct))
            v.scalar_tensor_tensor(u_flat[:, bass.ds(ct * UW + PAD, R)], tmp[2][:, :], 1.0, tmp[1][:, :], ALU.add,
                                   ALU.mult).then_inc(s.u_ready, 1)

        def taps(l, done, ct, k0, k1, first, last):
            done = done + TAPS_DONE * l
            even = c_flat[:, bass.ds(ct * R, SEQ)]
            odd = tmp[3][:, 0:SEQ]
            for m in range(first, last):
                src = u_flat[:, bass.ds(ct * UW + (k0 + m), SEQ)]
                w = dw(l, ct * TAPS + (k0 + m))
                if m == 0 and k0 == 0:
                    dve.wait_ge(s.u_ready, ct + (CT * l + 1))
                    v.tensor_scalar(even, src, w, vec(l, ct + V_BDW), ALU.mult, ALU.add).then_inc(s.tap_done, 1)
                elif m == 0:
                    dve.wait_ge(s.tap_done, done)
                    v.scalar_tensor_tensor(even, src, w, even, ALU.mult, ALU.add).then_inc(s.tap_done, 1)
                elif m == 1:
                    dve.wait_ge(s.tap_done, done + 1)
                    v.tensor_scalar(odd, src, w, None, ALU.mult).then_inc(s.tap_done, 1)
                else:
                    out = odd if m % 2 else even
                    dve.wait_ge(s.tap_done, done + (m - 1))
                    v.scalar_tensor_tensor(out, src, w, out, ALU.mult, ALU.add).then_inc(s.tap_done, 1)
            if last == k1 - k0:
                dve.wait_ge(s.tap_done, done + (k1 - k0))
                v.tensor_tensor(even, even, odd, ALU.add).then_inc(s.tap_done, 1)

        def sample_products(l, half):
            if half == 0:
                dve.wait_ge(s.ust_ready, CT * (l + 1))
                dve.wait_ge(s.convstate_in, 16 * (l + 1))
            else:
                dve.wait_ge(s.sconv_step, 5 * l + 2)
            c0, n = half * CT // 2, CT // 2
            w = vecs[:, l, V_DW + c0 * TAPS:V_DW + (c0 + n) * TAPS].rearrange("p (c k) -> p c k",
                    c=n).unsqueeze(2).to_broadcast([P, n, DEC, TAPS])
            v.tensor_tensor(sprod[:, :, :, :], ust[:, c0:c0 + n, :, :].rearrange("p c k b -> p c b k"), w,
                            ALU.mult).then_inc(s.sconv_step, 1)

        def sample_sums(l, half):
            dve.wait_ge(s.sconv_step, 5 * l + 2 * half + 1)
            n = CT // 2 * DEC
            v.tensor_reduce(r_t[:, half * n:half * n + n], sprod[:, :, :, :].rearrange("p c b k -> p (c b) k"), AX.X,
                            ALU.add).then_inc(s.sconv_step, 1)
            if half:
                dve.wait_ge(s.sconv_step, 5 * l + 4)
                bias = vecs[:, l, V_BDW:V_BDW + CT].unsqueeze(2).to_broadcast([P, CT, DEC])
                v.tensor_tensor(c_buf[:, :, SEQ:R], r_t[:, 0:CT * DEC].rearrange("p (c b) -> p c b", c=CT), bias,
                                ALU.add).then_inc(s.sconv_step, 1)

        def ret_scores(l, h):
            dve.wait_ge(s.scores_done, h + HEADS * l)
            kcol = lambda chunk: small[:, bass.ds((h - 1) * 2 + (16 + chunk), 1)]
            v.scalar_tensor_tensor(pmat[:, 0:P], ps_p[:, 0:P], kcol(0), tri, ALU.mult, ALU.mult)
            v.tensor_scalar(pmat[:, P:2 * P], ps_p[:, P:2 * P], kcol(0), None, ALU.mult)
            v.scalar_tensor_tensor(pmat[:, 2 * P:3 * P], ps_p[:, 2 * P:3 * P], kcol(1), tri, ALU.mult,
                                   ALU.mult).then_inc(s.p_ready, 1)

        def ret_state(l, h):
            n = h + HEADS * l
            gamma = cst[:, bass.ds((h - 1) + K_GAM, 1)]
            dve.wait_ge(s.values_done, n)
            dve.wait_ge(s.state_in, 16 * n)
            v.scalar_tensor_tensor(s_new[:, 0:4 * P], s_new[:, 0:4 * P], gamma, ps_s0[:, :], ALU.mult, ALU.add)
            v.scalar_tensor_tensor(s_new[:, 4 * P:8 * P], s_new[:, 4 * P:8 * P], gamma, ps_s1[:, :], ALU.mult,
                                   ALU.add).then_inc(s.snew_ready, 1)
            v.bn_stats(bn[:, 0:6], ps_o[:, 0:P])
            v.bn_stats(bn[:, 6:12], ps_o[:, P:2 * P]).then_inc(s.bn_done, 1)

        def ret_stats(l, h):
            n = h + HEADS * l
            dve.wait_ge(s.sample_rows_done, n)
            v.bn_stats(bn[0:DEC, 12:18], ps_st[0:DEC, 3 * P:4 * P]).then_inc(s.bn_done, 1)
            dve.wait_ge(s.bn_done, 2 * n)
            v.memset(held, 0.0)
            v.bn_aggr(mv[:, 0, :], bn[:, 0:6])
            v.bn_aggr(mv[:, 1, :], bn[:, 6:12])
            v.bn_aggr(mv[0:DEC, 2, :], bn[0:DEC, 12:18]).then_inc(s.stat_ready, 1)

        def ret_gate(l, h):
            n = h + HEADS * l
            dve.wait_ge(s.turn_done, n)
            dve.wait_ge(s.sg_ready, n + 1)
            dve.wait_ge(s.ret_ready, n)
            v.scalar_tensor_tensor(rt[:, :], ps_s0[:, 0:R], vec(l, (h - 1) + V_RET), sg[:, :], ALU.mult,
                                   ALU.mult).then_inc(s.rt_ready, 1)

        def ret_lo(l, h):
            dve.wait_ge(s.rhi_ready, h + HEADS * l)
            v.tensor_tensor(rows(b_lo, h - 1), rt[:, :], rows(b_hi, h - 1).bitcast(F32),
                            ALU.subtract).then_inc(s.ret_ready, 1)

        def head(l, h, prev, turn, beside):
            n = h + HEADS * l
            body = 5 + h
            if turn:
                ret_gate(l, h - 1)
            if prev:
                ret_scores(l, h)
            beside[0]()
            lo(l, body, 0)
            dve.wait_ge(acc_free[1], read_out_at(l, 2 * h + T_H // 2))
            v.tensor_tensor(zs[:, :, :], zs[:, :, :], wide(cst[:, K_COS:K_COS + R], [P, 2, R]),
                            ALU.mult).then_inc(s.rope_step, 1)
            v.tensor_tensor(zw[:, :, :], zw[:, :, :], wide(cst[:, K_SIN:K_SIN + R], [P, 2, R]),
                            ALU.mult).then_inc(s.rope_step, 1)
            if prev:
                ret_state(l, h)
            dve.wait_ge(s.rope_step, 2 * n + 2)
            v.tensor_tensor(qk[:, :, :], zs[:, :, :], zw[:, :, :], ALU.add).then_inc(s.rope_done, 1)
            beside[1]()
            if turn:
                ret_lo(l, h - 1)
            lo(l, body, 1)
            dve.wait_ge(acc_free[0], read_out_at(l, 2 * h + (T_H // 2 + 1)))
            if prev:
                dve.wait_ge(s.sample_out_done, n)
            dve.wait_ge(s.rope_done, n + 1)
            v.tensor_tensor(qks[:, :, :], qk[:, :, SEQ:R], rs8, ALU.mult)
            v.tensor_tensor(vs[:, :], vt[:, SEQ:R], r_x[:, SEQ:R], ALU.mult).then_inc(s.kv_ready, 1)
            beside[2]()
            dve.wait_ge(s.stack_hi_ready, n + 1)
            v.tensor_tensor(stack_cols[:, 0, 2:4, :], wide(qks[:, 1, :], [P, 2, DEC]),
                            stack_cols[:, 0, 0:2, :].bitcast(F32), ALU.subtract)
            v.tensor_tensor(stack_cols[:, 1, 1:4:2, :], wide(vs[:, :], [P, 2, DEC]),
                            stack_cols[:, 1, 0:4:2, :].bitcast(F32), ALU.subtract).then_inc(s.stack_in, 1)
            if prev:
                ret_stats(l, h)
            lo(l, body, 2)
            beside[3]()
            dve.wait_ge(s.tile_done, tile_done_at(l, 4 * h + (T_H + 3)))
            dve.wait_ge(s.sg_ready, n + 1)
            v.tensor_tensor(gz[:, :], accum[1][:, 0:R], r_x[:, :], ALU.mult).then_inc(acc_free[1], 1)
            lo(l, body, 3)

        def parts(l, segments):
            one_by_one = [(seg, m) for seg in segments for m in range(seg[3] - seg[2])]
            count = len(one_by_one)

            def run(j):
                for seg, m in one_by_one[count * j // 4:count * (j + 1) // 4]:
                    taps(l, *seg, m, m + 1)
            return [lambda j=j: run(j) for j in range(4)]

        u_flat = u_buf[:, :, :].rearrange("p c r -> p (c r)")
        c_flat = c_buf[:, :, :].rearrange("p c r -> p (c r)")
        v.memset(small[:, :], 0.0).then_inc(s.small_set, 1)
        dve.wait_ge(s.small_set, 1)
        v.memset(st[:, 2:3], 1.0).then_inc(acc_free[0], 1)
        v.memset(eps3, EPS)
        v.memset(minus_half, -0.5).then_inc(acc_free[1], 1)
        v.memset(rx3[:, 2:3], 1.0).then_inc(s.rt_ready, 1)
        v.memset(ones[:, :], 1.0).then_inc(s.sg_ready, 1)
        v.memset(ones_mean[:, :], 1.0 / CONV).then_inc(s.consts_set, 1)
        v.memset(r_x[:, 0:1], 0.0).then_inc(s.gc_ready, 1)
        v.memset(r_t[:, 0:1], 0.0).then_inc(s.sprompt_out, 1)
        v.memset(r_t[:, 1:2], 0.0).then_inc(s.sq_used, 1)
        v.memset(r_t[:, 2:3], 0.0).then_inc(s.ret_ready, 1)
        dve.wait_ge(s.gc_ready, 1)
        dve.wait_ge(s.vecs_in, 16)
        for g in range(4):
            for k in range(4 * g, 4 * g + 4):
                x_lo(0, k)
            if g == 0:
                lo(0, 0, 0)
        lo(0, 0, 1)
        for g in range(1, 4):
            dve.wait_ge(s.sq_ready, g + 1)
            dve.wait_ge(s.sq_used, g)
            v.tensor_tensor(e_buf[:, 0:4, :], e_buf[:, 0:4, :], e_buf[:, 4 * g:4 * g + 4, :],
                            ALU.add).then_inc(s.sq_used, 1)
        lo(0, 0, 2)
        dve.wait_ge(s.consts_in, 16)

        for l in range(DEPTH):
            last = l == DEPTH - 1
            v.memset(u_buf[:, :, 0:PAD], 0.0).then_inc(s.pad_set, 1)
            dve.wait_ge(s.pad_set, l + 1)
            stat_scale(l, ST_X, D_MODEL)
            stat_diag(l, ST_X)
            stat_read(l, ST_X, r_x)
            dve.wait_ge(s.bcast_read, spread_at(l, ST_X))
            for j in range(4):
                (conv_b, conv_a)[j % 2](l, j // 2, j == 1 and l == 0)
                if j == 0:
                    lo(l, 0, 3)
                lo(l, 1, j)
                if j == 1:
                    factors(l)
                if j % 2:
                    conv_u(l, j // 2)
                if j >= 2:
                    half = CONV_0 // 2
                    taps(l, 0, 0, 0, CONV_0, half * (j - 2), half * (j - 1))
            seen = CONV_C + 1
            with dve.Fori(1, 4) as i:
                beside = parts(l, [((i - 1) * seen + (CONV_0 + 1), i, 0, CONV_C)])
                for j in range(4):
                    (conv_b, conv_a)[j % 2](l, 2 * i + j // 2)
                    beside[j]()
                    lo(l, 1 + i, j)
                    if j % 2:
                        conv_u(l, 2 * i + j // 2)
            at = [CONV_0 + 1 + 3 * seen]

            def segment(ct, k0, k1):
                at[0] += k1 - k0 + 1
                return (at[0] - (k1 - k0 + 1), ct, k0, k1)

            conv_0 = parts(l, [segment(0, CONV_0, CONV_H0)])
            samples = (lambda: sample_products(l, 0), lambda: sample_sums(l, 0),
                       lambda: sample_products(l, 1), lambda: sample_sums(l, 1))
            head(l, 0, False, False, [lambda j=j: (samples[j](), conv_0[j]()) for j in range(4)])
            head(l, 1, True, False, parts(l, [segment(0, CONV_H0, TAPS), segment(1, CONV_C, TAPS),
                                              segment(2, CONV_C, TAPS)]))
            start, stride = at[0], TAPS + CONV_2 + 3
            with dve.Fori(0, 2) as i:
                first = start + i * stride
                head(l, 2 * i + 2, True, True, parts(l, [(first, i + 4, 0, CONV_1)]))
                head(l, 2 * i + 3, True, True, parts(l, [(first + (CONV_1 + 1), i + 4, CONV_1, TAPS),
                                                         (first + (TAPS + 2), i + 6, 0, CONV_2)]))
            at[0] += 2 * stride
            head(l, 6, True, True, parts(l, [segment(3, CONV_C, TAPS), segment(6, CONV_2, CONV_3)]))
            head(l, 7, True, True, parts(l, [segment(6, CONV_3, TAPS), segment(7, CONV_2, TAPS)]))
            assert at[0] == TAPS_DONE

            def channel_sum(src, dst):
                v.tensor_reduce(dst[:, :], src[:, :, :].rearrange("p c r -> p r c"), AX.X,
                                ALU.add).then_inc(s.ln_summed, 1)

            def gate_in(t):
                dve.wait_ge(s.tile_done, tile_done_at(l, T_G + t))
                if t >= 2:
                    dve.wait_ge(s.gc_ready, CT * l + t)
                v.tensor_tensor(tmp[t % 2][:, :], accum[t % 2][:, 0:R], r_x[:, :],
                                ALU.mult).then_inc(acc_free[t % 2], 1)

            ret_gate(l, 7)
            dve.wait_ge(s.tap_done, TAPS_DONE * (l + 1))
            dve.wait_ge(s.sconv_step, 5 * (l + 1))
            channel_sum(c_buf, acc[(3 * l + 1) % 2])
            gate_in(0)
            ret_scores(l, 8)
            dve.wait_ge(s.mean_done, l + 1)
            v.tensor_tensor(c_buf[:, :, :], c_buf[:, :, :], wide(ps_p[:, 0:R], [P, CT, R]),
                            ALU.subtract).then_inc(s.ln_centered, 1)
            lo(l, 13, 0)
            ret_lo(l, 7)
            gate_in(1)
            ret_state(l, 8)
            dve.wait_ge(s.ln_squared, l + 1)
            channel_sum(ln_sq, acc[3 * l % 2])
            lo(l, 13, 1)
            gate_in(2)
            stat_scale(l, ST_LN, CONV)
            lo(l, 13, 2)
            stat_diag(l, ST_LN)
            ret_stats(l, 8)
            gate_in(3)
            lo(l, 13, 3)
            dve.wait_ge(s.bcast_done, stat_at(l, ST_LN))
            for half in range(2):
                part = c_buf[:, 4 * half:4 * half + 4, :]
                v.tensor_tensor(part, part, wide(ps_p[:, 0:R], [P, 4, R]), ALU.mult).then_inc(s.ln_scaled, 1)

            def c_low(part, c0, c1):
                dve.wait_ge(s.chi_ready, 3 * l + part + 1)
                v.tensor_tensor(c_lo[:, c0:c1, :], c_buf[:, c0:c1, :], c_hi[:, c0:c1, :].bitcast(F32),
                                ALU.subtract).then_inc(s.c_ready, 1)

            gate_in(4)
            ret_gate(l, 8)
            lo(l, 14, 0)
            gate_in(5)
            ret_lo(l, 8)
            lo(l, 14, 1)
            gate_in(6)
            c_low(0, 0, 2)
            c_low(1, 2, 4)
            c_low(2, 4, 8)
            lo(l, 14, 2)
            gate_in(7)
            dve.wait_ge(s.gc_ready, CT * (l + 1) + 1)
            for j in range(4):
                for e in range(2):
                    c = 2 * j + e
                    dve.wait_ge(s.tile_done, tile_done_at(l, T_W + c))
                    v.scalar_tensor_tensor(gc_buf[:, c, :], accum[e][:, 0:R], vec(l, V_BPW + c), gc_buf[:, c, :],
                                           ALU.add, ALU.mult).then_inc(acc_free[e], 1)
                    if e == 0 and j:
                        lo(l, 15, j - 1)
                if j == 0:
                    lo(l, 14, 3)
                    dve.wait_ge(s.phi_ready, l + 1)
                    v.tensor_tensor(a_lo[:, CT:CT + PT, :], p_in[:, :, :], a_hi[:, CT:CT + PT, :].bitcast(F32),
                                    ALU.subtract).then_inc(s.pin_ready, 1)
                for e in range(2):
                    c = 2 * j + e
                    dve.wait_ge(s.cohi_ready, CT * l + c + 1)
                    v.tensor_tensor(a_lo[:, c, :], gc_buf[:, c, :], a_hi[:, c, :].bitcast(F32),
                                    ALU.subtract).then_inc(s.cout_ready, 1)
            lo(l, 15, 3)
            with dve.Fori(0, 2) as i:
                for j in range(4):
                    lo(l, 16 + i, j)
            for body in (18, 19):
                for j in range(4):
                    lo(l, body, j, (SLAB, 4 * PT * P)[j % 2])
            lo(l, 20, 0)
            lo(l, 20, 1)
            stat_scale(l, ST_M, D_MODEL)
            stat_diag(l, ST_M)
            stat_read(l, ST_M, r_t)
            dve.wait_ge(s.bcast_read, spread_at(l, ST_M))
            dve.wait_ge(acc_free[1], read_out_at(l, (T_O + M_DONE) // 2 - 1))
            group = lambda t, g: t[:, 4 * g:4 * g + 4, :]

            def scale_m(g):
                v.tensor_tensor(group(m_buf, g), group(m_buf, g), wide(r_t[:, :], [P, 4, R]),
                                ALU.mult).then_inc(s.h_step, 1)

            def add_m(g, behind):
                dve.wait_ge(s.h_step, 8 * l + behind)
                v.tensor_tensor(group(x, g), group(x, g), group(m_buf, g), ALU.add).then_inc(s.h_step, 1)

            def h_lo(g):
                dve.wait_ge(s.hhi_ready, 4 * l + g + 1)
                v.tensor_tensor(group(b_lo, g), group(x, g), group(b_hi, g).bitcast(F32),
                                ALU.subtract).then_inc(s.h_ready, 1)

            scale_m(0)
            add_m(0, 1)
            scale_m(1)
            h_lo(0)
            add_m(1, 3)
            scale_m(2)
            h_lo(1)
            lo(l, 20, 2)
            add_m(2, 5)
            scale_m(3)
            h_lo(2)
            add_m(3, 7)
            h_lo(3)
            lo(l, 20, 3)
            def gate_mul(t, pair, side):
                dve.wait_ge(acc_free[side], read_out_at(l, pair + T_T // 2))
                v.scalar_tensor_tensor(tmp[2 + side][:, :], tmp[side][:, :], 1.0, rows(e_buf, t), ALU.add,
                                       ALU.mult).then_inc(s.gate_step, 1)

            def gate_add(t, side):
                dve.wait_ge(s.gate_step, t + (KT * l + 1))
                v.tensor_tensor(rows(x, t), rows(x, t), tmp[2 + side][:, :], ALU.add).then_inc(s.xnew, 1)

            def gate_tiles(i, last_body=False):
                e = rows(e_buf, 4 * i, 4).rearrange("p (k r) -> p k r", k=4)
                v.tensor_tensor(e, e, wide(r_t[:, :], [P, 4, R]), ALU.mult).then_inc(s.e_step, 1)
                dve.wait_ge(s.e_step, i + (4 * l + 1))
                for j in range(4):
                    t = 4 * i + j
                    gate_mul(t, 2 * i + j // 2, j % 2)
                    gate_add(t, j % 2)
                    if not last and (not isinstance(i, int) or t):
                        x_lo(l + 1, t - 1)
                    if not last_body or (j < 2 and not last):
                        lo(l, 21 + i, j)

            stat_scale(l, ST_E, D_MODEL)
            stat_diag(l, ST_E)
            stat_read(l, ST_E, r_t, 0.5)
            dve.wait_ge(s.bcast_read, spread_at(l, ST_E))
            gate_tiles(0)
            with dve.Fori(1, 3) as i:
                gate_tiles(i)
            gate_tiles(3, last_body=True)
            if not last:
                x_lo(l + 1, KT - 1)
                lo(l + 1, 0, 2)

    @block.gpsimd
    def _(pool):
        def add_square(n, buf, first):
            pool.wait_ge(s.sq_ready, n + 1)
            pool.wait_ge(s.sq_used, n)
            if first:
                nc.gpsimd.tensor_copy(buf[:, :], sq[:, n % 2, :]).then_inc(s.sq_used, 1)
            else:
                nc.gpsimd.tensor_tensor(buf[:, :], buf[:, :], sq[:, n % 2, :], ALU.add).then_inc(s.sq_used, 1)

        def root(l, k):
            pool.wait_ge(s.stat_scaled, stat_at(l, k))
            nc.gpsimd.tensor_tensor(rs, st, minus_half, ALU.pow).then_inc(s.stat_rs, 1)

        def ret_root(l, h):
            n = h + HEADS * l
            at = 5 * n
            pool.wait_ge(s.stat_ready, n + 1)
            g2_h = small[:, bass.ds(h * 3 + 56, 3)]
            gi_h = small[:, bass.ds(h * 3 + 32, 3)]
            nc.gpsimd.tensor_tensor(var_t, mv[:, :, 1], g2_h, ALU.mult).then_inc(s.pool_step, 1)
            pool.wait_ge(s.pool_step, at + 1)
            nc.gpsimd.tensor_tensor(var_t, var_t, eps3, ALU.add).then_inc(s.pool_step, 1)
            pool.wait_ge(s.pool_step, at + 2)
            nc.gpsimd.tensor_tensor(rs_t, var_t, minus_half, ALU.pow).then_inc(s.pool_step, 1)
            pool.wait_ge(s.pool_step, at + 3)
            nc.gpsimd.tensor_tensor(sc_t, rs_t, gi_h, ALU.mult).then_inc(s.pool_step, 1)
            pool.wait_ge(s.pool_step, at + 4)
            nc.gpsimd.tensor_tensor(mean_sc, mv[:, :, 0], sc_t, ALU.mult).then_inc(s.pool_step, 1)
            pool.wait_ge(s.pool_step, at + 5)
            nc.gpsimd.tensor_tensor(nb_t, zero3, mean_sc, ALU.subtract).then_inc(s.ret_rs, 1)

        for l in range(DEPTH):
            root(l, ST_X)
            with pool.Fori(0, HEADS - 1) as h:
                ret_root(l, h)
            root(l, ST_LN)
            ret_root(l, HEADS - 1)
            pool.wait_ge(s.mean_done, l + 1)
            pool.wait_ge(s.sum_done, stat_at(l, ST_LN))
            m_sum, e_sum = acc[(3 * l + 1) % 2], acc[3 * l % 2]
            for n in range(T_OP - T_O):
                add_square(squares_at(l) + n, m_sum, n == 0)
            for n, (kind, tile, _, _) in enumerate(out_and_ple(), T_OP - T_O):
                add_square(squares_at(l) + n, m_sum if kind == "m" else e_sum, kind == "e" and tile == 0)
                if n == M_DONE + 1:
                    root(l, ST_M)
            root(l, ST_E)
            if l < DEPTH - 1:
                for n in range(KT):
                    add_square(squares_at(l) + 2 * KT + n, m_sum, n == 0)


def kernel(x_prompt, x_sample, state_ret, state_conv, p_prompt, p_sample, w_in, w_out, g_ret, w_dw,
           b_dw, g_cn, b_cn, w_pw2, b_pw2, g_pre, g_post, w_ple, g_ple, w_ple_gate):
    import concourse.bacc as bacc
    from concourse.bass_utils import run_bass_kernel_spmd

    def slabs(w, per_tile, tiles_per_slab):
        d, rows_in, cols = w.shape
        k = rows_in // P
        t = w.reshape(d, k, P, cols // (P * tiles_per_slab), tiles_per_slab, P)
        t = t.transpose(0, 3, 2, 4, 1, 5)
        return np.ascontiguousarray(t).reshape(-1, tiles_per_slab * k * P)

    def features_down(rows_by_features):
        r, f = rows_by_features.shape
        return rows_by_features.reshape(r, f // P, P).transpose(2, 1, 0)

    a = {k: np.asarray(w) for k, w in dict(
        x_prompt=x_prompt, x_sample=x_sample, state_ret=state_ret, state_conv=state_conv, p_prompt=p_prompt,
        p_sample=p_sample, w_in=w_in, w_out=w_out, g_ret=g_ret, w_dw=w_dw, b_dw=b_dw, g_cn=g_cn, b_cn=b_cn,
        w_pw2=w_pw2, b_pw2=b_pw2, g_pre=g_pre, g_post=g_post, w_ple=w_ple, g_ple=g_ple, w_ple_gate=w_ple_gate).items()}
    x_all = np.concatenate([a["x_prompt"][0], a["x_sample"][:, 0]])
    p_all = np.concatenate([a["p_prompt"][:, 0], a["p_sample"][:, :, 0]], axis=1)
    column = lambda w: w.reshape(DEPTH, -1, P).transpose(2, 0, 1)
    dw = a["w_dw"].reshape(DEPTH, TAPS, CT, P).transpose(3, 0, 2, 1).reshape(P, DEPTH, CT * TAPS)
    vectors = [column(a[n]) for n in ("g_pre", "g_post", "g_ple", "g_ret", "b_dw", "g_cn", "b_cn", "b_pw2")] + [dw]
    conv_state = a["state_conv"].reshape(DEPTH, DEC, PAD, CT, P).transpose(0, 4, 3, 2, 1)
    ins = {
        "x_t": features_down(x_all),
        "p_t": np.stack([features_down(p) for p in p_all]),
        "s_ret": a["state_ret"].transpose(0, 2, 3, 1, 4).reshape(DEPTH * HEADS * P, DEC * P),
        "s_conv": conv_state.reshape(DEPTH * P, CT * PAD * DEC),
        "vecs": np.concatenate(vectors, axis=2),
        "consts": constants(),
        "w_in": slabs(a["w_in"], KT, 1),
        "w_pw": slabs(a["w_pw2"], CT, 2),
        "w_out": slabs(a["w_out"], KT, 1),
        "w_ple": slabs(a["w_ple"], PT, 4),
        "w_gate": slabs(a["w_ple_gate"], KT, 1),
    }
    outs = {
        "y_t": (P, KT, R),
        "sp_out": (DEPTH * HEADS * P, P),
        "scp_out": (DEPTH, P, CT, PAD),
        "ss_out": (DEPTH * HEADS * P, DEC * P),
        "scs_out": (DEPTH * P, CT * PAD * DEC),
    }
    nc = bacc.Bacc("TRN2", target_bir_lowering=False, num_devices=1, dynamic_dma_scratch_size=1024)
    ins = {k: np.ascontiguousarray(w) for k, w in ins.items()}
    args = [nc.dram_tensor(k, w.shape, F32, kind="ExternalInput").ap() for k, w in ins.items()]
    args += [nc.dram_tensor(k, shape, F32, kind="ExternalOutput").ap() for k, shape in outs.items()]
    with ExitStack() as ctx:
        build(nc, ctx, *args)
    got = run_bass_kernel_spmd(nc, [ins], core_ids=[0]).results[0]
    y = got["y_t"].transpose(2, 1, 0).reshape(R, D_MODEL)
    new_states = got["ss_out"].reshape(DEPTH, HEADS, P, DEC, P).transpose(0, 3, 1, 2, 4)
    conv_prompt = got["scp_out"].transpose(0, 3, 2, 1).reshape(DEPTH, 1, PAD, CONV)
    conv_sample = got["scs_out"].reshape(DEPTH, P, CT, PAD, DEC).transpose(0, 4, 3, 2, 1).reshape(DEPTH, DEC, PAD, CONV)
    return (y[:SEQ].reshape(1, SEQ, D_MODEL), y[SEQ:].reshape(DEC, 1, D_MODEL),
            got["sp_out"].reshape(DEPTH, 1, HEADS, P, P), conv_prompt, new_states, conv_sample)
```
